# Optimizing a Trainium2 kernel written in Bass

```python
import jax, jax.numpy as jnp
from jax import lax
import numpy as np
import math
import jax
import jax.numpy as jnp

D_MODEL = 1024
BATCH = 1
SEQ = 512
DEPTH = 2

N_EVEN = (DEPTH + 1) // 2
N_ODD = DEPTH // 2

LRU_WIDTH = D_MODEL // 2
LRU_HEADS = 8
LRU_HEAD_DIM = LRU_WIDTH // LRU_HEADS
LRU_CONV = 4
LRU_C = 8.0
LRU_MIN_RAD = 0.9
LRU_MAX_RAD = 0.999
SC_WIDTH = D_MODEL // 2
SC_CONV = 3
EVEN_IN = 2 * LRU_WIDTH + 3 * SC_WIDTH

SGU_WIDTH = D_MODEL // 2
SGU_HEADS = 8
SGU_HEAD_DIM = SGU_WIDTH // SGU_HEADS
CHUNK = 128
FOX_HEADS = 8
FOX_HEAD_DIM = 64
FOX_WIDTH = FOX_HEADS * FOX_HEAD_DIM
Q_BLOCK = 128
ODD_IN = 2 * SGU_WIDTH + 3 * FOX_WIDTH + FOX_HEADS

D_FF = 2816
FFN_CONV = 3
EPS = 1e-6


def rmsnorm(x, g):
    xf = x.astype(jnp.float32)
    y = xf * lax.rsqrt(jnp.mean(xf * xf, axis=-1, keepdims=True) + EPS)
    return (y * g.astype(jnp.float32)).astype(x.dtype)

def causal_depthwise_conv(x, w, b):
    k_width, ch = w.shape
    out = lax.conv_general_dilated(
        x, w[:, None, :].astype(x.dtype), window_strides=(1,),
        padding=[(k_width - 1, 0)], dimension_numbers=('NWC', 'WIO', 'NWC'),
        feature_group_count=ch)
    return out + b.astype(x.dtype)

def rg_lru(x, w_a, b_a, w_x, b_x, lam):
    bsz, s, w = x.shape
    xh = x.reshape(bsz, s, LRU_HEADS, LRU_HEAD_DIM)
    r = jax.nn.sigmoid((jnp.einsum('bshi,hij->bshj', xh, w_a).reshape(bsz, s, w) + b_a).astype(jnp.float32))
    i = jax.nn.sigmoid((jnp.einsum('bshi,hij->bshj', xh, w_x).reshape(bsz, s, w) + b_x).astype(jnp.float32))
    log_a = -LRU_C * r * jax.nn.softplus(-lam.astype(jnp.float32))
    a = jnp.exp(log_a)
    u = jnp.sqrt(-jnp.expm1(2.0 * log_a)) * (i * x.astype(jnp.float32))

    def combine(left, right):
        a_l, h_l = left
        a_r, h_r = right
        return a_l * a_r, a_r * h_l + h_r

    _, h = lax.associative_scan(combine, (a, u), axis=1)
    return h.astype(x.dtype)

def even_mixer(x, w_in, lru_conv_w, lru_conv_b, lru_wa, lru_ba, lru_wx, lru_bx, lru_lambda,
               sconv_w, sconv_b, w_out):
    p = x @ w_in
    W, C = LRU_WIDTH, SC_WIDTH
    xa, ga, c_pre, b_post, vb = jnp.split(p, [W, 2 * W, 2 * W + C, 2 * W + 2 * C], axis=-1)
    xa = causal_depthwise_conv(xa, lru_conv_w, lru_conv_b)
    ya = rg_lru(xa, lru_wa, lru_ba, lru_wx, lru_bx, lru_lambda) * jax.nn.gelu(ga)
    yb = b_post * causal_depthwise_conv(c_pre * vb, sconv_w, sconv_b)
    return jnp.concatenate([ya, yb], axis=-1) @ w_out

def chunked_spatial_gating(u, g, g_norm, w_s, b_s):
    bsz, s, _ = u.shape
    n_chunks = s // CHUNK
    gv = rmsnorm(g.reshape(bsz, s, SGU_HEADS, SGU_HEAD_DIM), g_norm.reshape(SGU_HEADS, SGU_HEAD_DIM))
    gv = gv.reshape(bsz, n_chunks, CHUNK, SGU_HEADS, SGU_HEAD_DIM)
    w_causal = jnp.tril(w_s)
    mixed = jnp.einsum('gts,bnsgc->bntgc', w_causal, gv) + b_s.T[:, :, None]
    return u * mixed.reshape(bsz, s, SGU_WIDTH)

def forgetting_attention(q, k, v, f_logit, b_f):
    bsz, s, _ = q.shape
    nb = s // Q_BLOCK

    def heads(t):
        return t.reshape(bsz, s, FOX_HEADS, FOX_HEAD_DIM).transpose(0, 2, 1, 3)

    q, k, v = heads(q), heads(k), heads(v)
    log_f = jax.nn.log_sigmoid(f_logit.astype(jnp.float32) + b_f.astype(jnp.float32))
    c = jnp.cumsum(log_f, axis=1).transpose(0, 2, 1)
    q_blocks = q.reshape(bsz, FOX_HEADS, nb, Q_BLOCK, FOX_HEAD_DIM).transpose(2, 0, 1, 3, 4)
    c_blocks = c.reshape(bsz, FOX_HEADS, nb, Q_BLOCK).transpose(2, 0, 1, 3)
    starts = jnp.arange(nb) * Q_BLOCK
    key_pos = jnp.arange(s)
    scale = FOX_HEAD_DIM ** -0.5

    def block(args):
        qb, cb, start = args
        logits = (jnp.einsum('bhqd,bhkd->bhqk', qb, k).astype(jnp.float32) * scale
                  + cb[..., None] - c[:, :, None, :])
        q_pos = start + jnp.arange(Q_BLOCK)
        logits = jnp.where(key_pos[None, :] <= q_pos[:, None], logits, -jnp.inf)
        p = jax.nn.softmax(logits, axis=-1)
        return jnp.einsum('bhqk,bhkd->bhqd', p.astype(v.dtype), v)

    out = lax.map(block, (q_blocks, c_blocks, starts))
    return out.transpose(1, 0, 3, 2, 4).reshape(bsz, s, FOX_WIDTH)

def odd_mixer(x, w_in, sgu_norm, sgu_w, sgu_b, fox_bf, w_out):
    p = x @ w_in
    Z, F = 2 * SGU_WIDTH, FOX_WIDTH
    z, q, k, v, f = jnp.split(p, [Z, Z + F, Z + 2 * F, Z + 3 * F], axis=-1)
    z = jax.nn.gelu(z)
    u, g = jnp.split(z, 2, axis=-1)
    yc = chunked_spatial_gating(u, g, sgu_norm, sgu_w, sgu_b)
    yd = forgetting_attention(q, k, v, f, fox_bf)
    return jnp.concatenate([yc, yd], axis=-1) @ w_out

def conv_glu_ffn(x, w_up, conv_w, conv_b, w_down):
    h = causal_depthwise_conv(x @ w_up, conv_w, conv_b)
    gate, val = jnp.split(h, 2, axis=-1)
    return (jax.nn.silu(gate) * val) @ w_down

def first_inputs(seed: int = 0) -> dict:
    key = jax.random.key(seed)
    ks = jax.random.split(key, 32)
    f32 = jnp.float32

    def dense(k, shape, fan_in):
        return jax.random.normal(k, shape, f32) * fan_in ** -0.5

    def gain(k, shape):
        return 1.0 + 0.05 * jax.random.normal(k, shape, f32)

    def bias(k, shape):
        return 0.1 * jax.random.normal(k, shape, f32)

    a_c = jax.random.uniform(ks[9], (N_EVEN, LRU_WIDTH), f32, LRU_MIN_RAD, LRU_MAX_RAD)
    s_base = a_c ** (1.0 / LRU_C)
    lru_lambda = jnp.log(s_base) - jnp.log1p(-s_base)

    return {
        "x": jax.random.normal(ks[0], (BATCH, SEQ, D_MODEL), f32),
        "mix0_norm": gain(ks[1], (N_EVEN, D_MODEL)),
        "mix0_w_in": dense(ks[2], (N_EVEN, D_MODEL, EVEN_IN), D_MODEL),
        "lru_conv_w": dense(ks[3], (N_EVEN, LRU_CONV, LRU_WIDTH), LRU_CONV),
        "lru_conv_b": bias(ks[4], (N_EVEN, LRU_WIDTH)),
        "lru_wa": dense(ks[5], (N_EVEN, LRU_HEADS, LRU_HEAD_DIM, LRU_HEAD_DIM), LRU_HEAD_DIM),
        "lru_ba": bias(ks[6], (N_EVEN, LRU_WIDTH)),
        "lru_wx": dense(ks[7], (N_EVEN, LRU_HEADS, LRU_HEAD_DIM, LRU_HEAD_DIM), LRU_HEAD_DIM),
        "lru_bx": bias(ks[8], (N_EVEN, LRU_WIDTH)),
        "lru_lambda": lru_lambda,
        "sconv_w": dense(ks[10], (N_EVEN, SC_CONV, SC_WIDTH), SC_CONV),
        "sconv_b": bias(ks[11], (N_EVEN, SC_WIDTH)),
        "mix0_w_out": dense(ks[12], (N_EVEN, LRU_WIDTH + SC_WIDTH, D_MODEL), LRU_WIDTH + SC_WIDTH),
        "mix1_norm": gain(ks[13], (N_ODD, D_MODEL)),
        "mix1_w_in": dense(ks[14], (N_ODD, D_MODEL, ODD_IN), D_MODEL),
        "sgu_norm": gain(ks[15], (N_ODD, SGU_WIDTH)),
        "sgu_w": dense(ks[16], (N_ODD, SGU_HEADS, CHUNK, CHUNK), CHUNK),
        "sgu_b": 1.0 + bias(ks[17], (N_ODD, SGU_HEADS, CHUNK)),
        "fox_bf": bias(ks[18], (N_ODD, FOX_HEADS)),
        "mix1_w_out": dense(ks[19], (N_ODD, SGU_WIDTH + FOX_WIDTH, D_MODEL), SGU_WIDTH + FOX_WIDTH),
        "ffn_norm": gain(ks[20], (DEPTH, D_MODEL)),
        "ffn_up": dense(ks[21], (DEPTH, D_MODEL, 2 * D_FF), D_MODEL),
        "ffn_conv_w": dense(ks[22], (DEPTH, FFN_CONV, 2 * D_FF), FFN_CONV),
        "ffn_conv_b": bias(ks[23], (DEPTH, 2 * D_FF)),
        "ffn_down": dense(ks[24], (DEPTH, D_FF, D_MODEL), D_FF),
        "final_norm": gain(ks[25], (D_MODEL,)),
    }

def first_block(x, mix0_norm, mix0_w_in, lru_conv_w, lru_conv_b, lru_wa, lru_ba, lru_wx, lru_bx,
              lru_lambda, sconv_w, sconv_b, mix0_w_out, mix1_norm, mix1_w_in, sgu_norm, sgu_w,
              sgu_b, fox_bf, mix1_w_out, ffn_norm, ffn_up, ffn_conv_w, ffn_conv_b, ffn_down,
              final_norm):
    h = x
    for layer in range(DEPTH):
        i = layer // 2
        if layer % 2 == 0:
            h = h + even_mixer(rmsnorm(h, mix0_norm[i]), mix0_w_in[i], lru_conv_w[i], lru_conv_b[i],
                               lru_wa[i], lru_ba[i], lru_wx[i], lru_bx[i], lru_lambda[i],
                               sconv_w[i], sconv_b[i], mix0_w_out[i])
        else:
            h = h + odd_mixer(rmsnorm(h, mix1_norm[i]), mix1_w_in[i], sgu_norm[i], sgu_w[i],
                              sgu_b[i], fox_bf[i], mix1_w_out[i])
        h = h + conv_glu_ffn(rmsnorm(h, ffn_norm[layer]), ffn_up[layer], ffn_conv_w[layer],
                             ffn_conv_b[layer], ffn_down[layer])
    return rmsnorm(h, final_norm)


CTX_LEN = 256
GRID_W = 64
BR_W = D_MODEL // 2
N_BRANCH = 3
DA_DH = 64
DA_DV = 2 * DA_DH
DA_HEADS = BR_W // DA_DV
ROPE_BASE = 10000.0
ML_DH = 128
ML_HEADS = BR_W // ML_DH
ML_CHUNK = 64
ML_CONV = 3
NA_DH = 64
NA_HEADS = BR_W // NA_DH
NA_KH_MAX = 8
NA_KW = 16
NA_QB = 16
NA_KBW = NA_QB + NA_KW
PROJ_SIZES = (BR_W,) * 4 + (BR_W,) * 5 + (4 * ML_HEADS,) + (BR_W,) * 4 + (N_BRANCH * D_MODEL,)
D_IN = sum(PROJ_SIZES)


def rms_norm(x, g):
    xf = x.astype(jnp.float32)
    y = xf * lax.rsqrt(jnp.mean(xf * xf, axis=-1, keepdims=True) + EPS)
    return (y * g).astype(x.dtype)

def split_proj(p):
    idx = [int(i) for i in np.cumsum(PROJ_SIZES)[:-1]]
    return jnp.split(p, idx, axis=-1)

def axial_rope_tables(n_tok, dh):
    t = jnp.arange(n_tok, dtype=jnp.int32)
    row = (t // GRID_W).astype(jnp.float32)
    col = (t % GRID_W).astype(jnp.float32)
    inv = ROPE_BASE ** (-jnp.arange(0, dh // 2, 2, dtype=jnp.float32) / (dh // 2))
    ang = jnp.concatenate([row[:, None] * inv, col[:, None] * inv], axis=-1)
    return jnp.cos(ang), jnp.sin(ang)

def apply_rope(x, cos, sin):
    xp = x.reshape(x.shape[:-1] + (x.shape[-1] // 2, 2))
    x1, x2 = xp[..., 0], xp[..., 1]
    shp = (1, cos.shape[0]) + (1,) * (x.ndim - 3) + (cos.shape[1],)
    cs = cos.reshape(shp).astype(x.dtype)
    sn = sin.reshape(shp).astype(x.dtype)
    return jnp.stack([x1 * cs - x2 * sn, x1 * sn + x2 * cs], axis=-1).reshape(x.shape)

def softmax_attn(q, k, v):
    s = jnp.einsum('bqhd,bkhd->bhqk', q, k).astype(jnp.float32) * (q.shape[-1] ** -0.5)
    p = jax.nn.softmax(s, axis=-1).astype(v.dtype)
    return jnp.einsum('bhqk,bkhd->bqhd', p, v)

def diff_attn_dense(q, k, v, lam):
    s = jnp.einsum('bqhcd,bkhcd->bhcqk', q, k).astype(jnp.float32) * (q.shape[-1] ** -0.5)
    p = jax.nn.softmax(s, axis=-1)
    a = (p[:, :, 0] - lam * p[:, :, 1]).astype(v.dtype)
    return jnp.einsum('bhqk,bkhv->bqhv', a, v)

def diff_attn_blocks(q, k, v, lam):
    B, S = q.shape[:2]
    nb = S // Q_BLOCK
    qb = jnp.moveaxis(q.reshape((B, nb, Q_BLOCK) + q.shape[2:]), 1, 0)
    o = lax.map(lambda qq: diff_attn_dense(qq, k, v, lam), qb)
    return jnp.moveaxis(o, 0, 1).reshape((B, S) + o.shape[3:])

def diff_head_norm(o, g, lam_init):
    y = rms_norm(o, g) * (1.0 - lam_init)
    return y.reshape(o.shape[:2] + (-1,))

def dwconv_centred(x, w, b):
    K = w.shape[0]
    y = lax.conv_general_dilated(x, w[:, None, :].astype(x.dtype), window_strides=(1,),
                                 padding=[((K - 1) // 2, K // 2)],
                                 dimension_numbers=('NWC', 'WIO', 'NWC'),
                                 feature_group_count=x.shape[-1])
    return y + b

def mlstm_inputs(q, k, v, g, conv_w, conv_b, gate_b):
    B, T, _ = q.shape
    qk = jax.nn.silu(dwconv_centred(jnp.concatenate([q, k], axis=-1), conv_w, conv_b))
    qq, kk = jnp.split(qk, 2, axis=-1)
    shp = (B, T, ML_HEADS, ML_DH)
    gates = g.reshape(B, T, 2, 2, ML_HEADS).astype(jnp.float32) + gate_b.astype(jnp.float32)
    log_i = gates[:, :, :, 0]
    log_f = jax.nn.log_sigmoid(gates[:, :, :, 1])
    return qq.reshape(shp), kk.reshape(shp) * (ML_DH ** -0.5), v.reshape(shp), log_i, log_f

def mlstm_chunkwise(q, k, v, log_i, log_f, state, with_out):
    B, T, H, d = q.shape
    L = ML_CHUNK
    nc = T // L
    to_chunks = lambda a: jnp.moveaxis(a.reshape((B, nc, L) + a.shape[2:]), 1, 0)
    xs = (to_chunks(q), to_chunks(k), to_chunks(v), to_chunks(log_i), to_chunks(log_f))
    causal = jnp.tril(jnp.ones((L, L), dtype=bool))

    def step(carry, xc):
        C, n, m = carry
        qc, kc, vc, lic, lfc = xc
        qc = qc.astype(jnp.float32)
        kc = kc.astype(jnp.float32)
        vc = vc.astype(jnp.float32)
        b = jnp.moveaxis(jnp.cumsum(lfc.astype(jnp.float32), axis=1), 1, 2)
        li = jnp.moveaxis(lic.astype(jnp.float32), 1, 2)
        bL = b[..., -1]
        g_s = bL[..., None] - b + li
        m_new = jnp.maximum(bL + m, jnp.max(g_s, axis=-1))
        w_s = jnp.exp(g_s - m_new[..., None])
        decay = jnp.exp(bL + m - m_new)
        C_new = decay[..., None, None] * C + jnp.einsum('bhs,bshk,bshv->bhkv', w_s, kc, vc)
        n_new = decay[..., None] * n + jnp.einsum('bhs,bshk->bhk', w_s, kc)
        if with_out:
            dmat = jnp.where(causal, b[..., :, None] - b[..., None, :] + li[..., None, :], -jnp.inf)
            m_inter = b + m[..., None]
            m_t = jnp.maximum(m_inter, jnp.max(dmat, axis=-1))
            a_inter = jnp.exp(m_inter - m_t)
            qk = jnp.einsum('bthd,bshd->bhts', qc, kc) * jnp.exp(dmat - m_t[..., None])
            num = a_inter[..., None] * jnp.einsum('bthk,bhkv->bhtv', qc, C) + jnp.einsum('bhts,bshv->bhtv', qk, vc)
            den = a_inter * jnp.einsum('bthk,bhk->bht', qc, n) + jnp.sum(qk, axis=-1)
            h = num / jnp.maximum(jnp.abs(den), jnp.exp(-m_t))[..., None]
            h = jnp.moveaxis(h, 1, 2)
        else:
            h = None
        return (C_new, n_new, m_new), h

    final, hs = lax.scan(step, state, xs)
    if with_out:
        hs = jnp.moveaxis(hs, 0, 1).reshape(B, T, H, d).astype(q.dtype)
    return final, hs

def mlstm_bidirectional(lat, ctx, with_ctx_out):
    ql, kl, vl, lil, lfl = lat
    qc, kc, vc, lic, lfc = ctx
    B, _, H, d = ql.shape
    zero = (jnp.zeros((B, H, d, d), jnp.float32), jnp.zeros((B, H, d), jnp.float32), jnp.zeros((B, H), jnp.float32))
    flip = lambda a: jnp.flip(a, axis=1)
    st_f, hc_f = mlstm_chunkwise(qc, kc, vc, lic[:, :, 0], lfc[:, :, 0], zero, with_ctx_out)
    _, hl_f = mlstm_chunkwise(ql, kl, vl, lil[:, :, 0], lfl[:, :, 0], st_f, True)
    st_b, hc_b = mlstm_chunkwise(flip(qc), flip(kc), flip(vc), flip(lic[:, :, 1]), flip(lfc[:, :, 1]), zero, with_ctx_out)
    _, hl_b = mlstm_chunkwise(flip(ql), flip(kl), flip(vl), flip(lil[:, :, 1]), flip(lfl[:, :, 1]), st_b, True)
    h_lat = hl_f + flip(hl_b)
    h_ctx = hc_f + flip(hc_b) if with_ctx_out else None
    return h_lat, h_ctx

def mlstm_out(h, o_pre, z, g):
    hn = rms_norm(h, g).reshape(h.shape[:2] + (-1,))
    return jax.nn.sigmoid(o_pre) * hn * jax.nn.silu(z)

def neighbourhood_attn(q, k, v, kc, vc, rpb):
    B, S, H, d = q.shape
    rows = S // GRID_W
    kh = min(NA_KH_MAX, rows)
    ncb = GRID_W // NA_QB
    qcol = np.arange(GRID_W).reshape(ncb, NA_QB)
    kc0 = np.clip(np.arange(ncb) * NA_QB - NA_KW // 2, 0, GRID_W - NA_KBW)
    kcol = kc0[:, None] + np.arange(NA_KBW)[None, :]
    cs = np.clip(qcol - NA_KW // 2, 0, GRID_W - NA_KW)
    col_ok = (kcol[:, None, :] >= cs[:, :, None]) & (kcol[:, None, :] < cs[:, :, None] + NA_KW)
    col_idx = np.clip(kcol[:, None, :] - qcol[:, :, None] + NA_KW - 1, 0, 2 * NA_KW - 2)
    mask = jnp.asarray(col_ok[:, :, None, :])
    qb = q.reshape(B, rows, ncb, NA_QB, H, d)
    kb = k.reshape(B, rows, GRID_W, H, d)[:, :, kcol]
    vb = v.reshape(B, rows, GRID_W, H, d)[:, :, kcol]
    scale = d ** -0.5
    n_loc = kh * NA_KBW

    def row_block(r):
        rs = jnp.clip(r - kh // 2, 0, rows - kh)
        kr = lax.dynamic_slice_in_dim(kb, rs, kh, axis=1)
        vr = lax.dynamic_slice_in_dim(vb, rs, kh, axis=1)
        qr = lax.dynamic_index_in_dim(qb, r, axis=1, keepdims=False)
        row_idx = rs + jnp.arange(kh) - r + NA_KH_MAX - 1
        bias = rpb[:, row_idx[None, None, :, None], col_idx[:, :, None, :]]
        s_loc = jnp.einsum('bnqhd,binkhd->bhnqik', qr, kr).astype(jnp.float32) * scale + bias.astype(jnp.float32)
        s_loc = jnp.where(mask, s_loc, -jnp.inf)
        s_ctx = jnp.einsum('bnqhd,bjhd->bhnqj', qr, kc).astype(jnp.float32) * scale
        s_all = jnp.concatenate([s_loc.reshape(s_loc.shape[:4] + (n_loc,)), s_ctx], axis=-1)
        p = jax.nn.softmax(s_all, axis=-1).astype(v.dtype)
        p_loc = p[..., :n_loc].reshape(s_loc.shape)
        p_ctx = p[..., n_loc:]
        return jnp.einsum('bhnqik,binkhd->bnqhd', p_loc, vr) + jnp.einsum('bhnqj,bjhd->bnqhd', p_ctx, vc)

    o = lax.map(row_block, jnp.arange(rows))
    return jnp.moveaxis(o, 0, 1).reshape(B, S, H, d)

def merge_branches(ys, gm, w_br, w_out):
    y = jnp.stack(ys, axis=2)
    proj = jnp.einsum('btnw,nwd->btnd', y, w_br)
    g = jax.nn.sigmoid(gm.reshape(gm.shape[:2] + (N_BRANCH, -1)))
    return jnp.sum(g * proj, axis=2) @ w_out

def hybrid_layer(l, x, xc, sc, scc, cos, sin, w_mod, b_mod, norm_g, w_in, lam_q, lam_k, da_g,
                 conv_w, conv_b, gate_b, ml_g, rpb, w_br, w_out, update_ctx):
    B, S, _ = x.shape
    L = xc.shape[1]
    shift, scale, gate = jnp.split(sc @ w_mod + b_mod, 3, axis=-1)
    shift_c, scale_c, gate_c = jnp.split(scc @ w_mod + b_mod, 3, axis=-1)
    h = rms_norm(x, norm_g) * (1 + scale[:, None]) + shift[:, None]
    hc = rms_norm(xc, norm_g) * (1 + scale_c) + shift_c
    aq, ak, av, az, bq, bk, bv, bo, bz, bg, cq, ck, cv, cz, gm = split_proj(h @ w_in)
    aqc, akc, avc, azc, bqc, bkc, bvc, boc, bzc, bgc, cqc, ckc, cvc, czc, gmc = split_proj(hc @ w_in)

    lam_init = 0.8 - 0.6 * math.exp(-0.3 * l)
    lam = (jnp.exp(jnp.sum(lam_q[0] * lam_k[0])) - jnp.exp(jnp.sum(lam_q[1] * lam_k[1]))).astype(jnp.float32) + lam_init
    da_qk = lambda t: t.reshape(t.shape[:2] + (DA_HEADS, 2, DA_DH))
    da_v = lambda t: t.reshape(t.shape[:2] + (DA_HEADS, DA_DV))
    k_all = jnp.concatenate([apply_rope(da_qk(ak), cos, sin), da_qk(akc)], axis=1)
    v_all = jnp.concatenate([da_v(av), da_v(avc)], axis=1)
    o_a = diff_attn_blocks(apply_rope(da_qk(aq), cos, sin), k_all, v_all, lam)
    y_a = diff_head_norm(o_a, da_g, lam_init) * jax.nn.silu(az)

    lat_b = mlstm_inputs(bq, bk, bv, bg, conv_w, conv_b, gate_b)
    ctx_b = mlstm_inputs(bqc, bkc, bvc, bgc, conv_w, conv_b, gate_b)
    h_b, h_bc = mlstm_bidirectional(lat_b, ctx_b, update_ctx)
    y_b = mlstm_out(h_b, bo, bz, ml_g)

    na_h = lambda t: t.reshape(t.shape[:2] + (NA_HEADS, NA_DH))
    o_c = neighbourhood_attn(na_h(cq), na_h(ck), na_h(cv), na_h(ckc), na_h(cvc), rpb)
    y_c = o_c.reshape(B, S, BR_W) * jax.nn.silu(cz)

    x = x + gate[:, None] * merge_branches((y_a, y_b, y_c), gm, w_br, w_out)
    if update_ctx:
        o_ac = diff_attn_dense(da_qk(aqc), da_qk(akc), da_v(avc), lam)
        y_ac = diff_head_norm(o_ac, da_g, lam_init) * jax.nn.silu(azc)
        y_bc = mlstm_out(h_bc, boc, bzc, ml_g)
        y_cc = softmax_attn(na_h(cqc), na_h(ckc), na_h(cvc)).reshape(B, L, BR_W) * jax.nn.silu(czc)
        xc = xc + gate_c * merge_branches((y_ac, y_bc, y_cc), gmc, w_br, w_out)
    return x, xc

def second_inputs(seed: int = 0) -> dict:
    key = jax.random.key(seed)
    ks = jax.random.split(key, 20)
    f32 = jnp.float32
    nrm = lambda k, shape, s: jax.random.normal(k, shape, f32) * s
    f_base = jnp.linspace(3.0, 6.0, ML_HEADS, dtype=f32)
    gate_base = jnp.stack([jnp.zeros((ML_HEADS,), f32), f_base])[None, None]
    return {
        'x': nrm(ks[0], (BATCH, SEQ, D_MODEL), 1.0),
        'c': nrm(ks[1], (BATCH, D_MODEL), 1.0),
        'ctx': nrm(ks[2], (BATCH, CTX_LEN, D_MODEL), 1.0),
        'c_ctx': nrm(ks[3], (D_MODEL,), 1.0),
        'w_mod': nrm(ks[4], (DEPTH, D_MODEL, 3 * D_MODEL), 0.5 * D_MODEL ** -0.5),
        'b_mod': nrm(ks[5], (DEPTH, 3 * D_MODEL), 0.02),
        'norm_g': 1.0 + nrm(ks[6], (DEPTH, D_MODEL), 0.02),
        'w_in': nrm(ks[7], (DEPTH, D_MODEL, D_IN), D_MODEL ** -0.5),
        'da_lam_q': nrm(ks[8], (DEPTH, 2, DA_DH), 0.1),
        'da_lam_k': nrm(ks[9], (DEPTH, 2, DA_DH), 0.1),
        'da_norm_g': 1.0 + nrm(ks[10], (DEPTH, DA_DV), 0.02),
        'ml_conv_w': nrm(ks[11], (DEPTH, ML_CONV, 2 * BR_W), ML_CONV ** -0.5),
        'ml_conv_b': nrm(ks[12], (DEPTH, 2 * BR_W), 0.02),
        'ml_gate_b': gate_base + nrm(ks[13], (DEPTH, 2, 2, ML_HEADS), 0.1),
        'ml_norm_g': 1.0 + nrm(ks[14], (DEPTH, ML_DH), 0.02),
        'na_rpb': nrm(ks[15], (DEPTH, NA_HEADS, 2 * NA_KH_MAX - 1, 2 * NA_KW - 1), 0.05),
        'w_br': nrm(ks[16], (DEPTH, N_BRANCH, BR_W, D_MODEL), BR_W ** -0.5),
        'w_out': nrm(ks[17], (DEPTH, D_MODEL, D_MODEL), D_MODEL ** -0.5),
        'final_g': 1.0 + nrm(ks[18], (D_MODEL,), 0.02),
    }

def second_block(x, c, ctx, c_ctx, w_mod, b_mod, norm_g, w_in, da_lam_q, da_lam_k, da_norm_g,
              ml_conv_w, ml_conv_b, ml_gate_b, ml_norm_g, na_rpb, w_br, w_out, final_g):
    cos, sin = axial_rope_tables(x.shape[1], DA_DH)
    sc = jax.nn.silu(c)
    scc = jax.nn.silu(c_ctx)
    xc = ctx
    for l in range(DEPTH):
        x, xc = hybrid_layer(l, x, xc, sc, scc, cos, sin, w_mod[l], b_mod[l], norm_g[l], w_in[l],
                             da_lam_q[l], da_lam_k[l], da_norm_g[l], ml_conv_w[l], ml_conv_b[l],
                             ml_gate_b[l], ml_norm_g[l], na_rpb[l], w_br[l], w_out[l],
                             l < DEPTH - 1)
    return rms_norm(x, final_g)


def setup_inputs(seed=0):
    out = dict(first_inputs(seed))
    for name, value in second_inputs(seed + 1).items():
        if name != "x":
            out[name + "_2"] = value
    return out


def reference(
    x, mix0_norm, mix0_w_in, lru_conv_w, lru_conv_b, lru_wa, lru_ba, lru_wx, lru_bx, lru_lambda,
    sconv_w, sconv_b, mix0_w_out, mix1_norm, mix1_w_in, sgu_norm, sgu_w, sgu_b, fox_bf,
    mix1_w_out, ffn_norm, ffn_up, ffn_conv_w, ffn_conv_b, ffn_down, final_norm, c_2, ctx_2,
    c_ctx_2, w_mod_2, b_mod_2, norm_g_2, w_in_2, da_lam_q_2, da_lam_k_2, da_norm_g_2,
    ml_conv_w_2, ml_conv_b_2, ml_gate_b_2, ml_norm_g_2, na_rpb_2, w_br_2, w_out_2, final_g_2,
):
    x = first_block(
        x, mix0_norm, mix0_w_in, lru_conv_w, lru_conv_b, lru_wa, lru_ba, lru_wx, lru_bx,
        lru_lambda, sconv_w, sconv_b, mix0_w_out, mix1_norm, mix1_w_in, sgu_norm, sgu_w, sgu_b,
        fox_bf, mix1_w_out, ffn_norm, ffn_up, ffn_conv_w, ffn_conv_b, ffn_down, final_norm,
    )
    return second_block(
        x, c_2, ctx_2, c_ctx_2, w_mod_2, b_mod_2, norm_g_2, w_in_2, da_lam_q_2, da_lam_k_2,
        da_norm_g_2, ml_conv_w_2, ml_conv_b_2, ml_gate_b_2, ml_norm_g_2, na_rpb_2, w_br_2,
        w_out_2, final_g_2,
    )


_drawn_inputs = setup_inputs


def setup_inputs(seed=0):
    import zlib

    import numpy as np

    out = dict(_drawn_inputs(seed))
    spreads = {}
    factors = {'lru_ba': 7.393,
     'lru_bx': 4.655,
     'sgu_norm': 5.226,
     'fox_bf': 4.735,
     'b_mod_2': 3.788,
     'norm_g_2': 8.0,
     'da_lam_q_2': 7.643,
     'da_lam_k_2': 4.838,
     'da_norm_g_2': 8.0,
     'ml_conv_b_2': 54.005,
     'ml_norm_g_2': 8.0,
     'na_rpb_2': 8.0,
     'final_g_2': 7.92}
    for name, (base, spread) in spreads.items():
        noise = np.random.default_rng([zlib.crc32(name.encode()), seed]).standard_normal(out[name].shape)
        drawn = base * np.exp(spread * noise) if base else spread * noise
        out[name] = jnp.asarray(drawn.astype(out[name].dtype))
    for name, factor in factors.items():
        out[name] = (out[name] * factor).astype(out[name].dtype)
    return out
```

```python
from contextlib import ExitStack, contextmanager

import numpy as np
import concourse.bass as bass
from concourse import mybir

F32 = mybir.dt.float32
ALU = mybir.AluOpType
ACT = mybir.ActivationFunctionType
AX = mybir.AxisListType.X

P = 128
D = 1024
KT = D // P
T = 512
TC = 256
TA = T + TC
SLAB = 256
F = 2816
FT = F // P
FI = F // SLAB
BW = 512
LAYERS = 2
EPS = 1e-6
BIG = 1e30
MOD = LAYERS * 3 * D // BW

PARAMS = [("mix0_norm", 8), ("lru_conv", 4 * 5), ("lru_ba", 4), ("lru_bx", 4), ("lru_lambda", 4),
          ("sconv", 4 * 4), ("mix1_norm", 8), ("ffn_norm0", 8), ("ffn_norm1", 8), ("final_norm", 8),
          ("ffn_conv0", FI * 16), ("ffn_conv1", FI * 16), ("c", 16), ("b_mod", 96), ("norm_g", 32),
          ("da_g", 2), ("ml_conv", 2 * 8 * 4), ("ml_g", 2), ("final_g", 8),
          ("fox_bf", 1), ("gate_bi", 2), ("gate_bf", 2)]
PCOL, _n = {}, 0
for _name, _c in PARAMS:
    PCOL[_name] = _n
    _n += _c
NPARAM = _n
ROWS = {"lam_q": 0, "lam_k": 256, "sgu_norm": 512}
NROW = 1024


class Stage:

    def __init__(self, kind, base, prev, evs=(), at="H", ctx=False, layer=0, nt=4, mode="", src="", g="",
                 n=0, name="", jobs=(), passes=()):
        self.kind, self.base, self.prev = kind, base, prev
        self.evs, self.at, self.ctx, self.layer, self.nt = evs, at, ctx, layer, nt
        self.mode, self.src, self.g = mode, src, g
        self.n = n
        self.name, self.jobs, self.passes = name, jobs, passes

    def __getitem__(self, key):
        return self.base.get(key, 0)


class Own:

    def __init__(self, eng, sem):
        self.eng, self.sem, self.n, self.reg = eng, sem, 0, None

    def mark(self, ins):
        ins.then_inc(self.sem, 1)
        self.n += 1

    def wait(self):
        v = self.n if self.reg is None else self.reg[0] * self.reg[1] + self.n
        self.eng.wait_ge(self.sem, v)

    def link(self, ins):
        self.mark(ins)
        self.wait()

    @contextmanager
    def loop(self, count, per):
        start = self.n
        with self.eng.Fori(0, count) as i:
            self.reg = (i, per)
            yield i
            assert self.n - start == per, (self.n - start, per)
        self.n, self.reg = start + count * per, None


def plan_stages():
    base, out = {}, []

    def add(kind, counts, **args):
        out.append(Stage(kind, dict(base), out[-1] if out else None, **args))
        for k, v in counts.items():
            base[k] = base.get(k, 0) + v

    def full(*bs, n=1):
        return {("full", b): n for b in bs}

    def free(*bs, n=1):
        return {("free", b): n for b in bs}

    def norm(mode, src, g, ctx=False, layer=0, **kw):
        bs = (6, 7) if ctx else (6,)
        add("norm", {**full(*bs), **free(*bs), "sq": 8, "rs": len(bs),
                     **({"hr": 8} if mode in ("H", "mod") else {"xn": 8})},
            mode=mode, src=src, g=g, ctx=ctx, layer=layer, **kw)

    def units(evs, at, ctx=False, layer=0, **kw):
        n = len(evs)
        add("units", {"it": n, "w8": 2 * n, **full(0, 2, n=n), **free(0, 1, 2, 3, n=n),
                      **(full(1, 3, n=n) if ctx else {}), **(free(4, 5, n=n) if ctx else {})},
            evs=evs, ctx=ctx, layer=layer, at=at, **kw)

    def tok(evs, nt=4, **kw):
        n = len(evs)
        add("tok", {"it": n, "w8": 2 * n, **full(*range(nt - 1), n=n), **free(*range(nt), n=n)},
            evs=evs, nt=nt, **kw)

    def attn(name, jobs, **kw):
        use, nj, ex = {0: 0, 1: 0}, 0, 0
        for n, j in enumerate(jobs):
            j["n"] = n
            j["use"] = []
            for c in j["comps"]:
                j["use"].append(use[c["slot"]])
                use[c["slot"]] += 1
                c["ex"] = ex
                ex += not j["raw"]
            j["out"] = nj
            nj += j["last"]
        counts = {**full(0, n=use[0]), **free(0, n=use[0]), **full(2, n=use[1]), **free(2, n=use[1]),
                  **full(4, n=len(jobs)), **free(4, n=len(jobs)), **full(6, n=nj), **free(6, n=nj)}
        if name == "fox":
            counts.update(full(7, n=8))
            counts.update(free(7, n=8))
            counts.update({"it": MOD, "w8": 2 * MOD, **free(5, n=MOD)})
        if name.startswith("da"):
            counts.update(full(7, n=nj))
            counts.update(free(7, n=nj))
        add("attn", counts, name=name, jobs=jobs, **kw)

    add("prep", {})
    norm("H", "load", "mix0_norm")
    units(["xa", "ga"], at="H")
    add("lru", {**full(0, 1, 2, 3, n=2), **free(0, 1, 2, 3, n=2)})
    units(["cp", "vb", "bp"], at="H")
    units(["res", "res"], at="Y")
    norm("H", "res", "ffn_norm0")
    for f in range(2):
        add("up", {"it": FI, "w8": 2 * FI, **full(0, 2, n=FI), **free(0, 1, 2, 3, n=FI),
                   "cb": 4 * FI, "sg": 2 * FI, "hid": 2 * FI}, layer=f)
        add("down", {"it": 4, **full(0, 2, n=2), **free(0, 1, 2, 3, n=2)}, layer=f)
        if f == 0:
            norm("H", "down", "mix1_norm")
            add("foxgate", {**full(6, 7), **free(6, 7)})
            units(["u", "q", "k"], at="H")
            tok(["g", "v"])
            add("sgu", {**full(0, 1, 2, 3), **free(0, 1, 2, 3)})
            jobs = []
            for h in range(8):
                for qb in range(4):
                    jobs.append(dict(comps=[dict(slot=len(jobs) % 2, po=64 * (h % 2))], head=h, tile=h // 2,
                                     q0=128 * qb, k0=0, nk=128 * (qb + 1), qcol=128 * qb, first=qb == 0,
                                     last=qb == 3, nq=512, causal=True, raw=False, dv=64, po=64 * (h % 2), qb=qb))
            attn("fox", jobs)
            units(["res", "res"], at="Y")
            norm("H", "res", "ffn_norm1")
    norm("X", "down", "final_norm")
    for l in range(LAYERS):
        ctx = l == 0
        norm("mod", "xn" if l == 0 else "res", "norm_g", ctx=True, layer=l)

        def branch(keys, rest, v):
            if ctx:
                units(keys + rest, at="H", ctx=True, layer=l)
            else:
                units(keys, at="H", ctx=True, layer=l)
                units(rest, at="H", ctx=False, layer=l)
            tok([v], nt=6, layer=l)

        def merge(n):
            add("merge", {"it": 4, "w8": 4, **full(0, 2, n=4), **free(0, 1, 2, 3, n=4),
                          **(full(1, 3, n=4) if ctx else {}), **(free(4, 5, n=4) if ctx else {}),
                          "gate": 12 if ctx else 8}, n=n, ctx=ctx, layer=l)

        branch(["ak"], ["aq", "az"], "av")
        add("rope", {**full(6, 7, n=4), **free(6, 7, n=4)}, layer=l)
        jobs = []
        for h in range(4):
            for qb in range(6 if ctx else 4):
                lat = qb < 4
                jobs.append(dict(comps=[dict(slot=c, po=64 * c) for c in range(2)], head=h, tile=h,
                                 q0=128 * qb, k0=0 if lat else T, nk=TA if lat else TC,
                                 qcol=128 * qb if lat else 128 * (qb - 4), first=qb in (0, 4),
                                 last=qb in (3, 5), nq=512 if lat else 256, causal=False, raw=True, dv=128, po=0, qb=qb))
        attn(f"da{l}", jobs, layer=l)
        merge(0)
        branch(["bk"], ["bq", "bo", "bz"], "bv")
        add("mlgate", {**full(6, 7, n=2), **free(6, 7, n=2), **full(0), **free(0)}, layer=l)
        passes, n, np_ = [], 0, 0
        for h in range(4):
            for d in range(2):
                for g in range(2 if ctx else 1):
                    blocks = []
                    nb, nq = (4, 512) if g == 0 else (2, 256)
                    own = list(range(nb)) if d == 0 else list(range(nb))[::-1]
                    if g == 0:
                        blocks += [(4, 0, 512, None), (5, 0, 512, None)]
                    for j in own:
                        t0, t1 = (128 * j, nq) if d == 0 else (0, 128 * (j + 1))
                        blocks.append((j + 4 * g, t0, t1, j))
                    passes.append(dict(h=h, d=d, g=g, nq=nq, nb=nb, blocks=blocks, n0=n, p=np_))
                    n += len(blocks)
                    np_ += 1
        add("mlstm", {**full(0, n=(n + 1) // 2), **free(0, n=(n + 1) // 2), **full(1, n=n // 2),
                      **free(1, n=n // 2), **full(5, n=np_), **free(5, n=np_),
                      **full(2, n=(np_ + 1) // 2), **free(2, n=(np_ + 1) // 2),
                      **full(6, n=np_ // 2), **free(6, n=np_ // 2)}, layer=l, passes=passes, ctx=ctx)
        add("mlout", {**full(6, 7, n=4) , **free(6, 7, n=4)} if ctx else {**full(6, n=4), **free(6, n=4)},
            layer=l, ctx=ctx)
        merge(1)
        branch(["ck"], ["cq", "cz"], "cv")
        jobs = []
        for h in range(8):
            for qb in range(6 if ctx else 4):
                lat = qb < 4
                jobs.append(dict(comps=[dict(slot=len(jobs) % 2, po=64 * (h % 2))], head=h, tile=h // 2,
                                 q0=128 * qb, k0=0 if lat else T, nk=TA if lat else TC,
                                 qcol=128 * qb if lat else 128 * (qb - 4), first=qb in (0, 4),
                                 last=qb in (3, 5), nq=512 if lat else 256, causal=False, raw=not lat, dv=64,
                                 po=64 * (h % 2), qb=qb))
        attn(f"na{l}", jobs, layer=l)
        merge(2)
        units(["mres", "mres"], at="ACC", ctx=ctx, layer=l)
    norm("X", "res", "final_g")
    add("store", {})
    return out


def build(nc, x, ctx_in, w8, wd, wb, wf_in, wg_in, params, rows, lru_w, sgu_w, sgu_b, rope, rot, nbias, out):
    stages = plan_stages()
    cx = ExitStack()

    def sb(name, shape):
        return cx.enter_context(nc.sbuf_tensor(name, shape, F32))

    sems = {}

    def sem(name):
        if name not in sems:
            sems[name] = cx.enter_context(nc.semaphore(name))
        return sems[name]

    X = sb("X", [P, KT, T])
    XC = sb("XC", [P, KT, TC])
    H = sb("H", [P, KT, TA])
    W = sb("W", [P, 2, 11 * SLAB])
    PC = sb("PC", [P, NPARAM])
    PR = sb("PR", [P, NROW])
    RST = sb("RST", [P, TA])
    IDENT = sb("IDENT", [P, P])
    ONES = sb("ONES", [P, P])
    SEL = sb("SEL", [8, 8, P])
    MCAUS = sb("MCAUS", [P, P])
    MFWD = sb("MFWD", [P, P])
    MBWD = sb("MBWD", [P, P])
    EPSC = sb("EPSC", [P, 1])
    SC = sb("SC", [P, KT, 2])
    MODT = sb("MODT", [P, LAYERS, 24, 2])
    MG = sb("MG", [P, KT, 2])
    LAM = sb("LAM", [P, LAYERS, 8])
    DAG = sb("DAG", [P, LAYERS])
    SMALL = sb("SMALL", [P, 64])
    ARENA = sb("ARENA", [P, 29600])
    ROT = sb("ROT", [P, P])
    WFS = sb("WFS", [P, KT, 8])
    WGS = sb("WGS", [P, KT, 16])
    PS = cx.enter_context(nc.psum_tensor("PS", [P, 8, 512], F32))

    def bank(b, n=512, p0=0, p1=P):
        if n <= 512:
            return PS[p0:p1, b, 0:n]
        return PS[p0:p1, b:b + 2, :].rearrange("p a b -> p (a b)")[:, 0:n]

    class Carve:
        def __init__(self, at=0):
            self.at = at

        def __call__(self, *shape, parts=P):
            n = int(np.prod(shape))
            v = ARENA[0:parts, self.at:self.at + n]
            self.at += n
            assert self.at <= 29600, self.at
            if len(shape) == 2:
                v = v.rearrange("p (a b) -> p a b", a=shape[0])
            if len(shape) == 3:
                v = v.rearrange("p (a b c) -> p a b c", a=shape[0], b=shape[1])
            return v

    cv = Carve()
    XA, GA, CP, YB, RG, IG, AG, TH, HS, PV = (cv(4, T) for _ in range(10))
    Y = cv(8, T)
    LRUW = cv(8, P)
    NSP = cv(8, 4)
    cv = Carve()
    HID = cv(FT, T)
    CB, SG = cv(4, T), cv(2, T)
    cv = Carve()
    UU, FQ, FK, FV, GT, GSQ = (cv(4, T) for _ in range(6))
    WT = cv(8, P)
    FROW = cv(4, T)
    FCQ = cv(4, 8)
    FT1, FAT, FE, FL = cv(2, T), cv(4, T), cv(2, T), cv(2, T)
    GMS = cv(4, 8)
    OY = cv(8, T)
    BS = cv(P)
    cv = Carve()
    ACC = cv(8, TA)
    Q, K, Z = (cv(4, TA) for _ in range(3))
    V = cv(6, BW)
    YT = cv(4, TA)
    scratch = cv.at
    AT, E_, L_ = cv(6, T), cv(2, TA), cv(2, TA)
    NB = cv(2, 14 * 64)
    cv = Carve(scratch + 6 * T)
    DL, DE = cv(2, TA), cv(4, TA)
    cv = Carve(scratch)
    RC, RS_, RT1, RT2 = cv(T), cv(T), cv(T), cv(T)
    cv = Carve(scratch)
    GB, TM = cv(3, T), cv(T)
    cv = Carve(scratch)
    CV = cv(2, TA)
    BZ = cv(T)
    BZC = cv(T)
    cv = Carve(scratch)
    B0, B1, M0, M1 = (cv(TA) for _ in range(4))
    shared = cv.at
    LI, LF, A0, A1, ZERO, LX = (cv(TA) for _ in range(6))
    AC = cv(12, 8)
    cv = Carve(shared)
    DM, ZM = cv(2, T), cv(2, T)
    MK, EM, RCP, TMP = cv(4, P), cv(2, T), cv(T), cv(T)
    assert cv.at <= shared + 6 * TA, cv.at
    MSQ = ARENA[:, shared:shared + 2 * TA].rearrange("p (a b) -> p a b", a=2)

    def pc(name, i=0):
        c = PCOL[name] + i
        return PC[:, c:c + 1]

    loaded = sem("loaded")
    loaded_pool = sem("loaded_pool")
    consts = sem("consts")
    w_ready = [sem(f"w_ready{s}") for s in range(2)]
    slab_used = [sem(f"slab_used{s}") for s in range(2)]
    full = [sem(f"full{b}") for b in range(8)]
    freed = [sem(f"freed{b}") for b in range(8)]
    h_ready, x_normed = sem("h_ready"), sem("x_normed")
    sq_ready, rstd_ready = sem("sq_ready"), sem("rstd_ready")

    def wait_loaded(eng):
        eng.wait_ge(loaded, 4 * 16)
        eng.wait_ge(loaded_pool, 4 * 16)

    def wait(eng, s, v):
        if not (isinstance(v, int) and v <= 0):
            eng.wait_ge(s, v)

    def repeat(eng, n, first, body):
        if first or n == 1:
            body(0)
        if n > 1:
            with eng.Fori(int(first), n) as i:
                body(i)

    def wait_unit(eng, st, u, b, ctx):
        if b >= 4 or (not ctx and b % 2 == 1):
            eng.wait_ge(slab_used[b - 4 if b >= 4 else b // 2], st["it"] + u + 1)
        else:
            eng.wait_ge(full[b], st["full", b] + u + 1)

    def wait_free(eng, st, b, j):
        wait(eng, freed[b], j + st["free", b])

    def pe_unit(pe, st, u, src, ctx, ready=None, kb=KT, banks=(0, 1)):
        for s in banks:
            pe.wait_ge(w_ready[s], (u + st["it"]) * 16 + 16)
            for m in range(2):
                b = 2 * s + m
                wait_free(pe, st, b, u)
                for k in range(kb):
                    if ready and s == banks[0] and m == 0:
                        pe.wait_ge(ready[0], ready[1](k))
                    mm = pe.matmul(PS[:, b, :], W[:, s, k * SLAB + m * P:k * SLAB + m * P + P],
                                   src[:, k, 0:T], start=k == 0, stop=k == kb - 1)
                mm.then_inc(slab_used[s] if m == 1 and not ctx else full[b], 1)
            if ctx:
                wait_free(pe, st, 4 + s, u)
                for m in range(2):
                    for k in range(kb):
                        mm = pe.matmul(PS[:, 4 + s, m * TC:(m + 1) * TC],
                                       W[:, s, k * SLAB + m * P:k * SLAB + m * P + P],
                                       src[:, k, T:TA], start=k == 0, stop=k == kb - 1)
                mm.then_inc(slab_used[s], 1)

    def pe_mod(pe, st, i):
        if i == 0:
            pe.wait_ge(sem("sc_ready"), 1)
        for s in range(2):
            pe.wait_ge(w_ready[s], 16 * (st["it"] + i + 1))
            if s == 0:
                wait_free(pe, st, 5, i)
            for m in range(2):
                c = 2 * (2 * s + m)
                for k in range(KT):
                    mm = pe.matmul(PS[:, 5, c:c + 2], W[:, s, k * SLAB + m * P:k * SLAB + m * P + P],
                                   SC[:, k, :], start=k == 0, stop=k == KT - 1)
            mm.then_inc(slab_used[s], 1)

    def pe_norm(pe, st):
        for k in range(KT):
            pe.wait_ge(sq_ready, st["sq"] + k + 1)
            if k == 0:
                wait_free(pe, st, 6, 0)
                if st.ctx:
                    wait_free(pe, st, 7, 0)
            mm = pe.matmul(PS[:, 6, :], ONES[:, :], H[:, k, 0:T], start=k == 0, stop=k == KT - 1)
            if k == KT - 1:
                mm.then_inc(full[6], 1)
            if st.ctx:
                mm = pe.matmul(PS[:, 7, 0:TC], ONES[:, :], H[:, k, T:TA], start=k == 0, stop=k == KT - 1)
                if k == KT - 1:
                    mm.then_inc(full[7], 1)

    def pe_units(pe, st):
        src = {"H": H, "Y": Y, "ACC": ACC}[st.at]
        if st.at == "H":
            ready = (h_ready, lambda k: st["hr"] - 8 + k + 1)
        else:
            ready = None
            if st.evs[0] == "mres":
                for b in (2, 3, 5) if st.ctx else (2, 3):
                    wait_free(pe, st, b, 0)
            elif st.prev.kind == "attn":
                src = OY
                for b in range(4):
                    wait_free(pe, st, b, 0)
                pe.wait_ge(freed[6], st["free", 6])
            else:
                pe.wait_ge(sem("y_ready"), 4)
                for b in range(4):
                    wait_free(pe, st, b, 0)
        first = any(st["free", b] == 0 for b in range(6 if st.ctx else 4))
        repeat(pe, len(st.evs), first, lambda u: pe_unit(pe, st, u, src, st.ctx, ready))

    def pe_tok(pe, st):
        pe.wait_ge(h_ready, st["hr"])
        for u in range(len(st.evs)):
            for s in range(2):
                pe.wait_ge(w_ready[s], (st["it"] + u) * 16 + 16)
                for t in range(st.nt):
                    if s == 0:
                        wait_free(pe, st, t, u)
                    for k in range(4):
                        mm = pe.matmul(PS[:, t, :], H[:, 4 * s + k, t * P:(t + 1) * P],
                                       W[:, s, k * BW:(k + 1) * BW],
                                       start=s == 0 and k == 0, stop=s == 1 and k == 3)
                    if t == st.nt - 1:
                        mm.then_inc(slab_used[s], 1)
                    elif s == 1:
                        mm.then_inc(full[t], 1)

    def pe_lru(pe, st):
        pe.wait_ge(sem("lru_w"), 16 * 8)
        for m in range(4):
            wait_free(pe, st, m, 0)
        for m in range(4):
            for g in range(2):
                b = (2 * m + g) % 4
                wait_free(pe, st, b, m // 2)
                pe.matmul(PS[:, b, :], LRUW[:, 4 * g + m, :], XA[:, m, :],
                          start=True, stop=True).then_inc(full[b], 1)

    def pe_up(pe, st):
        with pe.Fori(0, FI) as i:
            pe_unit(pe, st, i, H, False, (h_ready, lambda k: st["hr"] - 8 + k + 1))

    def pe_down(pe, st):
        half = FT // 2
        with pe.Fori(0, 2) as i:
            for q in range(2):
                for s in range(2):
                    pe.wait_ge(w_ready[s], i * 32 + (st["it"] + q) * 16 + 16)
                    pe.wait_ge(sem("hidden"), st["hid"] - FT + half * (s + 1))
                    for m in range(2):
                        b = 2 * q + m
                        if s == 0:
                            wait_free(pe, st, b, i)
                        for k in range(half):
                            mm = pe.matmul(PS[:, b, :], W[:, s, k * SLAB + m * P:k * SLAB + m * P + P],
                                           HID[:, half * s + k, :], start=s == 0 and k == 0,
                                           stop=s == 1 and k == half - 1)
                        if m == 1:
                            mm.then_inc(slab_used[s], 1)
                        elif s == 1:
                            mm.then_inc(full[b], 1)

    def pe_foxgate(pe, st):
        pe.wait_ge(h_ready, st["hr"])
        wait_free(pe, st, 6, 0)
        for k in range(KT):
            mm = pe.matmul(PS[0:8, 6, :], WFS[:, k, :], H[:, k, 0:T], start=k == 0, stop=k == KT - 1)
        mm.then_inc(full[6], 1)
        pe.wait_ge(sem("fox_cum"), 1)
        wait_free(pe, st, 7, 0)
        for t in range(4):
            mm = pe.transpose(PS[:, 7, 8 * t:8 * t + 8], FROW[0:8, 3, t * P:(t + 1) * P], IDENT[0:8, 0:8])
        mm.then_inc(full[7], 1)

    def pe_sgu(pe, st):
        pe.wait_ge(sem("gv_ready"), 4)
        pe.wait_ge(sem("sgu_loaded"), 32)
        pe.wait_ge(sem("wt_masked"), 1)
        for t in range(4):
            wait_free(pe, st, t, 0)
            for hh in range(2):
                pe.matmul(PS[64 * hh:64 * hh + 64, t, :], SEL[:, 2 * t + hh, 0:64],
                          BS[0:8, :].unsqueeze(1).broadcast_to([8, 4, P]), start=True, stop=False,
                          skip_group_check=True)
            for hh in range(2):
                for c in range(4):
                    mm = pe.matmul(PS[64 * hh:64 * hh + 64, t, c * P:(c + 1) * P],
                                   GT[:, c, (2 * t + hh) * 64:(2 * t + hh) * 64 + 64],
                                   WT[:, 2 * t + hh, :], start=False, stop=c == 3 and hh == 1,
                                   skip_group_check=True)
            mm.then_inc(full[t], 1)

    def eslot(j, slot):
        return slot + 2 * (j["n"] % 2) if len(j["comps"]) == 2 else slot

    def attn_bufs(st):
        if st.name == "fox":
            return FQ, FK, FV, FAT, FE, FL
        if st.name.startswith("da"):
            return Q, K, V, AT, DE, DL
        return Q, K, V, AT, E_, L_

    def mod_steps(n):
        return min(MOD, (n * (MOD + 1)) // 31)

    def pe_attn(pe, st):
        q_, k_, v_, at_, e_, l_ = attn_bufs(st)
        jobs = st.jobs

        def scores(j):
            if st.name == "fox" and j["qb"] == 0:
                wait_free(pe, st, 7, j["head"])
                pe.matmul(PS[:, 7, :], SEL[:, j["head"], :], FROW[0:8, 3, :], start=True,
                          stop=True).then_inc(full[7], 1)
            for c, use in zip(j["comps"], j["use"]):
                b, po, nk, k0 = 2 * c["slot"], c["po"], j["nk"], j["k0"]
                wait_free(pe, st, b, use)
                for o in range(0, nk, 512):
                    n = min(512, nk - o)
                    mm = pe.matmul(PS[:, b + o // 512, 0:n], q_[po:po + 64, j["tile"], j["q0"]:j["q0"] + P],
                                   k_[po:po + 64, j["tile"], k0 + o:k0 + o + n], start=True, stop=True)
                mm.then_inc(full[b], 1)

        def transposes(j):
            pe.wait_ge(sem(f"probs_{st.name}"), j["n"] + 1)
            wait_free(pe, st, 4, j["n"])
            slot = eslot(j, j["comps"][0]["slot"])
            for kb in range(j["nk"] // P):
                mm = pe.transpose(bank(4, j["nk"])[:, kb * P:(kb + 1) * P],
                                  e_[:, slot, kb * P:(kb + 1) * P], IDENT[:, :])
            mm.then_inc(full[4], 1)

        def values(j):
            pe.wait_ge(freed[4], st["free", 4] + j["n"] + 1)
            wait_free(pe, st, 6, j["out"])
            nkb, dv, po = j["nk"] // P, j["dv"], j["po"]
            for kb in range(nkb):
                c0 = kb * P if j["causal"] else 0
                mm = pe.matmul(PS[po:po + dv, 6, c0:j["nq"]],
                               v_[:, j["k0"] // P + kb, j["head"] * dv:(j["head"] + 1) * dv],
                               at_[:, kb, c0:j["nq"]], start=kb == 0, stop=kb == nkb - 1,
                               skip_group_check=j["causal"])
            mm.then_inc(full[6], 1)
            if st.name.startswith("da"):
                pe.wait_ge(sem(f"o_sq_{st.name}"), j["out"] + 1)
                wait_free(pe, st, 7, j["out"])
                pe.matmul(PS[:, 7, 0:j["nq"]], ONES[:, :], l_[:, 0, 0:j["nq"]], start=True,
                          stop=True).then_inc(full[7], 1)

        if st.name == "fox":
            pe.wait_ge(freed[7], st["free", 7])
        elif st.name.startswith("da"):
            pe.wait_ge(sem(f"rope_done{st.layer}"), 8)
        for b in range(6):
            wait_free(pe, st, b, 0)
        ahead = 3 - len(jobs[0]["comps"])
        for j in jobs[:ahead]:
            scores(j)
        mod = 0
        for j in jobs:
            if j["n"] + ahead < len(jobs):
                scores(jobs[j["n"] + ahead])
            transposes(j)
            if j["last"]:
                values(j)
            if st.name == "fox" and mod < mod_steps(j["n"]):
                pe_mod(pe, st, mod)
                mod += 1
        assert mod == (MOD if st.name == "fox" else 0)

    def pe_rope(pe, st):
        pe.wait_ge(sem(f"rope_loaded{st.layer}"), 32)
        for n in range(8):
            b, buf = 6 + n % 2, (Q, K)[n // 4]
            wait_free(pe, st, b, n // 2)
            pe.matmul(PS[:, b, :], ROT[:, :], buf[:, n % 4, 0:T], start=True, stop=True).then_inc(full[b], 1)

    def pe_merge(pe, st):
        wait_y(pe, st)
        with pe.Fori(0, 4) as i:
            pe_unit(pe, st, i, H, st.ctx, None, KT, banks=(0,))
            pe_unit(pe, st, i, YT, st.ctx, None, 4, banks=(1,))

    def wait_y(pe, st):
        if st.n == 1:
            pe.wait_ge(sem(f"ml_y{st.layer}"), 4)
        elif st.n == 0:
            pe.wait_ge(sem(f"da_y{st.layer}"), 8 if st.ctx else 4)
        else:
            pe.wait_ge(freed[6], st["free", 6])

    def pe_mlgate(pe, st):
        pe.wait_ge(sem(f"wg_loaded{st.layer}"), 16)
        pe.wait_ge(h_ready, st["hr"])
        for g in range(2):
            t0, n = ((0, T), (T, TC))[g]
            for f in range(2):
                wait_free(pe, st, 6 + f, g)
                for k in range(KT):
                    mm = pe.matmul(PS[0:8, 6 + f, 0:n], WGS[:, k, 8 * f:8 * f + 8], H[:, k, t0:t0 + n],
                                   start=k == 0, stop=k == KT - 1)
                mm.then_inc(full[6 + f], 1)
        pe.wait_ge(sem(f"ml_rows{st.layer}"), 1)
        wait_free(pe, st, 0, 0)
        for d in range(2):
            for sbk in range(6):
                mm = pe.transpose(PS[:, 0, (6 * d + sbk) * 8:(6 * d + sbk) * 8 + 8],
                                  (A0, A1)[d][0:8, sbk * P:(sbk + 1) * P], IDENT[0:8, 0:8])
        mm.then_inc(full[0], 1)

    def pe_mlstm(pe, st):
        pe.wait_ge(sem(f"bqk{st.layer}"), 8)
        for b in range(8):
            wait_free(pe, st, b, 0)
        blocks = [(ps, i) for ps in st.passes for i in range(len(ps["blocks"]))]

        def qk(n):
            ps, i = blocks[n]
            h, d, nq, q0 = ps["h"], ps["d"], ps["nq"], T * ps["g"]
            if i == 0:
                if n:
                    pe.wait_ge(sem(f"decay{st.layer}"), n)
                wait_free(pe, st, 5, ps["p"])
                pe.matmul(PS[:, 4, 0:nq], SEL[:, 4 * d + h, :], (M0, M1)[d][0:8, q0:q0 + nq], start=True,
                          stop=True)
                pe.matmul(PS[:, 5, 0:nq], SEL[:, 4 * d + h, :], (B0, B1)[d][0:8, q0:q0 + nq], start=True,
                          stop=True).then_inc(full[5], 1)
            s_, t0, t1, _ = ps["blocks"][i]
            wait_free(pe, st, n % 2, n // 2)
            pe.matmul(PS[:, n % 2, t0:t1], K[:, h, s_ * P:(s_ + 1) * P], Q[:, h, q0 + t0:q0 + t1],
                      start=True, stop=True).then_inc(full[n % 2], 1)

        qk(0)
        for n, (ps, i) in enumerate(blocks):
            if n + 1 < len(blocks):
                qk(n + 1)
            s_, t0, t1, _ = ps["blocks"][i]
            nb, p, h = len(ps["blocks"]), ps["p"], ps["h"]
            num = 2 + 4 * (p % 2)
            pe.wait_ge(freed[n % 2], st["free", n % 2] + n // 2 + 1)
            if i == 0:
                wait_free(pe, st, num, p // 2)
            pe.matmul(PS[:, num, t0:t1], V[:, s_, h * P:(h + 1) * P], ZM[:, n % 2, t0:t1],
                      start=i == 0, stop=i == nb - 1, skip_group_check=True)
            mm = pe.matmul(PS[:, num + 1, t0:t1], ONES[:, :], ZM[:, n % 2, t0:t1],
                           start=i == 0, stop=i == nb - 1, skip_group_check=True)
            if i == nb - 1:
                mm.then_inc(full[num], 1)

    def pe_mlout(pe, st):
        for h in range(4):
            pe.wait_ge(sem(f"ml_sq{st.layer}"), h + 1)
            wait_free(pe, st, 6, h)
            pe.matmul(PS[:, 6, :], ONES[:, :], MSQ[:, h % 2, 0:T], start=True, stop=True).then_inc(full[6], 1)
            if st.ctx:
                wait_free(pe, st, 7, h)
                pe.matmul(PS[:, 7, 0:TC], ONES[:, :], MSQ[:, h % 2, T:TA], start=True,
                          stop=True).then_inc(full[7], 1)

    def act_norm(act, own, st):
        for m in range(KT):
            if st.src == "load":
                if m == 0:
                    wait_loaded(act)
            elif st.src == "xn":
                act.wait_ge(x_normed, st["xn"] - KT + m + 1)
            else:
                act.wait_ge(freed[m % 4], st.prev["free", m % 4] + m // 4 + 1)
                if st.ctx and st.prev.ctx:
                    c = 4 + m % 4 // 2
                    act.wait_ge(freed[c], st.prev["free", c] + m // 4 + 1)
            ins = act.activation(H[:, m, 0:T], X[:, m, :], ACT.Square)
            if st.ctx:
                ins = act.activation(H[:, m, T:TA], XC[:, m, :], ACT.Square)
            ins.then_inc(sq_ready, 1)
        for b, t0, t1 in ((6, 0, T), (7, T, TA))[:1 + st.ctx]:
            act.wait_ge(full[b], st["full", b] + 1)
            act.activation(RST[:, t0:t1], bank(b, t1 - t0), ACT.Ln, bias=EPSC[:, 0:1],
                           scale=1.0 / D).then_inc(freed[b], 1)
            act.wait_ge(freed[b], st["free", b] + 1)
            act.activation(RST[:, t0:t1], RST[:, t0:t1], ACT.Exp, scale=-0.5).then_inc(rstd_ready, 1)

    def act_prep(act, own, st):
        act.wait_ge(consts, 9)
        wait_loaded(act)
        c0 = PCOL["c"]
        act.activation(SC[:, :, :].rearrange("p a b -> p (a b)"), PC[:, c0:c0 + 16],
                       ACT.Silu).then_inc(sem("sc_ready"), 1)
        act.wait_ge(sem("lam_sum"), 1)
        act.activation(SMALL[:, 60:64], SMALL[:, 56:60], ACT.Exp).then_inc(sem("lam_exp"), 1)
        lam = PC[:, PCOL["lru_lambda"]:PCOL["lru_lambda"] + 4]
        own.link(act.activation(NSP[:, 0, :], lam, ACT.Abs))
        act.activation(NSP[:, 1, :], NSP[:, 0, :], ACT.Exp, scale=-1.0).then_inc(sem("lru_e"), 1)
        act.wait_ge(sem("lru_1e"), 1)
        act.activation(NSP[:, 3, :], NSP[:, 2, :], ACT.Ln).then_inc(sem("lru_ln"), 1)

    def act_units(act, own, st):
        for u, ev in enumerate(st.evs):
            if ev == "xa":
                for m in range(4):
                    wait_unit(act, st, u, m, False)
                    act.activation(XA[:, m, :], PS[:, m, :], ACT.Identity, bias=pc("lru_conv", 5 * m + 4),
                                   scale=pc("lru_conv", 5 * m + 3)).then_inc(sem("xa_scaled"), 1)
            elif ev in ("ga", "u"):
                dst = GA if ev == "ga" else UU
                for m in range(4):
                    wait_unit(act, st, u, m, False)
                    act.activation(dst[:, m, :], PS[:, m, :], ACT.Gelu_apprx_tanh).then_inc(freed[m], 1)
            elif ev in ("az", "cz", "bo"):
                fn = ACT.Sigmoid if ev == "bo" else ACT.Silu
                for s in range(2):
                    for m in (2 * s, 2 * s + 1):
                        wait_unit(act, st, u, m, st.ctx)
                        act.activation(Z[:, m, 0:T], PS[:, m, :], fn).then_inc(freed[m], 1)
                    if st.ctx:
                        wait_unit(act, st, u, 4 + s, True)
                        act.activation(Z[:, 2 * s:2 * s + 2, T:TA],
                                       PS[:, 4 + s, :].rearrange("p (a b) -> p a b", a=2),
                                       fn).then_inc(freed[4 + s], 1)
            elif ev == "bz":
                for s in range(2):
                    for b in (2 * s, 2 * s + 1, 4 + s)[:2 + st.ctx]:
                        wait_unit(act, st, u, b, st.ctx)
                        act.activation(PS[:, b, :], PS[:, b, :], ACT.Silu).then_inc(sem(f"bz{st.layer}"), 1)
            elif ev in ("bq", "bk"):
                dst, c0 = (Q, 0) if ev == "bq" else (K, 4)
                n0 = conv_no(st, u)
                for b in (2, 3, 5):
                    act.wait_ge(freed[b], st["free", b])
                for m in range(4):
                    w = 4 * (8 * st.layer + c0 + m)
                    wait_unit(act, st, u, m, st.ctx)
                    ins = act.activation(CV[:, m % 2, 0:T], PS[:, m, :], ACT.Identity,
                                         bias=pc("ml_conv", w + 3), scale=pc("ml_conv", w + 1))
                    if st.ctx:
                        c = 4 + m // 2
                        wait_unit(act, st, u, c, True)
                        ins = act.activation(CV[:, m % 2, T:TA], PS[:, c, m % 2 * TC:(m % 2 + 1) * TC],
                                             ACT.Identity, bias=pc("ml_conv", w + 3),
                                             scale=pc("ml_conv", w + 1))
                    ins.then_inc(sem(f"cv_scaled{st.layer}"), 1)
                    act.wait_ge(freed[m], st["free", m] + u + 1)
                    if st.ctx and m % 2:
                        act.wait_ge(freed[4 + m // 2], st["free", 4 + m // 2] + u + 1)
                    elif st.ctx:
                        act.wait_ge(sem(f"cv_done{st.layer}"), (n0 + m) // 2 + 1)
                    n = TA if st.ctx else T
                    act.activation(dst[:, m, 0:n], CV[:, m % 2, 0:n],
                                   ACT.Silu).then_inc(sem(f"bqk{st.layer}"), 1)

    def conv_no(st, u):
        if st.layer == 0:
            return 4 * u
        return 0 if st.evs[u] == "bk" else 4

    def act_tok(act, own, st):
        for u, ev in enumerate(st.evs):
            if ev == "g":
                for t in range(4):
                    wait_tok(act, st, u, t)
                    act.activation(GT[:, t, :], PS[:, t, :], ACT.Gelu_apprx_tanh).then_inc(freed[t], 1)
        if st.evs[0] == "g":
            for t in range(4):
                act.wait_ge(sem("sgu_ms"), t + 1)
                own.link(act.activation(GMS[:, t, :], GMS[:, t, :], ACT.Ln, bias=EPSC[:, 0:1], scale=1.0 / 64))
                act.activation(GMS[:, t, :], GMS[:, t, :], ACT.Exp, scale=-0.5).then_inc(sem("sgu_rs"), 1)

    def wait_tok(eng, st, u, t):
        if t == st.nt - 1:
            eng.wait_ge(slab_used[1], st["it"] + u + 1)
        else:
            eng.wait_ge(full[t], st["full", t] + u + 1)

    def act_lru(act, own, st):
        for m in range(4):
            for g in range(2):
                b = (2 * m + g) % 4
                act.wait_ge(full[b], st["full", b] + m // 2 + 1)
                act.activation((RG, IG)[g][:, m, :], PS[:, b, :], ACT.Sigmoid,
                               bias=pc(("lru_ba", "lru_bx")[g], m)).then_inc(freed[b], 1)
        act.wait_ge(sem("lru_sp"), 1)
        for m in range(4):
            act.wait_ge(freed[2 * m % 4], st["free", 2 * m % 4] + m // 2 + 1)
            act.activation(AG[:, m, :], RG[:, m, :], ACT.Exp, scale=NSP[:, 6, m:m + 1])
            act.activation(TH[:, m, :], RG[:, m, :], ACT.Tanh, scale=NSP[:, 7, m:m + 1]).then_inc(sem("lru_a"), 1)
        for m in range(4):
            act.wait_ge(sem("lru_t"), m + 1)
            act.activation(TH[:, m, :], TH[:, m, :], ACT.Sqrt).then_inc(sem("lru_s"), 1)

    def act_up(act, own, st):
        cb, sg, hid = (sem(n) for n in ("cb_scaled", "silu_done", "hidden"))
        base = PCOL[f"ffn_conv{st.layer}"]
        with act.Fori(0, FI) as i:
            for m in range(4):
                wait_unit(act, st, i, m, False)
                act.activation(CB[:, m, :], PS[:, m, :], ACT.Identity,
                               bias=PC[:, bass.ds(i * 16 + (base + 4 * m + 3), 1)],
                               scale=PC[:, bass.ds(i * 16 + (base + 4 * m + 2), 1)]).then_inc(cb, 1)
            for m in range(2):
                act.wait_ge(freed[m], i + (st["free", m] + 1))
                act.activation(SG[:, m, :], CB[:, m, :], ACT.Silu).then_inc(sg, 1)
            act.wait_ge(hid, i * 2 + (st["hid"] + 2))

    def act_foxgate(act, own, st):
        z, lz = FROW[0:8, 0, :], FROW[0:8, 1, :]
        act.wait_ge(full[6], st["full", 6] + 1)
        act.activation(z, PS[0:8, 6, :], ACT.Identity, bias=PC[0:8, PCOL["fox_bf"]:PCOL["fox_bf"] + 1],
                       ).then_inc(freed[6], 1)
        act.wait_ge(freed[6], st["free", 6] + 1)
        own.link(act.activation(lz, z, ACT.Abs))
        own.link(act.activation(lz, lz, ACT.Exp, scale=-1.0))
        act.activation(lz, lz, ACT.Ln, bias=1.0).then_inc(sem("fox_l"), 1)

    SCALE = 0.125

    def col(base, j, ci):
        c = base + 4 * (j["n"] % 2) + ci
        return SMALL[:, c:c + 1]

    def act_attn(act, own, st):
        q_, k_, v_, at_, e_, l_ = attn_bufs(st)
        jobs, name = st.jobs, st.name
        da = name.startswith("da")

        def exps(j):
            for ci, (c, use) in enumerate(zip(j["comps"], j["use"])):
                s, nk = c["slot"], j["nk"]
                es = eslot(j, s)
                act.wait_ge(sem(f"max_{name}"), j["n"] * len(j["comps"]) + ci + 1)
                if j["raw"]:
                    act.activation(e_[:, es, 0:nk], bank(2 * s, nk), ACT.Exp, bias=col(0, j, ci), scale=SCALE,
                                   accum_out=col(16, j, ci)).then_inc(freed[2 * s], 1)
                else:
                    act.activation(e_[:, es, 0:nk], l_[:, s, 0:nk], ACT.Exp, bias=col(0, j, ci),
                                   accum_out=col(16, j, ci)).then_inc(sem(f"exp_{name}"), 1)

        def evac(j):
            act.wait_ge(full[4], st["full", 4] + j["n"] + 1)
            nkb = j["nk"] // P
            act.activation(at_[:, 0:nkb, j["qcol"]:j["qcol"] + P],
                           bank(4, j["nk"]).rearrange("p (a b) -> p a b", b=P), ACT.Copy).then_inc(freed[4], 1)

        def post(j):
            nq, o = j["nq"], j["out"]
            act.wait_ge(full[6], st["full", 6] + o + 1)
            act.activation(l_[:, 0, 0:nq], PS[:, 6, 0:nq], ACT.Square).then_inc(sem(f"o_sq_{name}"), 1)
            act.wait_ge(full[7], st["full", 7] + o + 1)
            act.activation(l_[:, 1, 0:nq], PS[:, 7, 0:nq], ACT.Ln, bias=EPSC[:, 0:1],
                           scale=1.0 / P).then_inc(freed[7], 1)
            act.wait_ge(freed[7], st["free", 7] + o + 1)
            act.activation(l_[:, 1, 0:nq], l_[:, 1, 0:nq], ACT.Exp, scale=-0.5).then_inc(sem(f"o_rs_{name}"), 1)

        ahead = 1 if da else 2
        for j in jobs[:ahead]:
            exps(j)
        for j in jobs:
            nxt = jobs[j["n"] + ahead] if j["n"] + ahead < len(jobs) else None
            if nxt and da:
                exps(nxt)
            evac(j)
            if nxt and not da:
                exps(nxt)
            if da and j["last"]:
                post(j)

    def act_merge(act, own, st):
        with act.Fori(0, 4) as i:
            for m, b in enumerate((0, 1, 4)[:2 + st.ctx]):
                wait_unit(act, st, i, b, st.ctx)
                act.wait_ge(freed[(2, 3, 5)[m]], i + st["free", (2, 3, 5)[m]])
                act.activation(GB[:, m, :], PS[:, b, :], ACT.Sigmoid).then_inc(freed[b], 1)

    def act_mlgate(act, own, st):
        for g in range(2):
            t0, n = ((0, T), (T, TC))[g]
            act.wait_ge(full[7], st["full", 7] + g + 1)
            act.activation(LX[0:8, t0:t0 + n], PS[0:8, 7, 0:n], ACT.Identity,
                           bias=PC[0:8, PCOL["gate_bf"] + st.layer:PCOL["gate_bf"] + st.layer + 1],
                           ).then_inc(freed[7], 1)
        act.wait_ge(freed[7], st["free", 7] + 2)
        own.link(act.activation(LF[0:8, :], LX[0:8, :], ACT.Abs))
        own.link(act.activation(LF[0:8, :], LF[0:8, :], ACT.Exp, scale=-1.0))
        act.activation(LF[0:8, :], LF[0:8, :], ACT.Ln, bias=1.0).then_inc(sem(f"ml_l{st.layer}"), 1)

    def act_mlstm(act, own, st):
        dz, mk, dab = (sem(f"{n}{st.layer}") for n in ("decay", "ml_mask", "den_abs"))
        act.wait_ge(freed[0], st["free", 0])

        def den(ps):
            p, nq = ps["p"], ps["nq"]
            num = 2 + 4 * (p % 2)
            act.wait_ge(full[num], st["full", num] + p // 2 + 1)
            if p:
                prev = 2 + 4 * ((p - 1) % 2)
                act.wait_ge(freed[prev], st["free", prev] + (p - 1) // 2 + 1)
            act.activation(TMP[:, 0:nq], PS[:, num + 1, 0:nq], ACT.Abs).then_inc(dab, 1)

        for ps in st.passes:
            h, d, nq, n0, p = ps["h"], ps["d"], ps["nq"], ps["n0"], ps["p"]
            act.wait_ge(full[5], st["full", 5] + p + 1)
            if p > 1:
                num = 2 + 4 * (p % 2)
                act.wait_ge(freed[num], st["free", num] + p // 2)
            act.activation(EM[:, p % 2, 0:nq], PS[:, 5, 0:nq], ACT.Exp, scale=-1.0).then_inc(freed[5], 1)
            act.wait_ge(mk, p + 1)
            for i, (s_, t0, t1, j) in enumerate(ps["blocks"]):
                n = n0 + i
                ac = AC[:, 6 * d + s_, 4 * d + h:4 * d + h + 1]
                wait(act, freed[n % 2], st["free", n % 2] + n // 2)
                if j is None:
                    ins = act.activation(DM[:, n % 2, t0:t1], PS[:, 4, t0:t1], ACT.Exp, bias=ac, scale=-1.0)
                else:
                    ins = act.activation(DM[:, n % 2, j * P:(j + 1) * P], MK[:, j, :], ACT.Exp, bias=ac,
                                         scale=-1.0)
                    r0, r1 = (t0 + P, t1) if d == 0 else (t0, t1 - P)
                    if r1 > r0:
                        ins = act.activation(DM[:, n % 2, r0:r1], PS[:, 4, r0:r1], ACT.Exp, bias=ac, scale=-1.0)
                ins.then_inc(dz, 1)
                if i == 0 and p:
                    den(st.passes[p - 1])
        den(st.passes[-1])

    def act_mlout(act, own, st):
        act.wait_ge(freed[2], st["free", 2])
        act.wait_ge(freed[6], st["free", 6])
        n = TA if st.ctx else T
        for h in range(4):
            act.activation(MSQ[:, h % 2, 0:n], YT[:, h, 0:n], ACT.Square).then_inc(sem(f"ml_sq{st.layer}"), 1)
            wait(act, sem(f"ml_y{st.layer}"), h)
            for b, t0, t1 in ((6, 0, T), (7, T, TA))[:1 + st.ctx]:
                act.wait_ge(full[b], st["full", b] + h + 1)
                act.activation(RST[:, t0:t1], PS[:, b, 0:t1 - t0], ACT.Ln, bias=EPSC[:, 0:1],
                               scale=1.0 / P).then_inc(freed[b], 1)
                act.wait_ge(freed[b], st["free", b] + h + 1)
            act.activation(RST[:, 0:n], RST[:, 0:n], ACT.Exp, scale=-0.5).then_inc(sem(f"ml_rs{st.layer}"), 1)

    def dve_norm(dve, own, st):
        if st.mode == "mod":
            dve.wait_ge(freed[5], st["free", 5])
            g0 = PCOL["norm_g"] + 16 * st.layer
            own.link(dve.scalar_tensor_tensor(
                out=MG[:, :, :].rearrange("p a b -> p (a b)"),
                in0=MODT[:, st.layer, 8:16, :].rearrange("p a b -> p (a b)"), scalar=1.0,
                in1=PC[:, g0:g0 + 16], op0=ALU.add, op1=ALU.mult))
        dve.wait_ge(rstd_ready, st["rs"] + 1 + st.ctx)
        for k in range(KT):
            if st.mode == "mod":
                for src, t0, t1, c in ((X, 0, T, 0), (XC, T, TA, 1)):
                    own.mark(dve.scalar_tensor_tensor(out=H[:, k, t0:t1], in0=src[:, k, :],
                                                      scalar=MG[:, k, c:c + 1], in1=RST[:, t0:t1],
                                                      op0=ALU.mult, op1=ALU.mult))
                own.wait()
                for t0, t1, c in ((0, T, 0), (T, TA, 1)):
                    ins = dve.tensor_scalar(H[:, k, t0:t1], H[:, k, t0:t1],
                                            MODT[:, st.layer, k, c:c + 1], None, ALU.add)
                ins.then_inc(h_ready, 1)
            else:
                dst = H[:, k, 0:T] if st.mode == "H" else X[:, k, :]
                dve.scalar_tensor_tensor(out=dst, in0=X[:, k, :], scalar=pc(st.g, k), in1=RST[:, 0:T],
                                         op0=ALU.mult, op1=ALU.mult).then_inc(
                                             h_ready if st.mode == "H" else x_normed, 1)

    def dve_prep(dve, own, st):
        wait_loaded(dve)
        own.link(dve.tensor_tensor(RST[:, 0:256], PR[:, 0:256], PR[:, 256:512], ALU.mult))
        dve.tensor_reduce(SMALL[:, 56:60], RST[:, 0:256].rearrange("p (a b) -> p a b", b=64), AX,
                          ALU.add).then_inc(sem("lam_sum"), 1)
        dve.wait_ge(sem("lam_exp"), 1)
        for l in range(LAYERS):
            init = 0.8 - 0.6 * float(np.exp(-0.3 * l))
            own.link(dve.tensor_tensor(LAM[:, l, 0:1], SMALL[:, 61 + 2 * l:62 + 2 * l],
                                       SMALL[:, 60 + 2 * l:61 + 2 * l], ALU.subtract))
            own.mark(dve.tensor_scalar(LAM[:, l, 1:2], LAM[:, l, 0:1], -init, None, ALU.add))
            own.mark(dve.tensor_scalar(DAG[:, l:l + 1], pc("da_g", l), 1.0 - init, None, ALU.mult))
        lam = PC[:, PCOL["lru_lambda"]:PCOL["lru_lambda"] + 4]
        tiny = 1e-30
        dve.wait_ge(sem("lru_e"), 1)
        dve.tensor_scalar(NSP[:, 2, :], NSP[:, 1, :], 1.0, None, ALU.add).then_inc(sem("lru_1e"), 1)
        dve.wait_ge(sem("lru_1e"), 1)
        own.link(dve.tensor_scalar(NSP[:, 4, :], NSP[:, 2, :], -1.0, tiny, ALU.add, ALU.add))
        own.link(dve.reciprocal(NSP[:, 4, :], NSP[:, 4, :]))
        dve.wait_ge(sem("lru_ln"), 1)
        own.link(dve.tensor_scalar(NSP[:, 5, :], NSP[:, 3, :], tiny, None, ALU.add))
        own.link(dve.tensor_tensor(NSP[:, 5, :], NSP[:, 5, :], NSP[:, 4, :], ALU.mult))
        own.link(dve.tensor_tensor(NSP[:, 5, :], NSP[:, 5, :], NSP[:, 1, :], ALU.mult))
        own.link(dve.tensor_scalar(NSP[:, 4, :], lam, -1.0, 0.0, ALU.mult, ALU.max))
        own.link(dve.tensor_tensor(NSP[:, 5, :], NSP[:, 5, :], NSP[:, 4, :], ALU.add))
        own.mark(dve.tensor_scalar(NSP[:, 6, :], NSP[:, 5, :], -8.0, None, ALU.mult))
        dve.tensor_scalar(NSP[:, 7, :], NSP[:, 5, :], 8.0, None, ALU.mult).then_inc(sem("lru_sp"), 1)

    def dve_mod(dve, st, i):
        flat = MODT[:, :, :, :].rearrange("p a b c -> p (a b c)")
        c = PCOL["b_mod"] + 8 * i
        dve.wait_ge(slab_used[1], st["it"] + i + 1)
        dve.tensor_tensor(flat[:, 8 * i:8 * i + 8], PS[:, 5, 0:8], PC[:, c:c + 8], ALU.add).then_inc(freed[5], 1)

    def dve_units(dve, own, st):
        for u, ev in enumerate(st.evs):
            if ev == "xa":
                for m in range(4):
                    dve.wait_ge(sem("xa_scaled"), m + 1)
                    for d in (1, 2, 3):
                        ins = dve.scalar_tensor_tensor(
                            out=XA[:, m, d:T], in0=PS[:, m, 0:T - d], scalar=pc("lru_conv", 5 * m + 3 - d),
                            in1=XA[:, m, d:T], op0=ALU.mult, op1=ALU.add)
                        if d < 3:
                            own.link(ins)
                    ins.then_inc(freed[m], 1)
            elif ev in ("cp", "q", "k"):
                dst = {"cp": CP, "q": FQ, "k": FK}[ev]
                for m in range(4):
                    wait_unit(dve, st, u, m, False)
                    dve.tensor_copy(dst[:, m, :], PS[:, m, :]).then_inc(freed[m], 1)
            elif ev == "vb":
                for m in range(4):
                    wait_unit(dve, st, u, m, False)
                    dve.wait_ge(freed[m], st["free", m] + u)
                    dve.tensor_tensor(PV[:, m, :], PS[:, m, :], CP[:, m, :], ALU.mult).then_inc(freed[m], 1)
                    dve.wait_ge(freed[m], st["free", m] + u + 1)
                    own.link(dve.tensor_scalar(YB[:, m, :], PV[:, m, :], pc("sconv", 4 * m + 2),
                                               pc("sconv", 4 * m + 3), ALU.mult, ALU.add))
                    for d in (1, 2):
                        own.link(dve.scalar_tensor_tensor(
                            out=YB[:, m, d:T], in0=PV[:, m, 0:T - d], scalar=pc("sconv", 4 * m + 2 - d),
                            in1=YB[:, m, d:T], op0=ALU.mult, op1=ALU.add))
            elif ev == "bp":
                for m in range(4):
                    wait_unit(dve, st, u, m, False)
                    dve.tensor_tensor(Y[:, 4 + m, :], PS[:, m, :], YB[:, m, :], ALU.mult).then_inc(freed[m], 1)
            elif ev == "res":
                for m in range(4):
                    wait_unit(dve, st, u, m, False)
                    k = 4 * u + m
                    dve.tensor_tensor(X[:, k, :], PS[:, m, :], X[:, k, :], ALU.add).then_inc(freed[m], 1)
            elif ev == "mres":
                for s in range(2):
                    for m in (2 * s, 2 * s + 1):
                        wait_unit(dve, st, u, m, st.ctx)
                        k = 4 * u + m
                        dve.scalar_tensor_tensor(out=X[:, k, :], in0=PS[:, m, :],
                                                 scalar=MODT[:, st.layer, 16 + k, 0:1], in1=X[:, k, :],
                                                 op0=ALU.mult, op1=ALU.add).then_inc(freed[m], 1)
                    if st.ctx:
                        wait_unit(dve, st, u, 4 + s, True)
                        for c in range(2):
                            k = 4 * u + 2 * s + c
                            ins = dve.scalar_tensor_tensor(out=XC[:, k, :], in0=PS[:, 4 + s, c * TC:(c + 1) * TC],
                                                           scalar=MODT[:, st.layer, 16 + k, 1:2],
                                                           in1=XC[:, k, :], op0=ALU.mult, op1=ALU.add)
                        ins.then_inc(freed[4 + s], 1)
            elif ev in ("aq", "ak", "cq", "ck"):
                dst = Q if ev[1] == "q" else K
                for s in range(2):
                    for m in (2 * s, 2 * s + 1):
                        wait_unit(dve, st, u, m, st.ctx)
                        dve.tensor_copy(dst[:, m, 0:T], PS[:, m, :]).then_inc(freed[m], 1)
                    if st.ctx:
                        wait_unit(dve, st, u, 4 + s, True)
                        dve.tensor_copy(dst[:, 2 * s:2 * s + 2, T:TA],
                                        PS[:, 4 + s, :].rearrange("p (a b) -> p a b", a=2)).then_inc(freed[4 + s], 1)
            elif ev == "bz":
                n = 0
                for s in range(2):
                    for b in (2 * s, 2 * s + 1, 4 + s)[:2 + st.ctx]:
                        n += 1
                        dve.wait_ge(sem(f"bz{st.layer}"), n)
                        if b < 4:
                            zz, pp = Z[:, b, 0:T], PS[:, b, :]
                        else:
                            zz = Z[:, 2 * s:2 * s + 2, T:TA]
                            pp = PS[:, b, :].rearrange("p (a b) -> p a b", a=2)
                        dve.tensor_tensor(zz, pp, zz, ALU.mult).then_inc(freed[b], 1)
            elif ev in ("bq", "bk"):
                c0 = 0 if ev == "bq" else 4
                n0 = conv_no(st, u)
                done = sem(f"cv_done{st.layer}")
                for m in range(4):
                    w = 4 * (8 * st.layer + c0 + m)
                    dve.wait_ge(sem(f"cv_scaled{st.layer}"), n0 + m + 1)
                    b = CV[:, m % 2, :]
                    parts = [(0, T, PS[:, m, :])]
                    if st.ctx:
                        parts.append((T, TA, PS[:, 4 + m // 2, m % 2 * TC:(m % 2 + 1) * TC]))
                    for t0, t1, p_ in parts:
                        own.mark(dve.scalar_tensor_tensor(out=b[:, t0 + 1:t1], in0=p_[:, 0:t1 - t0 - 1],
                                                          scalar=pc("ml_conv", w), in1=b[:, t0 + 1:t1],
                                                          op0=ALU.mult, op1=ALU.add))
                    own.wait()
                    for t0, t1, p_ in parts:
                        ins = dve.scalar_tensor_tensor(out=b[:, t0:t1 - 1], in0=p_[:, 1:t1 - t0],
                                                       scalar=pc("ml_conv", w + 2), in1=b[:, t0:t1 - 1],
                                                       op0=ALU.mult, op1=ALU.add)
                        if t0 == 0:
                            ins.then_inc(freed[m], 1)
                        else:
                            ins.then_inc(freed[4 + m // 2] if m % 2 else done, 1)

    def dve_tok(dve, own, st):
        for u, ev in enumerate(st.evs):
            if ev == "g":
                for t in range(4):
                    dve.wait_ge(freed[t], st["free", t] + 1)
                    own.link(dve.tensor_tensor(GSQ[:, t, :], GT[:, t, :], GT[:, t, :], ALU.mult))
                    dve.tensor_reduce(GMS[:, t, :], GSQ[:, t, :].rearrange("p (a b) -> p a b", b=64), AX,
                                      ALU.add).then_inc(sem("sgu_ms"), 1)
                for t in range(4):
                    dve.wait_ge(sem("sgu_rs"), t + 1)
                    own.link(dve.tensor_tensor(GT[:, t, :].rearrange("p (a b) -> p a b", b=64),
                                               GT[:, t, :].rearrange("p (a b) -> p a b", b=64),
                                               GMS[:, t, :].unsqueeze(2).broadcast_to([P, 8, 64]), ALU.mult))
                    dve.tensor_tensor(GT[:, t, :], GT[:, t, :], PR[:, 512:1024], ALU.mult).then_inc(
                        sem("gv_ready"), 1)
            else:
                dst = FV if ev == "v" else V
                for t in range(st.nt):
                    wait_tok(dve, st, u, t)
                    dve.tensor_copy(dst[:, t, :], PS[:, t, :]).then_inc(freed[t], 1)

    def dve_lru(dve, own, st):
        for m in range(4):
            dve.wait_ge(sem("lru_a"), m + 1)
            own.link(dve.tensor_tensor(HS[:, m, :], AG[:, m, :], AG[:, m, :], ALU.mult))
            dve.scalar_tensor_tensor(out=TH[:, m, :], in0=HS[:, m, :], scalar=1.0, in1=TH[:, m, :],
                                     op0=ALU.add, op1=ALU.mult).then_inc(sem("lru_t"), 1)
        for m in range(4):
            b = (2 * m + 1) % 4
            dve.wait_ge(freed[b], st["free", b] + m // 2 + 1)
            own.link(dve.tensor_tensor(IG[:, m, :], IG[:, m, :], XA[:, m, :], ALU.mult))
            dve.wait_ge(sem("lru_s"), m + 1)
            own.link(dve.tensor_tensor(TH[:, m, :], TH[:, m, :], IG[:, m, :], ALU.mult))
            own.link(dve.tensor_tensor_scan(HS[:, m, :], AG[:, m, :], TH[:, m, :], 0.0, ALU.mult, ALU.add))
            dve.tensor_tensor(Y[:, m, :], HS[:, m, :], GA[:, m, :], ALU.mult).then_inc(sem("y_ready"), 1)

    def dve_up(dve, own, st):
        cb, sg, hid = (sem(n) for n in ("cb_scaled", "silu_done", "hidden"))
        base = PCOL[f"ffn_conv{st.layer}"]
        with own.loop(FI, 4) as i:
            for m in range(4):
                dve.wait_ge(cb, i * 4 + (st["cb"] + m + 1))
                for d in (1, 2):
                    ins = dve.scalar_tensor_tensor(
                        out=CB[:, m, d:T], in0=PS[:, m, 0:T - d],
                        scalar=PC[:, bass.ds(i * 16 + (base + 4 * m + 2 - d), 1)],
                        in1=CB[:, m, d:T], op0=ALU.mult, op1=ALU.add)
                    if d == 1:
                        own.link(ins)
                ins.then_inc(freed[m], 1)
            for m in range(2):
                dve.wait_ge(sg, i * 2 + (st["sg"] + m + 1))
                dve.wait_ge(freed[2 + m], i + (st["free", 2 + m] + 1))
                dve.tensor_tensor(ARENA[:, bass.ds(i * (2 * T) + m * T, T)], SG[:, m, :], CB[:, 2 + m, :],
                                  ALU.mult).then_inc(hid, 1)

    def dve_down(dve, own, st):
        for q in range(4):
            for m in range(2):
                b, k = 2 * (q % 2) + m, 2 * q + m
                if m:
                    dve.wait_ge(slab_used[1], st["it"] + q + 1)
                else:
                    dve.wait_ge(full[b], st["full", b] + q // 2 + 1)
                dve.tensor_tensor(X[:, k, :], PS[:, b, :], X[:, k, :], ALU.add).then_inc(freed[b], 1)

    def dve_foxgate(dve, own, st):
        z, lz, lf, cum = (FROW[0:8, i, :] for i in range(4))
        dve.wait_ge(sem("fox_l"), 1)
        own.link(dve.tensor_scalar(lf, z, 0.0, None, ALU.min))
        own.link(dve.tensor_tensor(lf, lf, lz, ALU.subtract))
        own.link(dve.memset(lz, 0.0))
        dve.tensor_tensor_scan(cum, lf, lz, 0.0, ALU.add, ALU.add).then_inc(sem("fox_cum"), 1)
        dve.wait_ge(full[7], st["full", 7] + 1)
        dve.tensor_copy(FCQ[:, :, :].rearrange("p a b -> p (a b)"), PS[:, 7, 0:32]).then_inc(freed[7], 1)

    def dve_sgu(dve, own, st):
        for t in range(4):
            dve.wait_ge(full[t], st["full", t] + 1)
            dve.tensor_tensor(OY[:, t, :], PS[:, t, :], UU[:, t, :], ALU.mult).then_inc(freed[t], 1)

    def dve_attn(dve, own, st):
        q_, k_, v_, at_, e_, l_ = attn_bufs(st)
        jobs, name = st.jobs, st.name
        da, fox = name.startswith("da"), name == "fox"
        if fox:
            dve.wait_ge(freed[7], st["free", 7])

        def maxima(j):
            for ci, (c, use) in enumerate(zip(j["comps"], j["use"])):
                s, nk, h = c["slot"], j["nk"], j["head"]
                b = 2 * s
                if fox:
                    dve.wait_ge(full[7], st["full", 7] + h + 1)
                    ins = dve.tensor_scalar(FT1[:, s, 0:nk], PS[:, 7, 0:nk], -1.0, FCQ[:, j["qb"], h:h + 1],
                                            ALU.mult, ALU.add)
                    if j["qb"] == 3:
                        ins.then_inc(freed[7], 1)
                        dve.wait_ge(freed[7], st["free", 7] + h + 1)
                    else:
                        own.link(ins)
                    own.link(dve.tensor_tensor(FT1[:, s, j["q0"]:nk], FT1[:, s, j["q0"]:nk], MCAUS[:, :],
                                               ALU.add))
                dve.wait_ge(full[b], st["full", b] + use + 1)
                src = bank(b, nk)
                if not j["raw"]:
                    if fox:
                        dve.scalar_tensor_tensor(out=l_[:, s, 0:nk], in0=src, scalar=SCALE, in1=FT1[:, s, 0:nk],
                                                 op0=ALU.mult, op1=ALU.add).then_inc(freed[b], 1)
                    else:
                        dve.wait_ge(sem(f"nb_{name}_{h % 2}"), 16 * (h // 2 + 1))
                        o = (7 - 2 * j["qb"] - 1) * 64
                        own.mark(dve.scalar_tensor_tensor(out=l_[:, s, 0:T], in0=PS[:, b, :], scalar=SCALE,
                                                          in1=NB[:, h % 2, o:o + T], op0=ALU.mult, op1=ALU.add))
                        dve.tensor_scalar(l_[:, s, T:TA], PS[:, b + 1, 0:TC], SCALE, None,
                                          ALU.mult).then_inc(freed[b], 1)
                    dve.wait_ge(freed[b], st["free", b] + use + 1)
                    src = l_[:, s, 0:nk]
                ins = dve.tensor_reduce(col(0, j, ci), src, AX, ALU.max, negate=True)
                if j["raw"]:
                    own.link(ins)
                    ins = dve.tensor_scalar(col(0, j, ci), col(0, j, ci), SCALE, None, ALU.mult)
                ins.then_inc(sem(f"max_{name}"), 1)

        def probs(j):
            pr = sem(f"probs_{name}")
            for ci, (c, use) in enumerate(zip(j["comps"], j["use"])):
                s = c["slot"]
                if j["raw"]:
                    dve.wait_ge(freed[2 * s], st["free", 2 * s] + use + 1)
                else:
                    dve.wait_ge(sem(f"exp_{name}"), c["ex"] + 1)
                own.link(dve.reciprocal(col(32, j, ci), col(16, j, ci)))
            s, nk = eslot(j, j["comps"][0]["slot"]), j["nk"]
            e0 = e_[:, s, 0:nk]
            if not da:
                dve.tensor_scalar(e0, e0, col(32, j, 0), None, ALU.mult).then_inc(pr, 1)
                return
            own.mark(dve.tensor_tensor(col(32, j, 1), col(32, j, 1), LAM[:, st.layer, 1:2], ALU.mult))
            own.link(dve.tensor_scalar(e0, e0, col(32, j, 0), None, ALU.mult))
            dve.scalar_tensor_tensor(out=e0, in0=e_[:, s + 1, 0:nk], scalar=col(32, j, 1), in1=e0,
                                     op0=ALU.mult, op1=ALU.add).then_inc(pr, 1)

        def post(j):
            nq, o, po, dv = j["nq"], j["out"], j["po"], j["dv"]
            c0 = 0 if nq == T else T
            src = PS[po:po + dv, 6, 0:nq]
            if fox:
                dve.wait_ge(full[6], st["full", 6] + o + 1)
                dve.tensor_copy(OY[po:po + dv, 4 + j["tile"], :], src).then_inc(freed[6], 1)
                return
            y = YT[po:po + dv, j["tile"], c0:c0 + nq]
            z = Z[po:po + dv, j["tile"], c0:c0 + nq]
            if da:
                dve.wait_ge(sem(f"o_rs_{name}"), o + 1)
                dve.scalar_tensor_tensor(out=y, in0=src, scalar=DAG[:, st.layer:st.layer + 1],
                                         in1=l_[:, 1, 0:nq], op0=ALU.mult, op1=ALU.mult).then_inc(freed[6], 1)
                dve.wait_ge(freed[6], st["free", 6] + o + 1)
                dve.tensor_tensor(y, y, z, ALU.mult).then_inc(sem(f"da_y{st.layer}"), 1)
            else:
                dve.wait_ge(full[6], st["full", 6] + o + 1)
                dve.tensor_tensor(y, src, z, ALU.mult).then_inc(freed[6], 1)

        ahead = 1 if da else 2
        for j in jobs[:ahead]:
            maxima(j)
        late, mod = None, 0
        for j in jobs:
            probs(j)
            if j["n"] + ahead < len(jobs):
                maxima(jobs[j["n"] + ahead])
            if late:
                post(late)
            late = j if j["last"] else None
            if fox and mod < mod_steps(j["n"] - 1):
                dve_mod(dve, st, mod)
                mod += 1
        post(late)
        if fox and mod < MOD:
            dve_mod(dve, st, mod)

    def dve_rope(dve, own, st):
        dve.wait_ge(sem(f"rope_loaded{st.layer}"), 32)
        for n in range(8):
            b, buf = 6 + n % 2, (Q, K)[n // 4]
            x_ = buf[:, n % 4, 0:T]
            dve.wait_ge(full[b], st["full", b] + n // 2 + 1)
            wait(dve, sem(f"rope_done{st.layer}"), n)
            own.mark(dve.tensor_tensor(RT1[:, :], x_, RC[:, :], ALU.mult))
            dve.tensor_tensor(RT2[:, :], PS[:, b, :], RS_[:, :], ALU.mult).then_inc(freed[b], 1)
            own.wait()
            dve.wait_ge(freed[b], st["free", b] + n // 2 + 1)
            dve.tensor_tensor(x_, RT1[:, :], RT2[:, :], ALU.add).then_inc(sem(f"rope_done{st.layer}"), 1)

    def dve_merge(dve, own, st):
        with own.loop(4, 0 if st.n == 0 else 2 + st.ctx) as i:
            for m, (g, b) in enumerate(((0, 2), (1, 3), (4, 5))[:2 + st.ctx]):
                wait_unit(dve, st, i, b, st.ctx)
                dve.wait_ge(freed[g], i + (st["free", g] + 1))
                if m < 2:
                    dst, gate, prod, tmp = (ARENA[:, bass.ds(i * (2 * TA) + m * TA, T)], GB[:, m, :],
                                            PS[:, b, :], TM[:, :])
                else:
                    dst = ACC[:, bass.ds(i * 2, 2), T:TA]
                    gate, prod, tmp = (v.rearrange("p (a b) -> p a b", a=2)
                                       for v in (GB[:, 2, :], PS[:, 5, :], TM[:, :]))
                if st.n == 0:
                    dve.tensor_tensor(dst, prod, gate, ALU.mult).then_inc(freed[b], 1)
                else:
                    last = ((5 if st.ctx else 3), 2, 3)[m]
                    dve.wait_ge(freed[last], i + (st["free", last] + (m > 0)))
                    own.link(dve.tensor_tensor(tmp, prod, gate, ALU.mult))
                    dve.tensor_tensor(dst, dst, tmp, ALU.add).then_inc(freed[b], 1)

    def dve_mlgate(dve, own, st):
        for g in range(2):
            t0, n = ((0, T), (T, TC))[g]
            dve.wait_ge(full[6], st["full", 6] + g + 1)
            dve.tensor_scalar(LI[0:8, t0:t0 + n], PS[0:8, 6, 0:n],
                              PC[0:8, PCOL["gate_bi"] + st.layer:PCOL["gate_bi"] + st.layer + 1], None,
                              ALU.add).then_inc(freed[6], 1)
        own.link(dve.memset(ZERO[0:8, :], 0.0))
        dve.wait_ge(sem(f"ml_l{st.layer}"), 1)
        own.link(dve.tensor_scalar(LX[0:8, :], LX[0:8, :], 0.0, None, ALU.min))
        own.link(dve.tensor_tensor(LF[0:8, :], LX[0:8, :], LF[0:8, :], ALU.subtract))
        dve.wait_ge(freed[6], st["free", 6] + 2)
        for d, (b_, a_, m_) in enumerate(((B0, A0, M0), (B1, A1, M1))):
            if d == 0:
                parts, seam = (slice(T, TA), slice(0, T)), TA - 1
            else:
                parts, seam = (slice(TA - 1, T - 1, -1), slice(T - 1, None, -1)), T
            for i, p_ in enumerate(parts):
                init = 0.0 if i == 0 else b_[0:8, seam:seam + 1]
                own.link(dve.tensor_tensor_scan(b_[0:8, p_], LF[0:8, p_], ZERO[0:8, p_], init,
                                                ALU.add, ALU.add))
            own.link(dve.tensor_tensor(a_[0:8, :], LI[0:8, :], b_[0:8, :], ALU.subtract))
            for i, p_ in enumerate(parts):
                init = 0.0 if i == 0 else m_[0:8, seam:seam + 1]
                own.link(dve.tensor_tensor_scan(m_[0:8, p_], a_[0:8, p_], a_[0:8, p_], init,
                                                ALU.max, ALU.max))
            ins = dve.tensor_tensor(b_[0:8, :], b_[0:8, :], m_[0:8, :], ALU.add)
            if d == 0:
                own.mark(ins)
            else:
                ins.then_inc(sem(f"ml_rows{st.layer}"), 1)
        dve.wait_ge(full[0], st["full", 0] + 1)
        dve.tensor_copy(AC[:, :, :].rearrange("p a b -> p (a b)"), PS[:, 0, 0:96]).then_inc(freed[0], 1)

    def dve_mlstm(dve, own, st):
        dz, mk, dab = (sem(f"{n}{st.layer}") for n in ("decay", "ml_mask", "den_abs"))

        def divide(ps, step):
            h, d, nq, p = ps["h"], ps["d"], ps["nq"], ps["p"]
            q0, num = T * ps["g"], 2 + 4 * (p % 2)
            y, c = YT[:, h, q0:q0 + nq], (step - 1) * P
            if step == 0:
                dve.wait_ge(dab, p + 1)
                own.link(dve.tensor_tensor(RCP[:, 0:nq], TMP[:, 0:nq], EM[:, p % 2, 0:nq], ALU.max))
            elif c < nq:
                own.link(dve.reciprocal(RCP[:, c:c + P], RCP[:, c:c + P]))
            else:
                dst = y if d == 0 else RCP[:, 0:nq]
                ins = dve.tensor_tensor(dst, PS[:, num, 0:nq], RCP[:, 0:nq], ALU.mult)
                if d == 1:
                    own.link(ins)
                    ins = dve.tensor_tensor(y, y, RCP[:, 0:nq], ALU.add)
                ins.then_inc(freed[num], 1)
                dve.wait_ge(freed[num], st["free", num] + p // 2 + 1)

        last = None
        for ps in st.passes:
            h, d, nq, n0, p, nb = ps["h"], ps["d"], ps["nq"], ps["n0"], ps["p"], ps["nb"]
            dve.wait_ge(full[5], st["full", 5] + p + 1)
            wait(dve, dz, n0)
            mask = (MFWD, MBWD)[d][:, :].unsqueeze(1).broadcast_to([P, nb, P])
            dve.tensor_tensor(MK[:, 0:nb, :], PS[:, 4, 0:nq].rearrange("p (a b) -> p a b", b=P), mask,
                              ALU.add).then_inc(mk, 1)
            nblocks = len(ps["blocks"])
            for i, (s_, t0, t1, j) in enumerate(ps["blocks"]):
                n = n0 + i
                dve.wait_ge(dz, n + 1)
                dve.wait_ge(full[n % 2], st["full", n % 2] + n // 2 + 1)
                dve.scalar_tensor_tensor(out=ZM[:, n % 2, t0:t1], in0=PS[:, n % 2, t0:t1],
                                         scalar=float(P) ** -0.5, in1=DM[:, n % 2, t0:t1],
                                         op0=ALU.mult, op1=ALU.mult).then_inc(freed[n % 2], 1)
                if last and i:
                    steps = last["nq"] // P + 2
                    for step in range(steps * (i - 1) // (nblocks - 1), steps * i // (nblocks - 1)):
                        divide(last, step)
            last = ps
        for step in range(last["nq"] // P + 2):
            divide(last, step)

    def dve_mlout(dve, own, st):
        n = TA if st.ctx else T
        for h in range(4):
            dve.wait_ge(sem(f"ml_rs{st.layer}"), h + 1)
            y = YT[:, h, 0:n]
            own.link(dve.scalar_tensor_tensor(out=y, in0=y, scalar=pc("ml_g", st.layer), in1=RST[:, 0:n],
                                              op0=ALU.mult, op1=ALU.mult))
            dve.tensor_tensor(y, y, Z[:, h, 0:n], ALU.mult).then_inc(sem(f"ml_y{st.layer}"), 1)

    def sp_slabs(sp, st, n, sources):
        def pair(i):
            for s, (src, size) in enumerate(sources(i)):
                wait(sp, slab_used[s], i + st["it"])
                sp.dma_start(W[:, s, 0:size], src.rearrange("a p n -> p (a n)")).then_inc(w_ready[s], 16)
        repeat(sp, n, st["it"] == 0, pair)

    def sp_stage(sp, st):
        S8 = KT * SLAB

        def both8(i):
            return [(w8[bass.ds(i * 2 + (st["w8"] + s), 1), :, :], S8) for s in range(2)]

        if st.kind == "attn" and st.name == "fox":
            sp_slabs(sp, st, MOD, both8)
        elif st.kind in ("units", "tok"):
            sp_slabs(sp, st, len(st.evs), both8)
        elif st.kind == "up":
            sp_slabs(sp, st, FI, both8)
        elif st.kind == "down":
            sp_slabs(sp, st, 4, lambda i: [(wd[bass.ds(i * 2 + (8 * st.layer + s), 1), :, :], 11 * SLAB)
                                           for s in range(2)])
        elif st.kind == "merge":
            sp_slabs(sp, st, 4, lambda i: [
                (w8[bass.ds(i + st["w8"], 1), :, :], S8),
                (wb[bass.ds(i + (12 * st.layer + 4 * st.n), 1), :, :], 4 * SLAB)])
        elif st.kind == "norm" and st.mode == "mod":
            if st.layer == 1:
                sp.wait_ge(sem("ml_rows0"), 1)
            sp.dma_start(WGS[:, :, :], wg_in[st.layer, :, :].rearrange("p (a b) -> p a b", a=KT)).then_inc(
                sem(f"wg_loaded{st.layer}"), 16)
        elif st.kind == "store":
            sp.wait_ge(x_normed, st["xn"])
            sp.dma_start(out, X[:, :, :]).then_inc(sem("stored"), 16)
            sp.wait_ge(sem("stored"), 16)

    PE = dict(norm=pe_norm, units=pe_units, tok=pe_tok, lru=pe_lru, up=pe_up, down=pe_down,
              foxgate=pe_foxgate, sgu=pe_sgu, attn=pe_attn, rope=pe_rope, merge=pe_merge,
              mlgate=pe_mlgate, mlstm=pe_mlstm, mlout=pe_mlout)
    SCALAR = dict(prep=act_prep, norm=act_norm, units=act_units, tok=act_tok, lru=act_lru, up=act_up,
                  foxgate=act_foxgate, attn=act_attn, merge=act_merge, mlgate=act_mlgate,
                  mlstm=act_mlstm, mlout=act_mlout)
    VECTOR = dict(prep=dve_prep, norm=dve_norm, units=dve_units, tok=dve_tok, lru=dve_lru, up=dve_up,
                  down=dve_down, foxgate=dve_foxgate, sgu=dve_sgu, attn=dve_attn, rope=dve_rope,
                  merge=dve_merge, mlgate=dve_mlgate, mlstm=dve_mlstm, mlout=dve_mlout)

    blocks = ExitStack()
    block = blocks.enter_context(nc.Block())

    @block.sync
    def _(sp):
        sp.dma_start(PC[:, :], params).then_inc(loaded, 16)
        sp.dma_start(PR[:, :], rows).then_inc(loaded, 16)
        for half in range(2):
            sp.dma_start(X[:, 4 * half:4 * half + 4, :], x[:, 4 * half:4 * half + 4, :]).then_inc(loaded, 16)
        for st in stages:
            sp_stage(sp, st)

    @block.gpsimd
    def _(pool):
        pool.memset(EPSC[:, :], EPS).then_inc(consts, 1)
        pool.memset(ONES[:, :], 1.0).then_inc(consts, 1)
        for v in (IDENT, MCAUS, MFWD, MBWD):
            pool.memset(v[:, :], 0.0).then_inc(consts, 1)
        pool.memset(SEL[:, :, :], 0.0).then_inc(consts, 1)
        pool.memset(LRUW[:, :, :], 0.0).then_inc(consts, 1)
        pool.wait_ge(consts, 8)
        pool.affine_select(out=IDENT[:, :], in_=IDENT[:, :], compare_op=ALU.not_equal, fill=1.0, base=0,
                           pattern=[[-1, P]], channel_multiplier=1)
        pool.affine_select(out=SEL[:, :, :], in_=SEL[:, :, :], compare_op=ALU.not_equal, fill=1.0, base=0,
                           pattern=[[-1, 8], [0, P]], channel_multiplier=1)
        pool.affine_select(out=MCAUS[:, :], in_=MCAUS[:, :], compare_op=ALU.is_ge, fill=-BIG, base=0,
                           pattern=[[-1, P]], channel_multiplier=1)
        pool.affine_select(out=MFWD[:, :], in_=MFWD[:, :], compare_op=ALU.is_ge, fill=BIG, base=0,
                           pattern=[[1, P]], channel_multiplier=-1)
        pool.affine_select(out=MBWD[:, :], in_=MBWD[:, :], compare_op=ALU.is_ge, fill=BIG, base=0,
                           pattern=[[-1, P]], channel_multiplier=1).then_inc(consts, 1)
        for half in range(2):
            pool.dma_start(XC[:, 4 * half:4 * half + 4, :], ctx_in[:, 4 * half:4 * half + 4, :]).then_inc(loaded_pool, 16)
        for src, dst in ((rot, ROT[:, :]), (wf_in.rearrange("p (a b) -> p a b", a=KT), WFS[:, :, :])):
            pool.dma_start(dst, src).then_inc(loaded_pool, 16)
        for g in range(2):
            for half in range(2):
                for q in range(2):
                    pool.dma_start(LRUW[64 * half:64 * half + 64, 4 * g + 2 * q:4 * g + 2 * q + 2,
                                        64 * half:64 * half + 64],
                                   lru_w[g, half, :, 2 * q:2 * q + 2, :]).then_inc(sem("lru_w"), 16)
        for st in stages:
            if st.kind == "foxgate":
                pool.wait_ge(h_ready, st["hr"])
                pool.dma_start(WT[:, :, :], sgu_w).then_inc(sem("sgu_loaded"), 16)
                pool.dma_start(BS[0:8, :], sgu_b).then_inc(sem("sgu_loaded"), 16)
                pool.wait_ge(sem("sgu_loaded"), 32)
                pool.affine_select(out=WT[:, :, :], in_=WT[:, :, :], compare_op=ALU.is_ge, fill=0.0, base=0,
                                   pattern=[[0, 8], [1, P]], channel_multiplier=-1).then_inc(sem("wt_masked"), 1)
            if st.kind == "rope":
                pool.wait_ge(h_ready, st["hr"])
                for dst, src in ((RC, rope[0, :, :]), (RS_, rope[1, :, :])):
                    pool.dma_start(dst[:, :], src).then_inc(sem(f"rope_loaded{st.layer}"), 16)
            if st.kind == "attn" and st.name.startswith("na"):
                pool.wait_ge(sem(f"ml_y{st.layer}"), 4)
                for h in range(8):
                    if h >= 2:
                        nj = sum(j["head"] < h - 1 for j in st.jobs)
                        pool.wait_ge(sem(f"probs_{st.name}"), nj)
                    pool.dma_start(NB[:, h % 2, :], nbias[st.layer, h, :, :]).then_inc(
                        sem(f"nb_{st.name}_{h % 2}"), 16)

    @block.scalar
    def _(act):
        own = Own(act, sem("act_step"))
        for st in stages:
            if st.kind in SCALAR:
                SCALAR[st.kind](act, own, st)

    @block.vector
    def _(dve):
        own = Own(dve, sem("dve_step"))
        for st in stages:
            if st.kind in VECTOR:
                VECTOR[st.kind](dve, own, st)

    @block.tensor
    def _(pe):
        pe.wait_ge(consts, 9)
        wait_loaded(pe)
        for st in stages:
            if st.kind in PE:
                PE[st.kind](pe, st)

    blocks.close()
    cx.close()


def _lay_out(a):
    def slabs(w, cols):
        return [w[:, c:c + SLAB].reshape(-1, P, SLAB).transpose(1, 0, 2).reshape(P, -1) for c in cols]

    def unit(w, c):
        return slabs(w, (c, c + SLAB))

    def unit_tok(w, c):
        return [w[4 * s * P:4 * (s + 1) * P, c:c + BW].reshape(4, P, BW).transpose(1, 0, 2).reshape(P, -1)
                for s in range(2)]

    even = dict(xa=0, ga=512, cp=1024, vb=2048, bp=1536)
    odd = dict(u=0, g=512, q=1024, k=1536, v=2048)
    h0 = 4 * BW
    hyb = dict(aq=0, ak=512, av=1024, az=1536, bq=h0, bk=h0 + 512, bv=h0 + 1024, bo=h0 + 1536, bz=h0 + 2048)
    h1 = 9 * BW + 16
    hyb.update(cq=h1, ck=h1 + 512, cv=h1 + 1024, cz=h1 + 1536)
    gm = h1 + 2048
    w8, wd, wb = [], [], []
    nres = 0
    for st in plan_stages():
        if st.name == "fox":
            for l in range(LAYERS):
                w8 += slabs(a["w_mod_2"][l], range(0, 3 * D, SLAB))
        elif st.kind in ("units", "tok"):
            put = unit if st.kind == "units" else unit_tok
            for u, ev in enumerate(st.evs):
                if ev == "res":
                    w8 += put((a["mix0_w_out"], a["mix1_w_out"])[nres // 2][0], BW * u)
                    nres += 1
                elif ev == "mres":
                    w8 += put(a["w_out_2"][st.layer], BW * u)
                elif ev in even:
                    w8 += put(a["mix0_w_in"][0], even[ev])
                elif ev in odd:
                    w8 += put(a["mix1_w_in"][0], odd[ev])
                else:
                    w8 += put(a["w_in_2"][st.layer], hyb[ev])
        elif st.kind == "up":
            for i in range(FI):
                w8 += slabs(a["ffn_up"][st.layer], (SLAB * i, F + SLAB * i))
        elif st.kind == "down":
            w = a["ffn_down"][st.layer]
            for q in range(4):
                for s in range(2):
                    wd += slabs(w[s * F // 2:(s + 1) * F // 2], (SLAB * q,))
        elif st.kind == "merge":
            for i in range(4):
                w8 += slabs(a["w_in_2"][st.layer], (gm + D * st.n + SLAB * i,))
                wb += slabs(a["w_br_2"][st.layer, st.n], (SLAB * i,))

    def cols(v):
        return np.asarray(v).reshape(-1, P).T

    def pad8(v):
        o = np.zeros((P, v.shape[1]), np.float32)
        o[:8] = v
        return o

    ffn = []
    for l in range(LAYERS):
        w = np.concatenate([a["ffn_conv_w"][l], a["ffn_conv_b"][l][None]])
        w = w.reshape(4, 2, FI, 2, P)
        ffn.append(w.transpose(4, 2, 1, 3, 0).reshape(P, FI * 16))
    taps = lambda w, b, n: np.concatenate([w, b[None]]).reshape(-1, n, P).transpose(2, 1, 0).reshape(P, -1)
    gb = a["ml_gate_b_2"]
    parts = dict(
        mix0_norm=cols(a["mix0_norm"]), lru_conv=taps(a["lru_conv_w"][0], a["lru_conv_b"][0], 4),
        lru_ba=cols(a["lru_ba"]), lru_bx=cols(a["lru_bx"]), lru_lambda=cols(a["lru_lambda"]),
        sconv=taps(a["sconv_w"][0], a["sconv_b"][0], 4), mix1_norm=cols(a["mix1_norm"]),
        ffn_norm0=cols(a["ffn_norm"][0]), ffn_norm1=cols(a["ffn_norm"][1]), final_norm=cols(a["final_norm"]),
        ffn_conv0=ffn[0], ffn_conv1=ffn[1],
        c=np.stack([cols(a["c_2"]), cols(a["c_ctx_2"])], 2).reshape(P, 16),
        b_mod=np.repeat(cols(a["b_mod_2"]), 2, 1), norm_g=np.repeat(cols(a["norm_g_2"]), 2, 1),
        da_g=cols(a["da_norm_g_2"]),
        ml_conv=np.concatenate([taps(a["ml_conv_w_2"][l], a["ml_conv_b_2"][l], 8) for l in range(LAYERS)], 1),
        ml_g=cols(a["ml_norm_g_2"]), final_g=cols(a["final_g_2"]), fox_bf=pad8(a["fox_bf"].reshape(8, 1)),
        gate_bi=pad8(gb[:, :, 0].reshape(LAYERS, 8).T), gate_bf=pad8(gb[:, :, 1].reshape(LAYERS, 8).T))
    params = np.concatenate([parts[n] for n, _ in PARAMS], 1)
    rows = np.concatenate([a["da_lam_q_2"].reshape(-1), a["da_lam_k_2"].reshape(-1), a["sgu_norm"].reshape(-1)])
    rows = np.broadcast_to(rows, (P, NROW))
    chan = lambda v: v[0].T.reshape(KT, P, -1).transpose(1, 0, 2)
    lru_w = np.stack([a["lru_wa"][0], a["lru_wx"][0]]).reshape(2, 4, 2, 64, 64).transpose(0, 2, 3, 1, 4)
    g0 = 9 * BW
    wg = a["w_in_2"][:, :, g0:g0 + 16].reshape(LAYERS, KT, P, 2, 2, 4).transpose(0, 2, 1, 4, 3, 5)
    wf = a["mix1_w_in"][0][:, 5 * BW:5 * BW + 8].reshape(KT, P, 8).transpose(1, 0, 2)
    rpb = a["na_rpb_2"]
    nb = np.full((LAYERS, 8, 2, 64, 14, 64), -BIG, np.float32)
    for c in range(64):
        lo = min(max(c - 8, 0), 48)
        for par in range(2):
            nb[:, :, par, c, :, lo:lo + 16] = rpb[:, :, 1 - par:15 - par, lo - c + 15:lo - c + 31]
    t = np.arange(T)
    inv = 10000.0 ** (-np.arange(0, 32, 2, dtype=np.float32) / np.float32(32))
    ang = np.concatenate([(t // 64)[:, None].astype(np.float32) * inv.astype(np.float32),
                          (t % 64)[:, None].astype(np.float32) * inv.astype(np.float32)], 1)
    ang = np.tile(np.repeat(ang.T, 2, 0), (2, 1)).astype(np.float32)
    rot = np.zeros((P, P), np.float32)
    for i in range(0, P, 2):
        rot[i + 1, i], rot[i, i + 1] = -1.0, 1.0
    d = dict(x=chan(a["x"]), ctx_in=chan(a["ctx_2"]), w8=np.stack(w8), wd=np.stack(wd), wb=np.stack(wb),
             wf_in=wf.reshape(P, -1), wg_in=wg.reshape(LAYERS, P, -1), params=params, rows=rows, lru_w=lru_w,
             sgu_w=a["sgu_w"][0].transpose(2, 0, 1), sgu_b=a["sgu_b"][0],
             rope=np.stack([np.cos(ang), np.sin(ang)]), rot=rot, nbias=nb.reshape(LAYERS, 8, P, 14 * 64))
    return {k: np.ascontiguousarray(v, dtype=np.float32) for k, v in d.items()}


def kernel(**inputs):
    import concourse.bacc as bacc
    from concourse.bass_utils import run_bass_kernel_spmd as run

    nc = bacc.Bacc("TRN2", target_bir_lowering=False, num_devices=1)
    laid = _lay_out({k: np.asarray(v) for k, v in inputs.items()})
    arrays, args = {}, {}
    for name, v in laid.items():
        arrays[f"in_{name}"] = v
        args[name] = nc.dram_tensor(f"in_{name}", v.shape, F32, kind="ExternalInput").ap()
    out = nc.dram_tensor("out", (P, KT, T), F32, kind="ExternalOutput").ap()
    build(nc, **args, out=out)
    r = run(nc, [arrays], core_ids=[0])
    got = np.asarray(r.results[0]["out"])
    return np.ascontiguousarray(got.transpose(2, 1, 0).reshape(1, T, D))
```

```python
from contextlib import ExitStack, contextmanager

import numpy as np
import concourse.bass as bass
from concourse import mybir

F32 = mybir.dt.float32
F32R = mybir.dt.float32r
ALU = mybir.AluOpType
ACT = mybir.ActivationFunctionType
AX = mybir.AxisListType.X

P = 128
D = 1024
KT = D // P
T = 512
TC = 256
TA = T + TC
SLAB = 256
F = 2816
FT = F // P
FI = F // SLAB
PARTS = (4, 4, 3)
BW = 512
LAYERS = 2
EPS = 1e-6
BIG = 1e30
AREN = 31744
MOD = LAYERS * 3 * D // BW

PARAMS = [("mix0_norm", 8), ("lru_conv", 4 * 5), ("lru_ba", 4), ("lru_bx", 4), ("lru_lambda", 4),
          ("sconv", 4 * 4), ("mix1_norm", 8), ("ffn_norm0", 8), ("ffn_norm1", 8), ("final_norm", 8),
          ("ffn_conv0", FI * 16), ("ffn_conv1", FI * 16), ("c", 16), ("b_mod", 96), ("norm_g", 32),
          ("da_g", 2), ("ml_conv", 2 * 8 * 4), ("ml_g", 2), ("final_g", 8),
          ("fox_bf", 1), ("gate_bi", 2), ("gate_bf", 2)]
PCOL, _n = {}, 0
for _name, _c in PARAMS:
    PCOL[_name] = _n
    _n += _c
NPARAM = _n
ROWS = {"lam_q": 0, "lam_k": 256, "sgu_norm": 512}
NROW = 1024


class Stage:

    def __init__(self, kind, base, prev, evs=(), at="H", ctx=False, layer=0, nt=4, mode="", src="", g="",
                 n=0, name="", jobs=(), passes=(), split=False, first=False, final=False, step0=0, apart=False,
                 era="hybrid"):
        self.kind, self.base, self.prev = kind, base, prev
        self.evs, self.at, self.ctx, self.layer, self.nt = evs, at, ctx, layer, nt
        self.mode, self.src, self.g = mode, src, g
        self.n = n
        self.name, self.jobs, self.passes = name, jobs, passes
        self.split, self.first, self.final, self.step0 = split, first, final, step0
        self.era = era
        self.apart = apart
        self.after_apart = False

    def __getitem__(self, key):
        return self.base.get(key, 0)


class Own:

    def __init__(self, eng, sem):
        self.eng, self.sem, self.n, self.reg = eng, sem, 0, None

    def mark(self, ins):
        ins.then_inc(self.sem, 1)
        self.n += 1

    def wait(self):
        v = self.n if self.reg is None else self.reg[0] * self.reg[1] + self.n
        self.eng.wait_ge(self.sem, v)

    def link(self, ins):
        self.mark(ins)
        self.wait()

    @contextmanager
    def loop(self, count, per):
        start = self.n
        with self.eng.Fori(0, count) as i:
            self.reg = (i, per)
            yield i
            assert self.n - start == per, (self.n - start, per)
        self.n, self.reg = start + count * per, None


def plan_stages():
    base, out, loads = {}, [], [Stage("", {}, None)]

    def add(kind, counts, **args):
        out.append(Stage(kind, dict(base), out[-1] if out else None, **args))
        if "it" in counts:
            out[-1].after_apart = loads[-1].apart
            loads.append(out[-1])
        for k, v in counts.items():
            base[k] = base.get(k, 0) + v

    def full(*bs, n=1):
        return {("full", b): n for b in bs}

    def free(*bs, n=1):
        return {("free", b): n for b in bs}

    def norm(mode, src, g, ctx=False, layer=0, **kw):
        bs = (6, 7) if ctx else (6,)
        add("norm", {**full(*bs), **free(*bs), "sq": 8, "rs": len(bs),
                     **({"hr": 8} if mode in ("H", "mod") else {"xn": 8})},
            mode=mode, src=src, g=g, ctx=ctx, layer=layer, **kw)

    def splits(n, kw):
        return {"ws": n * kw.get("split", False), "hl": KT * kw.get("first", False)}

    def units(evs, at, ctx=False, layer=0, **kw):
        n = len(evs)
        add("units", {"it": n, "w8": 2 * n, **full(0, 2, n=n), **free(0, 1, 2, 3, n=n),
                      **(full(1, 3, n=n) if ctx else {}), **(free(4, 5, n=n) if ctx else {}), **splits(n, kw)},
            evs=evs, ctx=ctx, layer=layer, at=at, **kw)

    def tok(evs, nt=4, **kw):
        n = len(evs)
        add("tok", {"it": n, "w8": 2 * n, **full(*range(nt - 1), n=n), **free(*range(nt), n=n), **splits(n, kw),
                    "back": KT * (nt == 6)},
            evs=evs, nt=nt, **kw)

    def attn(name, jobs, **kw):
        use, nj, ex = {0: 0, 1: 0}, 0, 0
        for n, j in enumerate(jobs):
            j["n"] = n
            j["use"] = []
            for c in j["comps"]:
                j["use"].append(use[c["slot"]])
                use[c["slot"]] += 1
                c["ex"] = ex
                ex += not j["raw"]
            j["out"] = nj
            nj += j["last"]
        counts = {**full(0, n=use[0]), **free(0, n=use[0]), **full(2, n=use[1]), **free(2, n=use[1]),
                  **full(4, n=len(jobs)), **free(4, n=len(jobs)), **full(6, n=nj), **free(6, n=nj)}
        if name == "fox":
            counts.update(full(7, n=8))
            counts.update(free(7, n=8))
            counts.update({"it": MOD, "w8": 2 * MOD, **free(5, n=(MOD + 1) // 2), **free(1, n=MOD // 2)})
        if name.startswith("da"):
            counts.update(full(7, n=nj))
            counts.update(free(7, n=nj))
        add("attn", counts, name=name, jobs=jobs, **kw)

    norm("H", "load", "mix0_norm")
    units(["xa", "ga"], at="H", era="even", split=True, first=True)
    add("prep", {})
    add("lru", {**full(0, 1, 2, 3, n=2), **free(0, 1, 2, 3, n=2)})
    units(["cp", "vb", "bp"], at="H", era="even", split=True)
    units(["res", "res"], at="Y", era="even", split=True, final=True)
    norm("H", "res", "ffn_norm0")
    for f in range(2):
        for part, n in enumerate(PARTS):
            add("up", {"it": n, "ws": n, "w8": 2 * n, **full(0, 2, n=n), **free(0, 1, 2, 3, n=n),
                       "cb": 4 * n, "sg": 2 * n, "hid": 2 * n, "hl": KT * (part == 0)}, layer=f, n=n, step0=sum(PARTS[:part]),
                split=True, apart=True, first=part == 0)
            add("down", {"it": 2, "ws": 2, "w8": 4, **full(0, 2, n=2), **free(0, 1, 2, 3, n=2)}, layer=f,
                n=2 * n, step0=sum(PARTS[:part]), split=True, apart=True, final=part == len(PARTS) - 1)
        if f == 0:
            norm("H", "down", "mix1_norm")
            add("foxgate", {**full(6, 7), **free(6, 7)})
            units(["u", "q", "k"], at="H", era="odd", split=True, first=True)
            tok(["g", "v"], era="odd", split=True, final=True)
            add("sgu", {**full(0, 1, 2, 3), **free(0, 1, 2, 3)})
            jobs = []
            for h in range(8):
                for qb in range(4):
                    jobs.append(dict(comps=[dict(slot=len(jobs) % 2, po=64 * (h % 2))], head=h, tile=h // 2,
                                     q0=128 * qb, k0=0, nk=128 * (qb + 1), qcol=128 * qb, first=qb == 0,
                                     last=qb == 3, nq=512, causal=True, raw=False, dv=64, po=64 * (h % 2), qb=qb))
            attn("fox", jobs)
            units(["res", "res"], at="Y", era="odd", split=True, first=True, final=True)
            norm("H", "res", "ffn_norm1")
    norm("X", "down", "final_norm")
    for l in range(LAYERS):
        ctx = l == 0
        norm("mod", "xn" if l == 0 else "res", "norm_g", ctx=True, layer=l)

        def branch(keys, rest, v):
            if ctx:
                units(keys + rest, at="H", ctx=True, layer=l, split=True, first=keys == ["ak"])
            else:
                units(keys, at="H", ctx=True, layer=l, split=True, first=keys == ["ak"])
                units(rest, at="H", ctx=False, layer=l, split=True)
            tok([v], nt=6, layer=l, split=True, final=True)

        def merge(n):
            add("merge", {"it": 4, "ws": 4, "hl": KT, "w8": 4, **full(0, 2, n=4), **free(0, 1, 2, 3, n=4),
                          **(full(1, 3, n=4) if ctx else {}), **(free(4, 5, n=4) if ctx else {}),
                          "gate": 12 if ctx else 8}, n=n, ctx=ctx, layer=l, split=True, apart=True, first=True)

        branch(["ak"], ["aq", "az"], "av")
        add("rope", {**full(6, 7, n=4), **free(6, 7, n=4)}, layer=l)
        jobs = []
        for h in range(4):
            for qb in range(6 if ctx else 4):
                lat = qb < 4
                jobs.append(dict(comps=[dict(slot=c, po=64 * c) for c in range(2)], head=h, tile=h,
                                 q0=128 * qb, k0=0 if lat else T, nk=TA if lat else TC,
                                 qcol=128 * qb if lat else 128 * (qb - 4), first=qb in (0, 4),
                                 last=qb in (3, 5), nq=512 if lat else 256, causal=False, raw=True, dv=128, po=0, qb=qb))
        attn(f"da{l}", jobs, layer=l)
        merge(0)
        branch(["bk"], ["bq", "bo", "bz"], "bv")
        add("mlgate", {**full(6, 7, n=2), **free(6, 7, n=2), **full(0), **free(0)}, layer=l)
        passes, n, np_ = [], 0, 0
        for h in range(4):
            for d in range(2):
                for g in range(2 if ctx else 1):
                    blocks = []
                    nb, nq = (4, 512) if g == 0 else (2, 256)
                    own = list(range(nb)) if d == 0 else list(range(nb))[::-1]
                    if g == 0:
                        blocks += [(4, 0, 512, None), (5, 0, 512, None)]
                    for j in own:
                        t0, t1 = (128 * j, nq) if d == 0 else (0, 128 * (j + 1))
                        blocks.append((j + 4 * g, t0, t1, j))
                    passes.append(dict(h=h, d=d, g=g, nq=nq, nb=nb, blocks=blocks, n0=n, p=np_))
                    n += len(blocks)
                    np_ += 1
        add("mlstm", {**full(0, n=(n + 1) // 2), **free(0, n=(n + 1) // 2), **full(1, n=n // 2),
                      **free(1, n=n // 2), **full(5, n=np_), **free(5, n=np_),
                      **full(2, n=(np_ + 1) // 2), **free(2, n=(np_ + 1) // 2),
                      **full(6, n=np_ // 2), **free(6, n=np_ // 2)}, layer=l, passes=passes, ctx=ctx)
        add("mlout", {**full(6, 7, n=4) , **free(6, 7, n=4)} if ctx else {**full(6, n=4), **free(6, n=4)},
            layer=l, ctx=ctx)
        merge(1)
        branch(["ck"], ["cq", "cz"], "cv")
        jobs = []
        for h in range(8):
            for qb in range(6 if ctx else 4):
                lat = qb < 4
                jobs.append(dict(comps=[dict(slot=len(jobs) % 2, po=64 * (h % 2))], head=h, tile=h // 2,
                                 q0=128 * qb, k0=0 if lat else T, nk=TA if lat else TC,
                                 qcol=128 * qb if lat else 128 * (qb - 4), first=qb in (0, 4),
                                 last=qb in (3, 5), nq=512 if lat else 256, causal=False, raw=not lat, dv=64,
                                 po=64 * (h % 2), qb=qb))
        attn(f"na{l}", jobs, layer=l)
        merge(2)
        units(["mres", "mres"], at="ACC", ctx=ctx, layer=l, split=True, final=True)
    norm("X", "res", "final_g")
    add("store", {})
    return out


def build(nc, x, ctx_in, w8, wb, wf_in, wg_in, params, rows, lru_w, sgu_w, sgu_b, rope, rot, nbias, out):
    stages = plan_stages()
    cx = ExitStack()

    def sb(name, shape):
        return cx.enter_context(nc.sbuf_tensor(name, shape, F32))

    sems = {}

    def sem(name):
        if name not in sems:
            sems[name] = cx.enter_context(nc.semaphore(name))
        return sems[name]

    arena_base = -(-nc.sbuf_base // 32) * 32
    ARENA = sb("ARENA", [P, AREN])
    h_base = arena_base + 4 * AREN
    H = sb("H", [P, KT, TA])
    w_base = h_base + 4 * KT * TA
    W = sb("W", [P, 2, KT * SLAB])
    X = sb("X", [P, KT, T])
    XC = sb("XC", [P, KT, TC])
    PC = sb("PC", [P, NPARAM])
    PR = sb("PR", [P, NROW])
    RST = sb("RST", [P, TA])
    IDENT = sb("IDENT", [P, P])
    ONES = sb("ONES", [P, P])
    SEL = sb("SEL", [8, 8, P])
    MCAUS = sb("MCAUS", [P, P])
    MFWD = sb("MFWD", [P, P])
    MBWD = sb("MBWD", [P, P])
    EPSC = sb("EPSC", [P, 1])
    SC = sb("SC", [P, KT, 2])
    MODT = sb("MODT", [P, LAYERS, 24, 2])
    MG = sb("MG", [P, KT, 2])
    LAM = sb("LAM", [P, LAYERS, 8])
    DAG = sb("DAG", [P, LAYERS])
    SMALL = sb("SMALL", [P, 64])
    NSP = sb("NSP", [P, 8, 4])
    ROT = sb("ROT", [P, P])
    WFS = sb("WFS", [P, KT, 8])
    WGS = sb("WGS", [P, KT, 16])
    PS = cx.enter_context(nc.psum_tensor("PS", [P, 8, 512], F32))

    def bank(b, n=512, p0=0, p1=P):
        if n <= 512:
            return PS[p0:p1, b, 0:n]
        return PS[p0:p1, b:b + 2, :].rearrange("p a b -> p (a b)")[:, 0:n]

    class Carve:
        def __init__(self, at=0):
            self.at = at

        def __call__(self, *shape, parts=P):
            n = int(np.prod(shape))
            v = ARENA[0:parts, self.at:self.at + n]
            self.at += n
            assert self.at <= AREN, self.at
            if len(shape) == 2:
                v = v.rearrange("p (a b) -> p a b", a=shape[0])
            if len(shape) == 3:
                v = v.rearrange("p (a b c) -> p a b c", a=shape[0], b=shape[1])
            return v

    cv = Carve()
    XA, GA, CP, YB, RG, IG, AG, TH, HS = (cv(4, T) for _ in range(9))
    PV = RG
    y_at = cv.at
    Y = cv(8, T)
    LRUW = cv(8, P)
    even_end = cv.at
    cv = Carve(KT * T)
    HID = cv(KT, T)
    CB, SG = cv(4, T), cv(2, T)
    split_at = cv.at

    cv = Carve()
    UU, FQ, FK, FV, GT, GSQ = (cv(4, T) for _ in range(6))
    WT = cv(8, P)
    FROW = cv(4, T)
    FCQ = cv(4, 8)
    odd_scratch = cv.at
    FT1, FAT, FE, FL = cv(2, T), cv(4, T), cv(2, T), cv(2, T)
    GMS = cv(4, 8)
    oy_at = cv.at
    OY = cv(8, T)
    BS = cv(P)
    odd_end = cv.at
    def over(name, base, at, shape):
        return nc.alloc_sbuf_tensor_at(name, shape, F32R, offset=base + 4 * at)

    HL = over("HL", h_base, 0, [P, KT, TA])
    HIDH = over("HIDH", arena_base, 0, [P, KT * T])
    HIDL = over("HIDL", arena_base, KT * T, [P, KT * T])
    WH = over("WH", arena_base, split_at, [P, 2, KT * SLAB])
    WL = over("WL", arena_base, split_at + 2 * KT * SLAB, [P, 2, KT * SLAB])
    HH = over("HH", arena_base, split_at + 4 * KT * SLAB, [P, KT, T])
    assert split_at + 4 * KT * SLAB + KT * T <= AREN
    HHE = over("HHE", arena_base, even_end, [P, KT, T])
    WHE = over("WHE", arena_base, even_end + KT * T, [P, 2, KT * SLAB])
    YL = over("YL", arena_base, y_at, [P, KT, T])
    assert even_end + KT * T + 2 * KT * SLAB <= AREN
    HHO = over("HHO", arena_base, odd_scratch, [P, KT, T])
    WHO = over("WHO", arena_base, odd_end, [P, 2, KT * SLAB])
    OYL = over("OYL", arena_base, oy_at, [P, KT, T])
    assert odd_end + 2 * KT * SLAB <= AREN
    hyb_at = 8 * TA + 12 * TA + 6 * BW + 4 * TA
    WLX = over("WLX", w_base, 0, [P, 2, KT * SLAB])
    WHX = over("WHX", arena_base, hyb_at, [P, 2, KT * SLAB])
    HHX = over("HHX", arena_base, hyb_at + 2 * KT * SLAB, [P, KT, TA])
    assert hyb_at + 2 * KT * SLAB + KT * TA <= AREN
    YTL = over("YTL", arena_base, hyb_at - 4 * TA, [P, 4, TA])
    YTH = over("YTH", arena_base, 8 * TA, [P, 4, TA])
    WLM = over("WLM", arena_base, 12 * TA, [P, 2, KT * SLAB])
    ACCL = over("ACCL", arena_base, 0, [P, KT, TA])
    ACCH = over("ACCH", arena_base, 12 * TA, [P, KT, TA])
    cv = Carve()
    ACC = cv(8, TA)
    Q, K, Z = (cv(4, TA) for _ in range(3))
    V = cv(6, BW)
    YT = cv(4, TA)
    scratch = cv.at
    assert scratch == hyb_at
    AT, E_, L_ = cv(6, T), cv(2, TA), cv(2, TA)
    NB = cv(2, 14 * 64)
    cv = Carve(scratch + 6 * T)
    DL, DE = cv(2, TA), cv(4, TA)
    cv = Carve(scratch - 4 * TA)
    RC, RS_, RT1, RT2 = cv(T), cv(T), cv(T), cv(T)
    cv = Carve(scratch - 4 * TA - 6 * BW)
    GB, TM = cv(3, T), cv(T)
    cv = Carve(scratch - 4 * TA)
    CV = cv(2, TA)
    cv = Carve(scratch)
    B0, B1, M0, M1 = (cv(TA) for _ in range(4))
    shared = cv.at
    LI, LF, A0, A1, ZERO, LX = (cv(TA) for _ in range(6))
    AC = cv(12, 8)
    cv = Carve(shared)
    DM, ZM = cv(2, T), cv(2, T)
    MK, EM, RCP, TMP = cv(4, P), cv(2, T), cv(T), cv(T)
    assert cv.at <= shared + 6 * TA, cv.at
    MSQ = ARENA[:, shared:shared + 2 * TA].rearrange("p (a b) -> p a b", a=2)

    def pc(name, i=0):
        c = PCOL[name] + i
        return PC[:, c:c + 1]

    loaded = sem("loaded")
    loaded_pool = sem("loaded_pool")
    x_loaded = [sem(f"x_loaded{i}") for i in range(2)]
    consts = sem("consts")
    w_ready = [sem(f"w_ready{s}") for s in range(2)]
    slab_used = [sem(f"slab_used{s}") for s in range(2)]
    full = [sem(f"full{b}") for b in range(8)]
    freed = [sem(f"freed{b}") for b in range(8)]
    h_ready, x_normed = sem("h_ready"), sem("x_normed")
    sq_ready, rstd_ready = sem("sq_ready"), sem("rstd_ready")
    wh_ready = [sem(f"wh_ready{s}") for s in range(2)]
    wl_ready = [sem(f"wl_ready{s}") for s in range(2)]
    hh_ready, hl_ready = sem("hh_ready"), sem("hl_ready")
    h_back = sem("h_back")
    hidden, hid_hi, hid_lo = sem("hidden"), sem("hid_hi"), sem("hid_lo")

    def wait_loaded(eng):
        eng.wait_ge(loaded, 2 * 16)
        for half in x_loaded:
            eng.wait_ge(half, 16)
        eng.wait_ge(loaded_pool, 4 * 16)

    def wait(eng, s, v):
        if not (isinstance(v, int) and v <= 0):
            eng.wait_ge(s, v)

    def repeat(eng, n, first, body):
        if first or n == 1:
            body(0)
        if n > 1:
            with eng.Fori(int(first), n) as i:
                body(i)

    def wait_unit(eng, st, u, b, ctx):
        if b >= 4 or (not ctx and b % 2 == 1):
            eng.wait_ge(slab_used[b - 4 if b >= 4 else b // 2], st["it"] + u + 1)
        else:
            eng.wait_ge(full[b], st["full", b] + u + 1)

    def wait_free(eng, st, b, j):
        wait(eng, freed[b], j + st["free", b])

    def split_bufs(st):
        if st.kind in ("up", "down"):
            return HH, HL, WH, WL, T
        if st.kind == "merge":
            return HHX, HL, WHX, WLM, TA
        if st.era == "even":
            return HHE, YL if st.at == "Y" else HL, WHE, WLX, T
        if st.era == "odd":
            return HHO, OYL if st.at == "Y" else HL, WHO, WLX, T
        if st.at == "ACC":
            return ACCH, ACCL, WHX, WLX, TA if st.ctx else T
        return HHX, HL, WHX, WLX, TA

    def hl_all(st):
        return st["hl"] + (KT if st.first else 0)

    def go_split(st, u):
        return st.split and not (st.final and u == len(st.evs) - 1)

    def mod_bank(i):
        return (5, 1)[i % 2], i // 2

    def pe_mod(pe, st, part):
        i, s, m = part // 4, part % 4 // 2, part % 2
        b, use = mod_bank(i)
        if part == 0:
            pe.wait_ge(sem("sc_ready"), 1)
        if m == 0:
            pe.wait_ge(w_ready[s], 16 * (st["it"] + i + 1))
            if s == 0:
                wait_free(pe, st, b, use)
        c = 2 * (2 * s + m)
        for k in range(KT):
            mm = pe.matmul(PS[:, b, c:c + 2], W[:, s, k * SLAB + m * P:k * SLAB + m * P + P],
                           SC[:, k, :], start=k == 0, stop=k == KT - 1)
        if m == 1:
            mm.then_inc(slab_used[s], 1)

    def pe_norm(pe, st):
        for k in range(KT):
            pe.wait_ge(sq_ready, st["sq"] + k + 1)
            if k == 0:
                wait_free(pe, st, 6, 0)
                if st.ctx:
                    wait_free(pe, st, 7, 0)
            mm = pe.matmul(PS[:, 6, :], ONES[:, :], H[:, k, 0:T], start=k == 0, stop=k == KT - 1)
            if k == KT - 1:
                mm.then_inc(full[6], 1)
            if st.ctx:
                mm = pe.matmul(PS[:, 7, 0:TC], ONES[:, :], H[:, k, T:TA], start=k == 0, stop=k == KT - 1)
                if k == KT - 1:
                    mm.then_inc(full[7], 1)

    def pe_units(pe, st):
        if st.split:
            hi, lo = split_bufs(st)[:2]
            ready = (hl_ready, hl_all(st) - KT + 1)
            if st.at == "ACC":
                ready = (sem("acc_lo"), KT * st.layer + 1)
            elif st.at == "Y" and not st.first:
                ready = (sem("y8_lo"), 1)
            for u in range(len(st.evs)):
                pe_split_unit_x(pe, st, u, hi, lo, ready)

    def pe_tok(pe, st):
        hi, lo, wh, wl, _ = split_bufs(st)
        for u in range(len(st.evs)):
            for s in range(2):
                pe.wait_ge(wl_ready[s], st["ws"] + u + 1)
                for t in range(st.nt):
                    if s == 0:
                        wait_free(pe, st, t, u)
                    tt = slice(t * P, (t + 1) * P)
                    for k in range(4):
                        c = slice(k * BW, (k + 1) * BW)
                        pe.matmul(PS[:, t, :], hi[:, 4 * s + k, tt], wh[:, s, c], start=s == 0 and k == 0,
                                  stop=False)
                        pe.matmul(PS[:, t, :], hi[:, 4 * s + k, tt], wl[:, s, c], start=False, stop=False)
                        mm = pe.matmul(PS[:, t, :], lo[:, 4 * s + k, tt], wh[:, s, c], start=False,
                                       stop=s == 1 and k == 3)
                    if t == st.nt - 1:
                        mm.then_inc(slab_used[s], 1)
                    elif s == 1:
                        mm.then_inc(full[t], 1)

    def pe_lru(pe, st):
        pe.wait_ge(sem("lru_w"), 16 * 8)
        for m in range(4):
            wait_free(pe, st, m, 0)
        for m in range(4):
            for g in range(2):
                b = (2 * m + g) % 4
                wait_free(pe, st, b, m // 2)
                pe.matmul(PS[:, b, :], LRUW[:, 4 * g + m, :], XA[:, m, :],
                          start=True, stop=True).then_inc(full[b], 1)

    def pe_split_unit(pe, st, u, hi, lo, ready, kb=KT):
        for s in range(2):
            pe.wait_ge(wl_ready[s], u + (st["ws"] + 1))
            for m in range(2):
                b = 2 * s + m
                wait_free(pe, st, b, u)
                for k in range(kb):
                    if s == 0 and m == 0:
                        pe.wait_ge(ready[0], ready[1] + k)
                    c = slice(k * SLAB + m * P, k * SLAB + m * P + P)
                    pe.matmul(PS[:, b, :], WH[:, s, c], hi(k), start=k == 0, stop=False)
                    pe.matmul(PS[:, b, :], WH[:, s, c], lo(k), start=False, stop=False)
                    mm = pe.matmul(PS[:, b, :], WL[:, s, c], hi(k), start=False, stop=k == kb - 1)
                mm.then_inc(slab_used[s] if m == 1 else full[b], 1)

    def pe_split_unit_x(pe, st, u, hi, lo, ready, kb=KT, slots=(0, 1)):
        _, _, wh, wl, _ = split_bufs(st)
        for s in slots:
            pe.wait_ge(wl_ready[s], u + (st["ws"] + 1))
            for t0, t1 in ((0, T), (T, TA))[:1 + st.ctx]:
                for m in range(2):
                    b = 2 * s + m if t0 == 0 else 4 + s
                    if t0 == 0 or m == 0:
                        wait_free(pe, st, b, u)
                    dst = PS[:, b, :] if t0 == 0 else PS[:, b, m * TC:(m + 1) * TC]
                    for k in range(kb):
                        if s == slots[0] and m == 0 and t0 == 0:
                            pe.wait_ge(ready[0], ready[1] + k)
                        c = slice(k * SLAB + m * P, k * SLAB + m * P + P)
                        pe.matmul(dst, wh[:, s, c], hi[:, k, t0:t1], start=k == 0, stop=False)
                        pe.matmul(dst, wh[:, s, c], lo[:, k, t0:t1], start=False, stop=False)
                        mm = pe.matmul(dst, wl[:, s, c], hi[:, k, t0:t1], start=False, stop=k == kb - 1)
                    last = m == 1 and (t0 == T or not st.ctx)
                    if t0 == 0:
                        mm.then_inc(slab_used[s] if last else full[b], 1)
                    elif last:
                        mm.then_inc(slab_used[s], 1)

    def pe_up(pe, st):
        with pe.Fori(0, st.n) as i:
            pe_split_unit(pe, st, i, lambda k: HH[:, k, :], lambda k: HL[:, k, 0:T],
                          (hl_ready, hl_all(st) - KT + 1))

    def pe_down(pe, st):
        for u in range(2):
            pe_split_unit(pe, st, u, lambda k: HIDH[:, k * T:(k + 1) * T],
                          lambda k: HIDL[:, k * T:(k + 1) * T], (hid_lo, st["hid"] - st.n + 1), kb=st.n)

    def pe_foxgate(pe, st):
        pe.wait_ge(h_ready, st["hr"])
        wait_free(pe, st, 6, 0)
        for k in range(KT):
            mm = pe.matmul(PS[0:8, 6, :], WFS[:, k, :], H[:, k, 0:T], start=k == 0, stop=k == KT - 1)
        mm.then_inc(full[6], 1)
        pe.wait_ge(sem("fox_cum"), 1)
        wait_free(pe, st, 7, 0)
        for t in range(4):
            mm = pe.transpose(PS[:, 7, 8 * t:8 * t + 8], FROW[0:8, 3, t * P:(t + 1) * P], IDENT[0:8, 0:8])
        mm.then_inc(full[7], 1)

    def pe_sgu(pe, st):
        pe.wait_ge(sem("gv_ready"), 4)
        pe.wait_ge(sem("sgu_loaded"), 32)
        pe.wait_ge(sem("wt_masked"), 1)
        for t in range(4):
            wait_free(pe, st, t, 0)
            for hh in range(2):
                pe.matmul(PS[64 * hh:64 * hh + 64, t, :], SEL[:, 2 * t + hh, 0:64],
                          BS[0:8, :].unsqueeze(1).broadcast_to([8, 4, P]), start=True, stop=False,
                          skip_group_check=True)
            for hh in range(2):
                for c in range(4):
                    mm = pe.matmul(PS[64 * hh:64 * hh + 64, t, c * P:(c + 1) * P],
                                   GT[:, c, (2 * t + hh) * 64:(2 * t + hh) * 64 + 64],
                                   WT[:, 2 * t + hh, :], start=False, stop=c == 3 and hh == 1,
                                   skip_group_check=True)
            mm.then_inc(full[t], 1)

    def eslot(j, slot):
        return slot + 2 * (j["n"] % 2) if len(j["comps"]) == 2 else slot

    def attn_bufs(st):
        if st.name == "fox":
            return FQ, FK, FV, FAT, FE, FL
        if st.name.startswith("da"):
            return Q, K, V, AT, DE, DL
        return Q, K, V, AT, E_, L_

    def mod_parts(n):
        return min(4 * MOD, (4 * MOD * (n + 1) + 30) // 31)

    def pe_attn(pe, st):
        q_, k_, v_, at_, e_, l_ = attn_bufs(st)
        jobs = st.jobs

        def scores(j):
            if st.name == "fox" and j["qb"] == 0:
                wait_free(pe, st, 7, j["head"])
                pe.matmul(PS[:, 7, :], SEL[:, j["head"], :], FROW[0:8, 3, :], start=True,
                          stop=True).then_inc(full[7], 1)
            for c, use in zip(j["comps"], j["use"]):
                b, po, nk, k0 = 2 * c["slot"], c["po"], j["nk"], j["k0"]
                wait_free(pe, st, b, use)
                for o in range(0, nk, 512):
                    n = min(512, nk - o)
                    mm = pe.matmul(PS[:, b + o // 512, 0:n], q_[po:po + 64, j["tile"], j["q0"]:j["q0"] + P],
                                   k_[po:po + 64, j["tile"], k0 + o:k0 + o + n], start=True, stop=True)
                mm.then_inc(full[b], 1)

        def transposes(j):
            pe.wait_ge(sem(f"probs_{st.name}"), j["n"] + 1)
            wait_free(pe, st, 4, j["n"])
            slot = eslot(j, j["comps"][0]["slot"])
            for kb in range(j["nk"] // P):
                mm = pe.transpose(bank(4, j["nk"])[:, kb * P:(kb + 1) * P],
                                  e_[:, slot, kb * P:(kb + 1) * P], IDENT[:, :])
            mm.then_inc(full[4], 1)

        def values(j):
            pe.wait_ge(freed[4], st["free", 4] + j["n"] + 1)
            wait_free(pe, st, 6, j["out"])
            nkb, dv, po = j["nk"] // P, j["dv"], j["po"]
            for kb in range(nkb):
                c0 = kb * P if j["causal"] else 0
                mm = pe.matmul(PS[po:po + dv, 6, c0:j["nq"]],
                               v_[:, j["k0"] // P + kb, j["head"] * dv:(j["head"] + 1) * dv],
                               at_[:, kb, c0:j["nq"]], start=kb == 0, stop=kb == nkb - 1,
                               skip_group_check=j["causal"])
            mm.then_inc(full[6], 1)
            if st.name.startswith("da"):
                pe.wait_ge(sem(f"o_sq_{st.name}"), j["out"] + 1)
                wait_free(pe, st, 7, j["out"])
                pe.matmul(PS[:, 7, 0:j["nq"]], ONES[:, :], l_[:, 0, 0:j["nq"]], start=True,
                          stop=True).then_inc(full[7], 1)

        if st.name == "fox":
            pe.wait_ge(freed[7], st["free", 7])
        elif st.name.startswith("da"):
            pe.wait_ge(sem(f"rope_done{st.layer}"), 8)
        for b in range(6):
            wait_free(pe, st, b, 0)
        ahead = 3 - len(jobs[0]["comps"])
        for j in jobs[:ahead]:
            scores(j)
        mod = 0
        for j in jobs:
            if j["n"] + ahead < len(jobs):
                scores(jobs[j["n"] + ahead])
            due = mod_parts(j["n"]) if st.name == "fox" else 0
            if mod < due:
                pe_mod(pe, st, mod)
                mod += 1
            transposes(j)
            if j["last"]:
                values(j)
            if mod < due:
                pe_mod(pe, st, mod)
                mod += 1
        assert mod == (4 * MOD if st.name == "fox" else 0)

    def pe_rope(pe, st):
        pe.wait_ge(sem(f"rope_loaded{st.layer}"), 32)
        for n in range(8):
            b, buf = 6 + n % 2, (Q, K)[n // 4]
            wait_free(pe, st, b, n // 2)
            pe.matmul(PS[:, b, :], ROT[:, :], buf[:, n % 4, 0:T], start=True, stop=True).then_inc(full[b], 1)

    def pe_merge(pe, st):
        with pe.Fori(0, 4) as i:
            pe_split_unit_x(pe, st, i, HHX, HL, (hl_ready, hl_all(st) - KT + 1), KT, (0,))
            pe_split_unit_x(pe, st, i, YTH, YTL, (sem("y_lo"), 4 * merge_no(st) + 1), 4, (1,))

    def merge_no(st):
        return 3 * st.layer + st.n

    def wait_y(pe, st):
        if st.n == 1:
            pe.wait_ge(sem(f"ml_y{st.layer}"), 4)
        elif st.n == 0:
            pe.wait_ge(sem(f"da_y{st.layer}"), 8 if st.ctx else 4)
        else:
            pe.wait_ge(freed[6], st["free", 6])

    def pe_mlgate(pe, st):
        pe.wait_ge(sem(f"wg_loaded{st.layer}"), 16)
        pe.wait_ge(h_back, st["back"])
        for g in range(2):
            t0, n = ((0, T), (T, TC))[g]
            for f in range(2):
                wait_free(pe, st, 6 + f, g)
                for k in range(KT):
                    mm = pe.matmul(PS[0:8, 6 + f, 0:n], WGS[:, k, 8 * f:8 * f + 8], H[:, k, t0:t0 + n],
                                   start=k == 0, stop=k == KT - 1)
                mm.then_inc(full[6 + f], 1)
        pe.wait_ge(sem(f"ml_rows{st.layer}"), 1)
        wait_free(pe, st, 0, 0)
        for d in range(2):
            for sbk in range(6):
                mm = pe.transpose(PS[:, 0, (6 * d + sbk) * 8:(6 * d + sbk) * 8 + 8],
                                  (A0, A1)[d][0:8, sbk * P:(sbk + 1) * P], IDENT[0:8, 0:8])
        mm.then_inc(full[0], 1)

    def pe_mlstm(pe, st):
        pe.wait_ge(sem(f"bqk{st.layer}"), 8)
        for b in range(8):
            wait_free(pe, st, b, 0)
        blocks = [(ps, i) for ps in st.passes for i in range(len(ps["blocks"]))]

        def qk(n):
            ps, i = blocks[n]
            h, d, nq, q0 = ps["h"], ps["d"], ps["nq"], T * ps["g"]
            if i == 0:
                if n:
                    pe.wait_ge(sem(f"decay{st.layer}"), n)
                wait_free(pe, st, 5, ps["p"])
                pe.matmul(PS[:, 4, 0:nq], SEL[:, 4 * d + h, :], (M0, M1)[d][0:8, q0:q0 + nq], start=True,
                          stop=True)
                pe.matmul(PS[:, 5, 0:nq], SEL[:, 4 * d + h, :], (B0, B1)[d][0:8, q0:q0 + nq], start=True,
                          stop=True).then_inc(full[5], 1)
            s_, t0, t1, _ = ps["blocks"][i]
            wait_free(pe, st, n % 2, n // 2)
            pe.matmul(PS[:, n % 2, t0:t1], K[:, h, s_ * P:(s_ + 1) * P], Q[:, h, q0 + t0:q0 + t1],
                      start=True, stop=True).then_inc(full[n % 2], 1)

        qk(0)
        for n, (ps, i) in enumerate(blocks):
            if n + 1 < len(blocks):
                qk(n + 1)
            s_, t0, t1, _ = ps["blocks"][i]
            nb, p, h = len(ps["blocks"]), ps["p"], ps["h"]
            num = 2 + 4 * (p % 2)
            pe.wait_ge(freed[n % 2], st["free", n % 2] + n // 2 + 1)
            if i == 0:
                wait_free(pe, st, num, p // 2)
            pe.matmul(PS[:, num, t0:t1], V[:, s_, h * P:(h + 1) * P], ZM[:, n % 2, t0:t1],
                      start=i == 0, stop=i == nb - 1, skip_group_check=True)
            mm = pe.matmul(PS[:, num + 1, t0:t1], ONES[:, :], ZM[:, n % 2, t0:t1],
                           start=i == 0, stop=i == nb - 1, skip_group_check=True)
            if i == nb - 1:
                mm.then_inc(full[num], 1)

    def pe_mlout(pe, st):
        for h in range(4):
            pe.wait_ge(sem(f"ml_sq{st.layer}"), h + 1)
            wait_free(pe, st, 6, h)
            pe.matmul(PS[:, 6, :], ONES[:, :], MSQ[:, h % 2, 0:T], start=True, stop=True).then_inc(full[6], 1)
            if st.ctx:
                wait_free(pe, st, 7, h)
                pe.matmul(PS[:, 7, 0:TC], ONES[:, :], MSQ[:, h % 2, T:TA], start=True,
                          stop=True).then_inc(full[7], 1)

    def act_norm(act, own, st):
        for m in range(KT):
            if st.src == "load":
                if m == 0:
                    act.wait_ge(consts, 9)
                if m % 4 == 0:
                    act.wait_ge(x_loaded[m // 4], 16)
            elif st.src == "xn":
                act.wait_ge(x_normed, st["xn"] - KT + m + 1)
            else:
                act.wait_ge(freed[m % 4], st.prev["free", m % 4] + m // 4 + 1)
                if st.ctx and st.prev.ctx:
                    c = 4 + m % 4 // 2
                    act.wait_ge(freed[c], st.prev["free", c] + m // 4 + 1)
            ins = act.activation(H[:, m, 0:T], X[:, m, :], ACT.Square)
            if st.ctx:
                ins = act.activation(H[:, m, T:TA], XC[:, m, :], ACT.Square)
            ins.then_inc(sq_ready, 1)
        for b, t0, t1 in ((6, 0, T), (7, T, TA))[:1 + st.ctx]:
            act.wait_ge(full[b], st["full", b] + 1)
            act.activation(RST[:, t0:t1], bank(b, t1 - t0), ACT.Ln, bias=EPSC[:, 0:1],
                           scale=1.0 / D).then_inc(freed[b], 1)
            act.wait_ge(freed[b], st["free", b] + 1)
            act.activation(RST[:, t0:t1], RST[:, t0:t1], ACT.Exp, scale=-0.5).then_inc(rstd_ready, 1)

    def act_prep(act, own, st):
        act.wait_ge(consts, 9)
        wait_loaded(act)
        c0 = PCOL["c"]
        act.activation(SC[:, :, :].rearrange("p a b -> p (a b)"), PC[:, c0:c0 + 16],
                       ACT.Silu).then_inc(sem("sc_ready"), 1)
        act.wait_ge(sem("lam_sum"), 1)
        act.activation(SMALL[:, 60:64], SMALL[:, 56:60], ACT.Exp).then_inc(sem("lam_exp"), 1)
        lam = PC[:, PCOL["lru_lambda"]:PCOL["lru_lambda"] + 4]
        own.link(act.activation(NSP[:, 0, :], lam, ACT.Abs))
        act.activation(NSP[:, 1, :], NSP[:, 0, :], ACT.Exp, scale=-1.0).then_inc(sem("lru_e"), 1)
        act.wait_ge(sem("lru_1e"), 1)
        act.activation(NSP[:, 3, :], NSP[:, 2, :], ACT.Ln).then_inc(sem("lru_ln"), 1)

    def act_units(act, own, st):
        if st.first:
            act_split_first(act, st)
        if st.at == "Y" and not st.first:
            act.wait_ge(sem("y_ready"), 4)
            for b in range(4):
                act.wait_ge(freed[b], st["free", b])
            for k in range(KT):
                act.activation(HHE[:, k, :], Y[:, k, :], ACT.Copy).then_inc(sem("y8_hi"), 1)
        if st.at == "ACC":
            for b in (2, 3, 5) if st.ctx else (2, 3):
                wait_free(act, st, b, 0)
            n = TA if st.ctx else T
            for k in range(KT):
                act.activation(ACCH[:, k, 0:n], ACC[:, k, 0:n], ACT.Copy).then_inc(sem("acc_hi"), 1)
        for u, ev in enumerate(st.evs):
            if ev == "xa":
                for m in range(4):
                    wait_unit(act, st, u, m, False)
                    act.activation(XA[:, m, :], PS[:, m, :], ACT.Identity, bias=pc("lru_conv", 5 * m + 4),
                                   scale=pc("lru_conv", 5 * m + 3)).then_inc(sem("xa_scaled"), 1)
                    if go_split(st, u) and m % 2:
                        act_split(act, st, u + 1, m // 2)
            elif ev in ("ga", "u"):
                dst = GA if ev == "ga" else UU
                for m in range(4):
                    wait_unit(act, st, u, m, False)
                    act.activation(dst[:, m, :], PS[:, m, :], ACT.Gelu_apprx_tanh).then_inc(freed[m], 1)
                    if go_split(st, u) and m % 2:
                        act_split(act, st, u + 1, m // 2)
            elif ev in ("az", "cz", "bo"):
                fn = ACT.Sigmoid if ev == "bo" else ACT.Silu
                for s in range(2):
                    for m in (2 * s, 2 * s + 1):
                        wait_unit(act, st, u, m, st.ctx)
                        act.activation(Z[:, m, 0:T], PS[:, m, :], fn).then_inc(freed[m], 1)
                    if st.ctx:
                        wait_unit(act, st, u, 4 + s, True)
                        act.activation(Z[:, 2 * s:2 * s + 2, T:TA],
                                       PS[:, 4 + s, :].rearrange("p (a b) -> p a b", a=2),
                                       fn).then_inc(freed[4 + s], 1)
                    if go_split(st, u):
                        act_split(act, st, u + 1, s)
            elif ev == "bz":
                for s in range(2):
                    for b in (2 * s, 2 * s + 1, 4 + s)[:2 + st.ctx]:
                        wait_unit(act, st, u, b, st.ctx)
                        act.activation(PS[:, b, :], PS[:, b, :], ACT.Silu).then_inc(sem(f"bz{st.layer}"), 1)
                    if go_split(st, u):
                        act_split(act, st, u + 1, s)
            elif ev in ("bq", "bk"):
                dst, c0 = (Q, 0) if ev == "bq" else (K, 4)
                n0 = conv_no(st, u)
                for b in (2, 3, 5):
                    act.wait_ge(freed[b], st["free", b])
                for m in range(4):
                    w = 4 * (8 * st.layer + c0 + m)
                    wait_unit(act, st, u, m, st.ctx)
                    ins = act.activation(CV[:, m % 2, 0:T], PS[:, m, :], ACT.Identity,
                                         bias=pc("ml_conv", w + 3), scale=pc("ml_conv", w + 1))
                    if st.ctx:
                        c = 4 + m // 2
                        wait_unit(act, st, u, c, True)
                        ins = act.activation(CV[:, m % 2, T:TA], PS[:, c, m % 2 * TC:(m % 2 + 1) * TC],
                                             ACT.Identity, bias=pc("ml_conv", w + 3),
                                             scale=pc("ml_conv", w + 1))
                    ins.then_inc(sem(f"cv_scaled{st.layer}"), 1)
                    act.wait_ge(freed[m], st["free", m] + u + 1)
                    if st.ctx and m % 2:
                        act.wait_ge(freed[4 + m // 2], st["free", 4 + m // 2] + u + 1)
                    elif st.ctx:
                        act.wait_ge(sem(f"cv_done{st.layer}"), (n0 + m) // 2 + 1)
                    n = TA if st.ctx else T
                    act.activation(dst[:, m, 0:n], CV[:, m % 2, 0:n],
                                   ACT.Silu).then_inc(sem(f"bqk{st.layer}"), 1)
                    if go_split(st, u) and m % 2:
                        act_split(act, st, u + 1, m // 2)
            elif go_split(st, u):
                for s in range(2):
                    act_split(act, st, u + 1, s)

    def conv_no(st, u):
        if st.layer == 0:
            return 4 * u
        return 0 if st.evs[u] == "bk" else 4

    def act_tok(act, own, st):
        for u, ev in enumerate(st.evs):
            if go_split(st, u):
                act_split(act, st, u + 1, 0)
            if ev == "g":
                for t in range(4):
                    wait_tok(act, st, u, t)
                    act.activation(GT[:, t, :], PS[:, t, :], ACT.Gelu_apprx_tanh).then_inc(freed[t], 1)
            if go_split(st, u):
                act_split(act, st, u + 1, 1)
        if st.evs[0] == "g":
            for t in range(4):
                act.wait_ge(sem("sgu_ms"), t + 1)
                own.link(act.activation(GMS[:, t, :], GMS[:, t, :], ACT.Ln, bias=EPSC[:, 0:1], scale=1.0 / 64))
                act.activation(GMS[:, t, :], GMS[:, t, :], ACT.Exp, scale=-0.5).then_inc(sem("sgu_rs"), 1)

    def wait_tok(eng, st, u, t):
        if t == st.nt - 1:
            eng.wait_ge(slab_used[1], st["it"] + u + 1)
        else:
            eng.wait_ge(full[t], st["full", t] + u + 1)

    def act_lru(act, own, st):
        for m in range(4):
            for g in range(2):
                b = (2 * m + g) % 4
                act.wait_ge(full[b], st["full", b] + m // 2 + 1)
                act.activation((RG, IG)[g][:, m, :], PS[:, b, :], ACT.Sigmoid,
                               bias=pc(("lru_ba", "lru_bx")[g], m)).then_inc(freed[b], 1)
        act.wait_ge(sem("lru_sp"), 1)
        for m in range(4):
            act.wait_ge(freed[2 * m % 4], st["free", 2 * m % 4] + m // 2 + 1)
            act.activation(AG[:, m, :], RG[:, m, :], ACT.Exp, scale=NSP[:, 6, m:m + 1])
            act.activation(TH[:, m, :], RG[:, m, :], ACT.Tanh, scale=NSP[:, 7, m:m + 1]).then_inc(sem("lru_a"), 1)
        for m in range(4):
            act.wait_ge(sem("lru_t"), m + 1)
            act.activation(TH[:, m, :], TH[:, m, :], ACT.Sqrt).then_inc(sem("lru_s"), 1)

    def slab_size(st, s, last=False):
        return 4 * SLAB if st.kind == "merge" and s == 1 and not last else KT * SLAB

    def act_split(act, st, u, s, last=False):
        act.wait_ge(w_ready[s], (u + (st["it"] + 1)) * 16)
        wait(act, slab_used[s], u + st["it"])
        dst = split_bufs(st)[2]
        n = slab_size(st, s, last)
        act.activation(dst[:, s, 0:n], W[:, s, 0:n], ACT.Copy).then_inc(wh_ready[s], 1)

    def act_split_first(act, st):
        dst, _, _, _, n = split_bufs(st)
        if st.kind == "merge":
            wait_y(act, st)
        act_split(act, st, 0, 0)
        src = OY if st.at == "Y" else H
        if st.at == "Y":
            for b in (0, 1, 2, 3, 6):
                act.wait_ge(freed[b], st["free", b])
        for k in range(KT):
            if src is H:
                act.wait_ge(h_ready, st["hr"] - KT + k + 1)
            act.activation(dst[:, k, :], src[:, k, 0:n], ACT.Copy).then_inc(hh_ready, 1)
        if st.kind == "merge":
            n = TA if st.ctx else T
            for k in range(4):
                act.activation(YTH[:, k, 0:n], YT[:, k, 0:n], ACT.Copy).then_inc(sem("y_hi"), 1)
        act_split(act, st, 0, 1)

    def act_up(act, own, st):
        cb, sg = sem("cb_scaled"), sem("silu_done")
        base = PCOL[f"ffn_conv{st.layer}"] + 16 * st.step0
        if st.first:
            act_split_first(act, st)
        with act.Fori(0, st.n) as i:
            for m in range(4):
                if m % 2:
                    act_split(act, st, i + 1, m // 2)
                wait_unit(act, st, i, m, False)
                act.activation(CB[:, m, :], PS[:, m, :], ACT.Identity,
                               bias=PC[:, bass.ds(i * 16 + (base + 4 * m + 3), 1)],
                               scale=PC[:, bass.ds(i * 16 + (base + 4 * m + 2), 1)]).then_inc(cb, 1)
                if m == 1:
                    for g in range(2):
                        act.wait_ge(freed[g], i + (st["free", g] + 1))
                        act.activation(SG[:, g, :], CB[:, g, :], ACT.Silu).then_inc(sg, 1)
            for m in range(2):
                act.wait_ge(hidden, i * 2 + (st["hid"] + m + 1))
                act.activation(HIDH[:, bass.ds(i * (2 * T) + m * T, T)],
                               ARENA[:, bass.ds(i * (2 * T) + (KT + m) * T, T)], ACT.Copy).then_inc(hid_hi, 1)

    def act_down(act, own, st):
        for u in range(2 - st.final):
            for s in range(2):
                act_split(act, st, u + 1, s)

    def act_foxgate(act, own, st):
        z, lz = FROW[0:8, 0, :], FROW[0:8, 1, :]
        act.wait_ge(full[6], st["full", 6] + 1)
        act.activation(z, PS[0:8, 6, :], ACT.Identity, bias=PC[0:8, PCOL["fox_bf"]:PCOL["fox_bf"] + 1],
                       ).then_inc(freed[6], 1)
        act.wait_ge(freed[6], st["free", 6] + 1)
        own.link(act.activation(lz, z, ACT.Abs))
        own.link(act.activation(lz, lz, ACT.Exp, scale=-1.0))
        act.activation(lz, lz, ACT.Ln, bias=1.0).then_inc(sem("fox_l"), 1)

    SCALE = 0.125

    def col(base, j, ci):
        c = base + 4 * (j["n"] % 2) + ci
        return SMALL[:, c:c + 1]

    def act_attn(act, own, st):
        q_, k_, v_, at_, e_, l_ = attn_bufs(st)
        jobs, name = st.jobs, st.name
        da = name.startswith("da")

        def exps(j):
            for ci, (c, use) in enumerate(zip(j["comps"], j["use"])):
                s, nk = c["slot"], j["nk"]
                es = eslot(j, s)
                act.wait_ge(sem(f"max_{name}"), j["n"] * len(j["comps"]) + ci + 1)
                if j["raw"]:
                    act.activation(e_[:, es, 0:nk], bank(2 * s, nk), ACT.Exp, bias=col(0, j, ci), scale=SCALE,
                                   accum_out=col(16, j, ci)).then_inc(freed[2 * s], 1)
                else:
                    act.activation(e_[:, es, 0:nk], l_[:, s, 0:nk], ACT.Exp, bias=col(0, j, ci),
                                   accum_out=col(16, j, ci)).then_inc(sem(f"exp_{name}"), 1)

        def evac(j):
            act.wait_ge(full[4], st["full", 4] + j["n"] + 1)
            nkb = j["nk"] // P
            act.activation(at_[:, 0:nkb, j["qcol"]:j["qcol"] + P],
                           bank(4, j["nk"]).rearrange("p (a b) -> p a b", b=P), ACT.Copy).then_inc(freed[4], 1)

        def post(j):
            nq, o = j["nq"], j["out"]
            act.wait_ge(full[6], st["full", 6] + o + 1)
            act.activation(l_[:, 0, 0:nq], PS[:, 6, 0:nq], ACT.Square).then_inc(sem(f"o_sq_{name}"), 1)
            act.wait_ge(full[7], st["full", 7] + o + 1)
            act.activation(l_[:, 1, 0:nq], PS[:, 7, 0:nq], ACT.Ln, bias=EPSC[:, 0:1],
                           scale=1.0 / P).then_inc(freed[7], 1)
            act.wait_ge(freed[7], st["free", 7] + o + 1)
            act.activation(l_[:, 1, 0:nq], l_[:, 1, 0:nq], ACT.Exp, scale=-0.5).then_inc(sem(f"o_rs_{name}"), 1)

        ahead = 1 if da else 2
        for j in jobs[:ahead]:
            exps(j)
        for j in jobs:
            nxt = jobs[j["n"] + ahead] if j["n"] + ahead < len(jobs) else None
            if nxt and da:
                exps(nxt)
            evac(j)
            if nxt and not da:
                exps(nxt)
            if da and j["last"]:
                post(j)

    def act_merge(act, own, st):
        act_split_first(act, st)

        def step(i, last=False):
            for m, b in enumerate((0, 1, 4)[:2 + st.ctx]):
                if m == 1 + st.ctx:
                    act_split(act, st, i + 1, 0, last)
                wait_unit(act, st, i, b, st.ctx)
                act.wait_ge(freed[(2, 3, 5)[m]], i + st["free", (2, 3, 5)[m]])
                act.activation(GB[:, m, :], PS[:, b, :], ACT.Sigmoid).then_inc(freed[b], 1)
            act_split(act, st, i + 1, 1, last)

        with act.Fori(0, 3) as i:
            step(i)
        step(3, True)

    def act_mlgate(act, own, st):
        for g in range(2):
            t0, n = ((0, T), (T, TC))[g]
            act.wait_ge(full[7], st["full", 7] + g + 1)
            act.activation(LX[0:8, t0:t0 + n], PS[0:8, 7, 0:n], ACT.Identity,
                           bias=PC[0:8, PCOL["gate_bf"] + st.layer:PCOL["gate_bf"] + st.layer + 1],
                           ).then_inc(freed[7], 1)
        act.wait_ge(freed[7], st["free", 7] + 2)
        own.link(act.activation(LF[0:8, :], LX[0:8, :], ACT.Abs))
        own.link(act.activation(LF[0:8, :], LF[0:8, :], ACT.Exp, scale=-1.0))
        act.activation(LF[0:8, :], LF[0:8, :], ACT.Ln, bias=1.0).then_inc(sem(f"ml_l{st.layer}"), 1)

    def act_mlstm(act, own, st):
        dz, mk, dab = (sem(f"{n}{st.layer}") for n in ("decay", "ml_mask", "den_abs"))
        act.wait_ge(freed[0], st["free", 0])

        def den(ps):
            p, nq = ps["p"], ps["nq"]
            num = 2 + 4 * (p % 2)
            act.wait_ge(full[num], st["full", num] + p // 2 + 1)
            if p:
                prev = 2 + 4 * ((p - 1) % 2)
                act.wait_ge(freed[prev], st["free", prev] + (p - 1) // 2 + 1)
            act.activation(TMP[:, 0:nq], PS[:, num + 1, 0:nq], ACT.Abs).then_inc(dab, 1)

        for ps in st.passes:
            h, d, nq, n0, p = ps["h"], ps["d"], ps["nq"], ps["n0"], ps["p"]
            act.wait_ge(full[5], st["full", 5] + p + 1)
            if p > 1:
                num = 2 + 4 * (p % 2)
                act.wait_ge(freed[num], st["free", num] + p // 2)
            act.activation(EM[:, p % 2, 0:nq], PS[:, 5, 0:nq], ACT.Exp, scale=-1.0).then_inc(freed[5], 1)
            act.wait_ge(mk, p + 1)
            for i, (s_, t0, t1, j) in enumerate(ps["blocks"]):
                n = n0 + i
                ac = AC[:, 6 * d + s_, 4 * d + h:4 * d + h + 1]
                wait(act, freed[n % 2], st["free", n % 2] + n // 2)
                if j is None:
                    ins = act.activation(DM[:, n % 2, t0:t1], PS[:, 4, t0:t1], ACT.Exp, bias=ac, scale=-1.0)
                else:
                    ins = act.activation(DM[:, n % 2, j * P:(j + 1) * P], MK[:, j, :], ACT.Exp, bias=ac,
                                         scale=-1.0)
                    r0, r1 = (t0 + P, t1) if d == 0 else (t0, t1 - P)
                    if r1 > r0:
                        ins = act.activation(DM[:, n % 2, r0:r1], PS[:, 4, r0:r1], ACT.Exp, bias=ac, scale=-1.0)
                ins.then_inc(dz, 1)
                if i == 0 and p:
                    den(st.passes[p - 1])
        den(st.passes[-1])

    def act_mlout(act, own, st):
        act.wait_ge(freed[2], st["free", 2])
        act.wait_ge(freed[6], st["free", 6])
        n = TA if st.ctx else T
        for h in range(4):
            act.activation(MSQ[:, h % 2, 0:n], YT[:, h, 0:n], ACT.Square).then_inc(sem(f"ml_sq{st.layer}"), 1)
            wait(act, sem(f"ml_y{st.layer}"), h)
            for b, t0, t1 in ((6, 0, T), (7, T, TA))[:1 + st.ctx]:
                act.wait_ge(full[b], st["full", b] + h + 1)
                act.activation(RST[:, t0:t1], PS[:, b, 0:t1 - t0], ACT.Ln, bias=EPSC[:, 0:1],
                               scale=1.0 / P).then_inc(freed[b], 1)
                act.wait_ge(freed[b], st["free", b] + h + 1)
            act.activation(RST[:, 0:n], RST[:, 0:n], ACT.Exp, scale=-0.5).then_inc(sem(f"ml_rs{st.layer}"), 1)

    def dve_norm(dve, own, st):
        if st.mode == "mod":
            for b in (1, 5):
                dve.wait_ge(freed[b], st["free", b])
            g0 = PCOL["norm_g"] + 16 * st.layer
            own.link(dve.scalar_tensor_tensor(
                out=MG[:, :, :].rearrange("p a b -> p (a b)"),
                in0=MODT[:, st.layer, 8:16, :].rearrange("p a b -> p (a b)"), scalar=1.0,
                in1=PC[:, g0:g0 + 16], op0=ALU.add, op1=ALU.mult))
        if st.src == "load":
            wait_loaded(dve)
        dve.wait_ge(rstd_ready, st["rs"] + 1 + st.ctx)
        for k in range(KT):
            if st.mode == "mod":
                for src, t0, t1, c in ((X, 0, T, 0), (XC, T, TA, 1)):
                    own.mark(dve.scalar_tensor_tensor(out=H[:, k, t0:t1], in0=src[:, k, :],
                                                      scalar=MG[:, k, c:c + 1], in1=RST[:, t0:t1],
                                                      op0=ALU.mult, op1=ALU.mult))
                own.wait()
                for t0, t1, c in ((0, T, 0), (T, TA, 1)):
                    ins = dve.tensor_scalar(H[:, k, t0:t1], H[:, k, t0:t1],
                                            MODT[:, st.layer, k, c:c + 1], None, ALU.add)
                ins.then_inc(h_ready, 1)
            else:
                dst = H[:, k, 0:T] if st.mode == "H" else X[:, k, :]
                dve.scalar_tensor_tensor(out=dst, in0=X[:, k, :], scalar=pc(st.g, k), in1=RST[:, 0:T],
                                         op0=ALU.mult, op1=ALU.mult).then_inc(
                                             h_ready if st.mode == "H" else x_normed, 1)

    def dve_prep(dve, own, st):
        dve.wait_ge(h_ready, st["hr"])
        own.link(dve.tensor_tensor(RST[:, 0:256], PR[:, 0:256], PR[:, 256:512], ALU.mult))
        dve.tensor_reduce(SMALL[:, 56:60], RST[:, 0:256].rearrange("p (a b) -> p a b", b=64), AX,
                          ALU.add).then_inc(sem("lam_sum"), 1)
        dve.wait_ge(sem("lam_exp"), 1)
        for l in range(LAYERS):
            init = 0.8 - 0.6 * float(np.exp(-0.3 * l))
            own.link(dve.tensor_tensor(LAM[:, l, 0:1], SMALL[:, 61 + 2 * l:62 + 2 * l],
                                       SMALL[:, 60 + 2 * l:61 + 2 * l], ALU.subtract))
            own.mark(dve.tensor_scalar(LAM[:, l, 1:2], LAM[:, l, 0:1], -init, None, ALU.add))
            own.mark(dve.tensor_scalar(DAG[:, l:l + 1], pc("da_g", l), 1.0 - init, None, ALU.mult))
        lam = PC[:, PCOL["lru_lambda"]:PCOL["lru_lambda"] + 4]
        tiny = 1e-30
        dve.wait_ge(sem("lru_e"), 1)
        dve.tensor_scalar(NSP[:, 2, :], NSP[:, 1, :], 1.0, None, ALU.add).then_inc(sem("lru_1e"), 1)
        dve.wait_ge(sem("lru_1e"), 1)
        own.link(dve.tensor_scalar(NSP[:, 4, :], NSP[:, 2, :], -1.0, tiny, ALU.add, ALU.add))
        own.link(dve.reciprocal(NSP[:, 4, :], NSP[:, 4, :]))
        dve.wait_ge(sem("lru_ln"), 1)
        own.link(dve.tensor_scalar(NSP[:, 5, :], NSP[:, 3, :], tiny, None, ALU.add))
        own.link(dve.tensor_tensor(NSP[:, 5, :], NSP[:, 5, :], NSP[:, 4, :], ALU.mult))
        own.link(dve.tensor_tensor(NSP[:, 5, :], NSP[:, 5, :], NSP[:, 1, :], ALU.mult))
        own.link(dve.tensor_scalar(NSP[:, 4, :], lam, -1.0, 0.0, ALU.mult, ALU.max))
        own.link(dve.tensor_tensor(NSP[:, 5, :], NSP[:, 5, :], NSP[:, 4, :], ALU.add))
        own.mark(dve.tensor_scalar(NSP[:, 6, :], NSP[:, 5, :], -8.0, None, ALU.mult))
        dve.tensor_scalar(NSP[:, 7, :], NSP[:, 5, :], 8.0, None, ALU.mult).then_inc(sem("lru_sp"), 1)

    def dve_mod(dve, st, i):
        flat = MODT[:, :, :, :].rearrange("p a b c -> p (a b c)")
        c = PCOL["b_mod"] + 8 * i
        b, _ = mod_bank(i)
        dve.wait_ge(slab_used[1], st["it"] + i + 1)
        dve.tensor_tensor(flat[:, 8 * i:8 * i + 8], PS[:, b, 0:8], PC[:, c:c + 8], ALU.add).then_inc(freed[b], 1)

    def dve_units(dve, own, st):
        if st.first:
            dve_split_first(dve, st)
        if st.at == "Y" and not st.first:
            for k in range(KT):
                dve.wait_ge(sem("y8_hi"), k + 1)
                dve.tensor_tensor(YL[:, k, :], Y[:, k, :], HHE[:, k, :].bitcast(F32),
                                  ALU.subtract).then_inc(sem("y8_lo"), 1)
        if st.at == "ACC":
            n = TA if st.ctx else T
            for k in range(KT):
                dve.wait_ge(sem("acc_hi"), KT * st.layer + k + 1)
                dve.tensor_tensor(ACCL[:, k, 0:n], ACC[:, k, 0:n], ACCH[:, k, 0:n].bitcast(F32),
                                  ALU.subtract).then_inc(sem("acc_lo"), 1)
        for u, ev in enumerate(st.evs):
            if ev == "xa":
                for m in range(4):
                    dve.wait_ge(sem("xa_scaled"), m + 1)
                    for d in (1, 2, 3):
                        ins = dve.scalar_tensor_tensor(
                            out=XA[:, m, d:T], in0=PS[:, m, 0:T - d], scalar=pc("lru_conv", 5 * m + 3 - d),
                            in1=XA[:, m, d:T], op0=ALU.mult, op1=ALU.add)
                        if d < 3:
                            own.link(ins)
                    ins.then_inc(freed[m], 1)
                    if go_split(st, u) and m % 2:
                        dve_split(dve, st, u + 1, m // 2)
            elif ev in ("cp", "q", "k"):
                dst = {"cp": CP, "q": FQ, "k": FK}[ev]
                for m in range(4):
                    wait_unit(dve, st, u, m, False)
                    dve.tensor_copy(dst[:, m, :], PS[:, m, :]).then_inc(freed[m], 1)
                    if go_split(st, u) and m % 2:
                        dve_split(dve, st, u + 1, m // 2)
            elif ev == "vb":
                for m in range(4):
                    wait_unit(dve, st, u, m, False)
                    dve.wait_ge(freed[m], st["free", m] + u)
                    dve.tensor_tensor(PV[:, m, :], PS[:, m, :], CP[:, m, :], ALU.mult).then_inc(freed[m], 1)
                    dve.wait_ge(freed[m], st["free", m] + u + 1)
                    own.link(dve.tensor_scalar(YB[:, m, :], PV[:, m, :], pc("sconv", 4 * m + 2),
                                               pc("sconv", 4 * m + 3), ALU.mult, ALU.add))
                    for d in (1, 2):
                        own.link(dve.scalar_tensor_tensor(
                            out=YB[:, m, d:T], in0=PV[:, m, 0:T - d], scalar=pc("sconv", 4 * m + 2 - d),
                            in1=YB[:, m, d:T], op0=ALU.mult, op1=ALU.add))
                    if go_split(st, u) and m % 2:
                        dve_split(dve, st, u + 1, m // 2)
            elif ev == "bp":
                for m in range(4):
                    wait_unit(dve, st, u, m, False)
                    dve.tensor_tensor(Y[:, 4 + m, :], PS[:, m, :], YB[:, m, :], ALU.mult).then_inc(freed[m], 1)
                    if go_split(st, u) and m % 2:
                        dve_split(dve, st, u + 1, m // 2)
            elif ev == "res":
                for m in range(4):
                    wait_unit(dve, st, u, m, False)
                    k = 4 * u + m
                    dve.tensor_tensor(X[:, k, :], PS[:, m, :], X[:, k, :], ALU.add).then_inc(freed[m], 1)
                    if go_split(st, u) and m % 2:
                        dve_split(dve, st, u + 1, m // 2)
            elif ev == "mres":
                for s in range(2):
                    for m in (2 * s, 2 * s + 1):
                        wait_unit(dve, st, u, m, st.ctx)
                        k = 4 * u + m
                        dve.scalar_tensor_tensor(out=X[:, k, :], in0=PS[:, m, :],
                                                 scalar=MODT[:, st.layer, 16 + k, 0:1], in1=X[:, k, :],
                                                 op0=ALU.mult, op1=ALU.add).then_inc(freed[m], 1)
                    if st.ctx:
                        wait_unit(dve, st, u, 4 + s, True)
                        for c in range(2):
                            k = 4 * u + 2 * s + c
                            ins = dve.scalar_tensor_tensor(out=XC[:, k, :], in0=PS[:, 4 + s, c * TC:(c + 1) * TC],
                                                           scalar=MODT[:, st.layer, 16 + k, 1:2],
                                                           in1=XC[:, k, :], op0=ALU.mult, op1=ALU.add)
                        ins.then_inc(freed[4 + s], 1)
                    if go_split(st, u):
                        dve_split(dve, st, u + 1, s)
            elif ev in ("aq", "ak", "cq", "ck"):
                dst = Q if ev[1] == "q" else K
                for s in range(2):
                    for m in (2 * s, 2 * s + 1):
                        wait_unit(dve, st, u, m, st.ctx)
                        dve.tensor_copy(dst[:, m, 0:T], PS[:, m, :]).then_inc(freed[m], 1)
                    if st.ctx:
                        wait_unit(dve, st, u, 4 + s, True)
                        dve.tensor_copy(dst[:, 2 * s:2 * s + 2, T:TA],
                                        PS[:, 4 + s, :].rearrange("p (a b) -> p a b", a=2)).then_inc(freed[4 + s], 1)
                    if go_split(st, u):
                        dve_split(dve, st, u + 1, s)
            elif ev == "bz":
                n = 0
                for s in range(2):
                    for b in (2 * s, 2 * s + 1, 4 + s)[:2 + st.ctx]:
                        n += 1
                        dve.wait_ge(sem(f"bz{st.layer}"), n)
                        if b < 4:
                            zz, pp = Z[:, b, 0:T], PS[:, b, :]
                        else:
                            zz = Z[:, 2 * s:2 * s + 2, T:TA]
                            pp = PS[:, b, :].rearrange("p (a b) -> p a b", a=2)
                        dve.tensor_tensor(zz, pp, zz, ALU.mult).then_inc(freed[b], 1)
                    if go_split(st, u):
                        dve_split(dve, st, u + 1, s)
            elif ev in ("bq", "bk"):
                c0 = 0 if ev == "bq" else 4
                n0 = conv_no(st, u)
                done = sem(f"cv_done{st.layer}")
                for m in range(4):
                    w = 4 * (8 * st.layer + c0 + m)
                    dve.wait_ge(sem(f"cv_scaled{st.layer}"), n0 + m + 1)
                    b = CV[:, m % 2, :]
                    parts = [(0, T, PS[:, m, :])]
                    if st.ctx:
                        parts.append((T, TA, PS[:, 4 + m // 2, m % 2 * TC:(m % 2 + 1) * TC]))
                    for t0, t1, p_ in parts:
                        own.mark(dve.scalar_tensor_tensor(out=b[:, t0 + 1:t1], in0=p_[:, 0:t1 - t0 - 1],
                                                          scalar=pc("ml_conv", w), in1=b[:, t0 + 1:t1],
                                                          op0=ALU.mult, op1=ALU.add))
                    own.wait()
                    for t0, t1, p_ in parts:
                        ins = dve.scalar_tensor_tensor(out=b[:, t0:t1 - 1], in0=p_[:, 1:t1 - t0],
                                                       scalar=pc("ml_conv", w + 2), in1=b[:, t0:t1 - 1],
                                                       op0=ALU.mult, op1=ALU.add)
                        if t0 == 0:
                            ins.then_inc(freed[m], 1)
                        else:
                            ins.then_inc(freed[4 + m // 2] if m % 2 else done, 1)
                    if go_split(st, u) and m % 2:
                        dve_split(dve, st, u + 1, m // 2)
            elif go_split(st, u):
                for s in range(2):
                    dve_split(dve, st, u + 1, s)

    def dve_tok(dve, own, st):
        for u, ev in enumerate(st.evs):
            if ev == "g":
                dve_split(dve, st, u + 1, 0)
                for t in range(4):
                    dve.wait_ge(freed[t], st["free", t] + 1)
                    own.link(dve.tensor_tensor(GSQ[:, t, :], GT[:, t, :], GT[:, t, :], ALU.mult))
                    dve.tensor_reduce(GMS[:, t, :], GSQ[:, t, :].rearrange("p (a b) -> p a b", b=64), AX,
                                      ALU.add).then_inc(sem("sgu_ms"), 1)
                dve_split(dve, st, u + 1, 1)
                for t in range(4):
                    dve.wait_ge(sem("sgu_rs"), t + 1)
                    own.link(dve.tensor_tensor(GT[:, t, :].rearrange("p (a b) -> p a b", b=64),
                                               GT[:, t, :].rearrange("p (a b) -> p a b", b=64),
                                               GMS[:, t, :].unsqueeze(2).broadcast_to([P, 8, 64]), ALU.mult))
                    dve.tensor_tensor(GT[:, t, :], GT[:, t, :], PR[:, 512:1024], ALU.mult).then_inc(
                        sem("gv_ready"), 1)
            else:
                dst = FV if ev == "v" else V
                for t in range(st.nt):
                    wait_tok(dve, st, u, t)
                    dve.tensor_copy(dst[:, t, :], PS[:, t, :]).then_inc(freed[t], 1)
        if st.era == "hybrid":
            for k in range(KT):
                dve.tensor_tensor(H[:, k, :], HHX[:, k, :].bitcast(F32), HL[:, k, :].bitcast(F32),
                                  ALU.add).then_inc(h_back, 1)
            dve.wait_ge(h_back, st["back"] + KT)

    def dve_lru(dve, own, st):
        for m in range(4):
            dve.wait_ge(sem("lru_a"), m + 1)
            own.link(dve.tensor_tensor(HS[:, m, :], AG[:, m, :], AG[:, m, :], ALU.mult))
            dve.scalar_tensor_tensor(out=TH[:, m, :], in0=HS[:, m, :], scalar=1.0, in1=TH[:, m, :],
                                     op0=ALU.add, op1=ALU.mult).then_inc(sem("lru_t"), 1)
        for m in range(4):
            b = (2 * m + 1) % 4
            dve.wait_ge(freed[b], st["free", b] + m // 2 + 1)
            own.link(dve.tensor_tensor(IG[:, m, :], IG[:, m, :], XA[:, m, :], ALU.mult))
            dve.wait_ge(sem("lru_s"), m + 1)
            own.link(dve.tensor_tensor(TH[:, m, :], TH[:, m, :], IG[:, m, :], ALU.mult))
            own.link(dve.tensor_tensor_scan(HS[:, m, :], AG[:, m, :], TH[:, m, :], 0.0, ALU.mult, ALU.add))
            dve.tensor_tensor(Y[:, m, :], HS[:, m, :], GA[:, m, :], ALU.mult).then_inc(sem("y_ready"), 1)

    def dve_split(dve, st, u, s, last=False):
        dve.wait_ge(wh_ready[s], u + (st["ws"] + 1))
        _, _, hi, lo, _ = split_bufs(st)
        if last:
            lo = WLX
        n = slab_size(st, s, last)
        dve.tensor_tensor(lo[:, s, 0:n], W[:, s, 0:n], hi[:, s, 0:n].bitcast(F32),
                          ALU.subtract).then_inc(wl_ready[s], 1)

    def dve_split_first(dve, st):
        hi, lo, _, _, n = split_bufs(st)
        src = OY if st.at == "Y" else H
        dve_split(dve, st, 0, 0)
        for k in range(KT):
            dve.wait_ge(hh_ready, st["hl"] + k + 1)
            dve.tensor_tensor(lo[:, k, 0:n], src[:, k, 0:n], hi[:, k, :].bitcast(F32),
                              ALU.subtract).then_inc(hl_ready, 1)
        if st.kind == "merge":
            n = TA if st.ctx else T
            for k in range(4):
                dve.wait_ge(sem("y_hi"), 4 * merge_no(st) + k + 1)
                dve.tensor_tensor(YTL[:, k, 0:n], YT[:, k, 0:n], YTH[:, k, 0:n].bitcast(F32),
                                  ALU.subtract).then_inc(sem("y_lo"), 1)
        dve_split(dve, st, 0, 1)

    def dve_up(dve, own, st):
        cb, sg = sem("cb_scaled"), sem("silu_done")
        base = PCOL[f"ffn_conv{st.layer}"] + 16 * st.step0
        if st.first:
            dve_split_first(dve, st)

        def hid(i, m):
            dve.wait_ge(sg, i * 2 + (st["sg"] + m + 1))
            dve.wait_ge(freed[2 + m], i + (st["free", 2 + m] + 1))
            dve.tensor_tensor(ARENA[:, bass.ds(i * (2 * T) + (KT + m) * T, T)], SG[:, m, :], CB[:, 2 + m, :],
                              ALU.mult).then_inc(hidden, 1)

        with own.loop(st.n, 4) as i:
            for m in range(4):
                if m % 2:
                    dve_split(dve, st, i + 1, m // 2)
                dve.wait_ge(cb, i * 4 + (st["cb"] + m + 1))
                for d in (1, 2):
                    ins = dve.scalar_tensor_tensor(
                        out=CB[:, m, d:T], in0=PS[:, m, 0:T - d],
                        scalar=PC[:, bass.ds(i * 16 + (base + 4 * m + 2 - d), 1)],
                        in1=CB[:, m, d:T], op0=ALU.mult, op1=ALU.add)
                    if d == 1:
                        own.link(ins)
                ins.then_inc(freed[m], 1)
                if m >= 2:
                    hid(i, m - 2)
            for m in range(2):
                at = bass.ds(i * (2 * T) + m * T, T)
                dve.wait_ge(hid_hi, i * 2 + (st["hid"] + m + 1))
                dve.tensor_tensor(HIDL[:, at], ARENA[:, bass.ds(i * (2 * T) + (KT + m) * T, T)],
                                  HIDH[:, at].bitcast(F32), ALU.subtract).then_inc(hid_lo, 1)

    def dve_down(dve, own, st):
        for u in range(2):
            for m in range(4):
                if m % 2 and not (st.final and u == 1):
                    dve_split(dve, st, u + 1, m // 2)
                wait_unit(dve, st, u, m, False)
                k = 4 * u + m
                dve.tensor_tensor(X[:, k, :], PS[:, m, :], X[:, k, :], ALU.add).then_inc(freed[m], 1)

    def dve_foxgate(dve, own, st):
        z, lz, lf, cum = (FROW[0:8, i, :] for i in range(4))
        dve.wait_ge(sem("fox_l"), 1)
        own.link(dve.tensor_scalar(lf, z, 0.0, None, ALU.min))
        own.link(dve.tensor_tensor(lf, lf, lz, ALU.subtract))
        own.link(dve.memset(lz, 0.0))
        dve.tensor_tensor_scan(cum, lf, lz, 0.0, ALU.add, ALU.add).then_inc(sem("fox_cum"), 1)
        dve.wait_ge(full[7], st["full", 7] + 1)
        dve.tensor_copy(FCQ[:, :, :].rearrange("p a b -> p (a b)"), PS[:, 7, 0:32]).then_inc(freed[7], 1)

    def dve_sgu(dve, own, st):
        for t in range(4):
            dve.wait_ge(full[t], st["full", t] + 1)
            dve.tensor_tensor(OY[:, t, :], PS[:, t, :], UU[:, t, :], ALU.mult).then_inc(freed[t], 1)

    def dve_attn(dve, own, st):
        q_, k_, v_, at_, e_, l_ = attn_bufs(st)
        jobs, name = st.jobs, st.name
        da, fox = name.startswith("da"), name == "fox"
        if fox:
            dve.wait_ge(freed[7], st["free", 7])

        def maxima(j):
            for ci, (c, use) in enumerate(zip(j["comps"], j["use"])):
                s, nk, h = c["slot"], j["nk"], j["head"]
                b = 2 * s
                if fox:
                    dve.wait_ge(full[7], st["full", 7] + h + 1)
                    ins = dve.tensor_scalar(FT1[:, s, 0:nk], PS[:, 7, 0:nk], -1.0, FCQ[:, j["qb"], h:h + 1],
                                            ALU.mult, ALU.add)
                    if j["qb"] == 3:
                        ins.then_inc(freed[7], 1)
                        dve.wait_ge(freed[7], st["free", 7] + h + 1)
                    else:
                        own.link(ins)
                    own.link(dve.tensor_tensor(FT1[:, s, j["q0"]:nk], FT1[:, s, j["q0"]:nk], MCAUS[:, :],
                                               ALU.add))
                dve.wait_ge(full[b], st["full", b] + use + 1)
                src = bank(b, nk)
                if not j["raw"]:
                    if fox:
                        dve.scalar_tensor_tensor(out=l_[:, s, 0:nk], in0=src, scalar=SCALE, in1=FT1[:, s, 0:nk],
                                                 op0=ALU.mult, op1=ALU.add).then_inc(freed[b], 1)
                    else:
                        dve.wait_ge(sem(f"nb_{name}_{h % 2}"), 16 * (h // 2 + 1))
                        o = (7 - 2 * j["qb"] - 1) * 64
                        own.mark(dve.scalar_tensor_tensor(out=l_[:, s, 0:T], in0=PS[:, b, :], scalar=SCALE,
                                                          in1=NB[:, h % 2, o:o + T], op0=ALU.mult, op1=ALU.add))
                        dve.tensor_scalar(l_[:, s, T:TA], PS[:, b + 1, 0:TC], SCALE, None,
                                          ALU.mult).then_inc(freed[b], 1)
                    dve.wait_ge(freed[b], st["free", b] + use + 1)
                    src = l_[:, s, 0:nk]
                ins = dve.tensor_reduce(col(0, j, ci), src, AX, ALU.max, negate=True)
                if j["raw"]:
                    own.link(ins)
                    ins = dve.tensor_scalar(col(0, j, ci), col(0, j, ci), SCALE, None, ALU.mult)
                ins.then_inc(sem(f"max_{name}"), 1)

        def probs(j):
            pr = sem(f"probs_{name}")
            for ci, (c, use) in enumerate(zip(j["comps"], j["use"])):
                s = c["slot"]
                if j["raw"]:
                    dve.wait_ge(freed[2 * s], st["free", 2 * s] + use + 1)
                else:
                    dve.wait_ge(sem(f"exp_{name}"), c["ex"] + 1)
                own.link(dve.reciprocal(col(32, j, ci), col(16, j, ci)))
            s, nk = eslot(j, j["comps"][0]["slot"]), j["nk"]
            e0 = e_[:, s, 0:nk]
            if not da:
                dve.tensor_scalar(e0, e0, col(32, j, 0), None, ALU.mult).then_inc(pr, 1)
                return
            own.mark(dve.tensor_tensor(col(32, j, 1), col(32, j, 1), LAM[:, st.layer, 1:2], ALU.mult))
            own.link(dve.tensor_scalar(e0, e0, col(32, j, 0), None, ALU.mult))
            dve.scalar_tensor_tensor(out=e0, in0=e_[:, s + 1, 0:nk], scalar=col(32, j, 1), in1=e0,
                                     op0=ALU.mult, op1=ALU.add).then_inc(pr, 1)

        def post(j):
            nq, o, po, dv = j["nq"], j["out"], j["po"], j["dv"]
            c0 = 0 if nq == T else T
            src = PS[po:po + dv, 6, 0:nq]
            if fox:
                dve.wait_ge(full[6], st["full", 6] + o + 1)
                dve.tensor_copy(OY[po:po + dv, 4 + j["tile"], :], src).then_inc(freed[6], 1)
                return
            y = YT[po:po + dv, j["tile"], c0:c0 + nq]
            z = Z[po:po + dv, j["tile"], c0:c0 + nq]
            if da:
                dve.wait_ge(sem(f"o_rs_{name}"), o + 1)
                dve.scalar_tensor_tensor(out=y, in0=src, scalar=DAG[:, st.layer:st.layer + 1],
                                         in1=l_[:, 1, 0:nq], op0=ALU.mult, op1=ALU.mult).then_inc(freed[6], 1)
                dve.wait_ge(freed[6], st["free", 6] + o + 1)
                dve.tensor_tensor(y, y, z, ALU.mult).then_inc(sem(f"da_y{st.layer}"), 1)
            else:
                dve.wait_ge(full[6], st["full", 6] + o + 1)
                dve.tensor_tensor(y, src, z, ALU.mult).then_inc(freed[6], 1)

        ahead = 1 if da else 2
        for j in jobs[:ahead]:
            maxima(j)
        late, mod = None, 0
        for j in jobs:
            probs(j)
            if j["n"] + ahead < len(jobs):
                maxima(jobs[j["n"] + ahead])
            if late:
                post(late)
            late = j if j["last"] else None
            if fox and j["n"] and mod < mod_parts(j["n"] - 1) // 4:
                dve_mod(dve, st, mod)
                mod += 1
        post(late)
        while fox and mod < MOD:
            dve_mod(dve, st, mod)
            mod += 1

    def dve_rope(dve, own, st):
        dve.wait_ge(sem(f"rope_loaded{st.layer}"), 32)
        for n in range(8):
            b, buf = 6 + n % 2, (Q, K)[n // 4]
            x_ = buf[:, n % 4, 0:T]
            dve.wait_ge(full[b], st["full", b] + n // 2 + 1)
            wait(dve, sem(f"rope_done{st.layer}"), n)
            own.mark(dve.tensor_tensor(RT1[:, :], x_, RC[:, :], ALU.mult))
            dve.tensor_tensor(RT2[:, :], PS[:, b, :], RS_[:, :], ALU.mult).then_inc(freed[b], 1)
            own.wait()
            dve.wait_ge(freed[b], st["free", b] + n // 2 + 1)
            dve.tensor_tensor(x_, RT1[:, :], RT2[:, :], ALU.add).then_inc(sem(f"rope_done{st.layer}"), 1)

    def dve_merge(dve, own, st):
        dve_split_first(dve, st)

        def step(i, last=False):
            dve_split(dve, st, i + 1, 0, last)
            for m, (g, b) in enumerate(((0, 2), (1, 3), (4, 5))[:2 + st.ctx]):
                wait_unit(dve, st, i, b, st.ctx)
                dve.wait_ge(freed[g], i + (st["free", g] + 1))
                if m < 2:
                    dst, gate, prod, tmp = (ARENA[:, bass.ds(i * (2 * TA) + m * TA, T)], GB[:, m, :],
                                            PS[:, b, :], TM[:, :])
                else:
                    dst = ACC[:, bass.ds(i * 2, 2), T:TA]
                    gate, prod, tmp = (v.rearrange("p (a b) -> p a b", a=2)
                                       for v in (GB[:, 2, :], PS[:, 5, :], TM[:, :]))
                if st.n == 0:
                    dve.tensor_tensor(dst, prod, gate, ALU.mult).then_inc(freed[b], 1)
                else:
                    f = ((5 if st.ctx else 3), 2, 3)[m]
                    dve.wait_ge(freed[f], i + (st["free", f] + (m > 0)))
                    own.link(dve.tensor_tensor(tmp, prod, gate, ALU.mult))
                    dve.tensor_tensor(dst, dst, tmp, ALU.add).then_inc(freed[b], 1)
            dve_split(dve, st, i + 1, 1, last)

        with own.loop(3, 0 if st.n == 0 else 2 + st.ctx) as i:
            step(i)
        step(3, True)

    def dve_mlgate(dve, own, st):
        for g in range(2):
            t0, n = ((0, T), (T, TC))[g]
            dve.wait_ge(full[6], st["full", 6] + g + 1)
            dve.tensor_scalar(LI[0:8, t0:t0 + n], PS[0:8, 6, 0:n],
                              PC[0:8, PCOL["gate_bi"] + st.layer:PCOL["gate_bi"] + st.layer + 1], None,
                              ALU.add).then_inc(freed[6], 1)
        own.link(dve.memset(ZERO[0:8, :], 0.0))
        dve.wait_ge(sem(f"ml_l{st.layer}"), 1)
        own.link(dve.tensor_scalar(LX[0:8, :], LX[0:8, :], 0.0, None, ALU.min))
        own.link(dve.tensor_tensor(LF[0:8, :], LX[0:8, :], LF[0:8, :], ALU.subtract))
        dve.wait_ge(freed[6], st["free", 6] + 2)
        for d, (b_, a_, m_) in enumerate(((B0, A0, M0), (B1, A1, M1))):
            if d == 0:
                parts, seam = (slice(T, TA), slice(0, T)), TA - 1
            else:
                parts, seam = (slice(TA - 1, T - 1, -1), slice(T - 1, None, -1)), T
            for i, p_ in enumerate(parts):
                init = 0.0 if i == 0 else b_[0:8, seam:seam + 1]
                own.link(dve.tensor_tensor_scan(b_[0:8, p_], LF[0:8, p_], ZERO[0:8, p_], init,
                                                ALU.add, ALU.add))
            own.link(dve.tensor_tensor(a_[0:8, :], LI[0:8, :], b_[0:8, :], ALU.subtract))
            for i, p_ in enumerate(parts):
                init = 0.0 if i == 0 else m_[0:8, seam:seam + 1]
                own.link(dve.tensor_tensor_scan(m_[0:8, p_], a_[0:8, p_], a_[0:8, p_], init,
                                                ALU.max, ALU.max))
            ins = dve.tensor_tensor(b_[0:8, :], b_[0:8, :], m_[0:8, :], ALU.add)
            if d == 0:
                own.mark(ins)
            else:
                ins.then_inc(sem(f"ml_rows{st.layer}"), 1)
        dve.wait_ge(full[0], st["full", 0] + 1)
        dve.tensor_copy(AC[:, :, :].rearrange("p a b -> p (a b)"), PS[:, 0, 0:96]).then_inc(freed[0], 1)

    def dve_mlstm(dve, own, st):
        dz, mk, dab = (sem(f"{n}{st.layer}") for n in ("decay", "ml_mask", "den_abs"))

        def divide(ps, step):
            h, d, nq, p = ps["h"], ps["d"], ps["nq"], ps["p"]
            q0, num = T * ps["g"], 2 + 4 * (p % 2)
            y, c = YT[:, h, q0:q0 + nq], (step - 1) * P
            if step == 0:
                dve.wait_ge(dab, p + 1)
                own.link(dve.tensor_tensor(RCP[:, 0:nq], TMP[:, 0:nq], EM[:, p % 2, 0:nq], ALU.max))
            elif c < nq:
                own.link(dve.reciprocal(RCP[:, c:c + P], RCP[:, c:c + P]))
            else:
                dst = y if d == 0 else RCP[:, 0:nq]
                ins = dve.tensor_tensor(dst, PS[:, num, 0:nq], RCP[:, 0:nq], ALU.mult)
                if d == 1:
                    own.link(ins)
                    ins = dve.tensor_tensor(y, y, RCP[:, 0:nq], ALU.add)
                ins.then_inc(freed[num], 1)
                dve.wait_ge(freed[num], st["free", num] + p // 2 + 1)

        last = None
        for ps in st.passes:
            h, d, nq, n0, p, nb = ps["h"], ps["d"], ps["nq"], ps["n0"], ps["p"], ps["nb"]
            dve.wait_ge(full[5], st["full", 5] + p + 1)
            wait(dve, dz, n0)
            mask = (MFWD, MBWD)[d][:, :].unsqueeze(1).broadcast_to([P, nb, P])
            dve.tensor_tensor(MK[:, 0:nb, :], PS[:, 4, 0:nq].rearrange("p (a b) -> p a b", b=P), mask,
                              ALU.add).then_inc(mk, 1)
            nblocks = len(ps["blocks"])
            for i, (s_, t0, t1, j) in enumerate(ps["blocks"]):
                n = n0 + i
                dve.wait_ge(dz, n + 1)
                dve.wait_ge(full[n % 2], st["full", n % 2] + n // 2 + 1)
                dve.scalar_tensor_tensor(out=ZM[:, n % 2, t0:t1], in0=PS[:, n % 2, t0:t1],
                                         scalar=float(P) ** -0.5, in1=DM[:, n % 2, t0:t1],
                                         op0=ALU.mult, op1=ALU.mult).then_inc(freed[n % 2], 1)
                if last and i:
                    steps = last["nq"] // P + 2
                    for step in range(steps * (i - 1) // (nblocks - 1), steps * i // (nblocks - 1)):
                        divide(last, step)
            last = ps
        for step in range(last["nq"] // P + 2):
            divide(last, step)

    def dve_mlout(dve, own, st):
        n = TA if st.ctx else T
        for h in range(4):
            dve.wait_ge(sem(f"ml_rs{st.layer}"), h + 1)
            y = YT[:, h, 0:n]
            own.link(dve.scalar_tensor_tensor(out=y, in0=y, scalar=pc("ml_g", st.layer), in1=RST[:, 0:n],
                                              op0=ALU.mult, op1=ALU.mult))
            dve.tensor_tensor(y, y, Z[:, h, 0:n], ALU.mult).then_inc(sem(f"ml_y{st.layer}"), 1)

    def sp_slabs(sp, st, n, sources):
        peel = st["it"] == 0 or st.apart != st.after_apart

        def pair(i):
            for s, (src, size) in enumerate(sources(i)):
                if st.after_apart if isinstance(i, int) and i == 0 else st.apart:
                    sp.wait_ge(wl_ready[s], i + st["ws"])
                else:
                    wait(sp, slab_used[s], i + st["it"])
                sp.dma_start(W[:, s, 0:size], src.rearrange("a p n -> p (a n)")).then_inc(w_ready[s], 16)
        repeat(sp, n, peel, pair)

    def sp_stage(sp, st):
        S8 = KT * SLAB

        def both8(i):
            return [(w8[bass.ds(i * 2 + (st["w8"] + s), 1), :, :], S8) for s in range(2)]

        if st.kind == "attn" and st.name == "fox":
            sp_slabs(sp, st, MOD, both8)
        elif st.kind in ("units", "tok"):
            sp_slabs(sp, st, len(st.evs), both8)
        elif st.kind == "up":
            sp_slabs(sp, st, st.n, both8)
        elif st.kind == "down":
            for u in range(2):
                for s in range(2):
                    sp.wait_ge(wl_ready[s], u + st["ws"])
                    sp.dma_start(W[:, s, 0:st.n * SLAB],
                                 w8[st["w8"] + 2 * u + s, :, 0:st.n * SLAB]).then_inc(w_ready[s], 16)
        elif st.kind == "merge":
            sp_slabs(sp, st, 4, lambda i: [
                (w8[bass.ds(i + st["w8"], 1), :, :], S8),
                (wb[bass.ds(i + (12 * st.layer + 4 * st.n), 1), :, :], 4 * SLAB)])
        elif st.kind == "norm" and st.mode == "mod":
            if st.layer == 1:
                sp.wait_ge(sem("ml_rows0"), 1)
            sp.dma_start(WGS[:, :, :], wg_in[st.layer, :, :].rearrange("p (a b) -> p a b", a=KT)).then_inc(
                sem(f"wg_loaded{st.layer}"), 16)
        elif st.kind == "store":
            sp.wait_ge(x_normed, st["xn"])
            sp.dma_start(out, X[:, :, :]).then_inc(sem("stored"), 16)
            sp.wait_ge(sem("stored"), 16)

    PE = dict(norm=pe_norm, units=pe_units, tok=pe_tok, lru=pe_lru, up=pe_up, down=pe_down,
              foxgate=pe_foxgate, sgu=pe_sgu, attn=pe_attn, rope=pe_rope, merge=pe_merge,
              mlgate=pe_mlgate, mlstm=pe_mlstm, mlout=pe_mlout)
    SCALAR = dict(prep=act_prep, norm=act_norm, units=act_units, tok=act_tok, lru=act_lru, up=act_up, down=act_down,
                  foxgate=act_foxgate, attn=act_attn, merge=act_merge, mlgate=act_mlgate,
                  mlstm=act_mlstm, mlout=act_mlout)
    VECTOR = dict(prep=dve_prep, norm=dve_norm, units=dve_units, tok=dve_tok, lru=dve_lru, up=dve_up,
                  down=dve_down, foxgate=dve_foxgate, sgu=dve_sgu, attn=dve_attn, rope=dve_rope,
                  merge=dve_merge, mlgate=dve_mlgate, mlstm=dve_mlstm, mlout=dve_mlout)

    blocks = ExitStack()
    block = blocks.enter_context(nc.Block())

    @block.sync
    def _(sp):
        for half in range(2):
            sp.dma_start(X[:, 4 * half:4 * half + 4, :],
                         x[:, 4 * half:4 * half + 4, :]).then_inc(x_loaded[half], 16)
        sp.dma_start(PC[:, :], params).then_inc(loaded, 16)
        sp.dma_start(PR[:, :], rows).then_inc(loaded, 16)
        for st in stages:
            sp_stage(sp, st)

    @block.gpsimd
    def _(pool):
        pool.memset(EPSC[:, :], EPS).then_inc(consts, 1)
        pool.memset(ONES[:, :], 1.0).then_inc(consts, 1)
        for v in (IDENT, MCAUS, MFWD, MBWD):
            pool.memset(v[:, :], 0.0).then_inc(consts, 1)
        pool.memset(SEL[:, :, :], 0.0).then_inc(consts, 1)
        pool.memset(LRUW[:, :, :], 0.0).then_inc(consts, 1)
        pool.wait_ge(consts, 8)
        pool.affine_select(out=IDENT[:, :], in_=IDENT[:, :], compare_op=ALU.not_equal, fill=1.0, base=0,
                           pattern=[[-1, P]], channel_multiplier=1)
        pool.affine_select(out=SEL[:, :, :], in_=SEL[:, :, :], compare_op=ALU.not_equal, fill=1.0, base=0,
                           pattern=[[-1, 8], [0, P]], channel_multiplier=1)
        pool.affine_select(out=MCAUS[:, :], in_=MCAUS[:, :], compare_op=ALU.is_ge, fill=-BIG, base=0,
                           pattern=[[-1, P]], channel_multiplier=1)
        pool.affine_select(out=MFWD[:, :], in_=MFWD[:, :], compare_op=ALU.is_ge, fill=BIG, base=0,
                           pattern=[[1, P]], channel_multiplier=-1)
        pool.affine_select(out=MBWD[:, :], in_=MBWD[:, :], compare_op=ALU.is_ge, fill=BIG, base=0,
                           pattern=[[-1, P]], channel_multiplier=1).then_inc(consts, 1)
        for half in range(2):
            pool.dma_start(XC[:, 4 * half:4 * half + 4, :], ctx_in[:, 4 * half:4 * half + 4, :]).then_inc(loaded_pool, 16)
        for src, dst in ((rot, ROT[:, :]), (wf_in.rearrange("p (a b) -> p a b", a=KT), WFS[:, :, :])):
            pool.dma_start(dst, src).then_inc(loaded_pool, 16)
        for g in range(2):
            for half in range(2):
                for q in range(2):
                    pool.dma_start(LRUW[64 * half:64 * half + 64, 4 * g + 2 * q:4 * g + 2 * q + 2,
                                        64 * half:64 * half + 64],
                                   lru_w[g, half, :, 2 * q:2 * q + 2, :]).then_inc(sem("lru_w"), 16)
        for st in stages:
            if st.kind == "foxgate":
                pool.wait_ge(h_ready, st["hr"])
                pool.dma_start(WT[:, :, :], sgu_w).then_inc(sem("sgu_loaded"), 16)
                pool.dma_start(BS[0:8, :], sgu_b).then_inc(sem("sgu_loaded"), 16)
                pool.wait_ge(sem("sgu_loaded"), 32)
                pool.affine_select(out=WT[:, :, :], in_=WT[:, :, :], compare_op=ALU.is_ge, fill=0.0, base=0,
                                   pattern=[[0, 8], [1, P]], channel_multiplier=-1).then_inc(sem("wt_masked"), 1)
            if st.kind == "rope":
                pool.wait_ge(h_ready, st["hr"])
                for dst, src in ((RC, rope[0, :, :]), (RS_, rope[1, :, :])):
                    pool.dma_start(dst[:, :], src).then_inc(sem(f"rope_loaded{st.layer}"), 16)
            if st.kind == "attn" and st.name.startswith("na"):
                pool.wait_ge(h_back, st["back"])
                for h in range(8):
                    if h >= 2:
                        nj = sum(j["head"] < h - 1 for j in st.jobs)
                        pool.wait_ge(sem(f"probs_{st.name}"), nj)
                    pool.dma_start(NB[:, h % 2, :], nbias[st.layer, h, :, :]).then_inc(
                        sem(f"nb_{st.name}_{h % 2}"), 16)

    @block.scalar
    def _(act):
        own = Own(act, sem("act_step"))
        for st in stages:
            if st.kind in SCALAR:
                SCALAR[st.kind](act, own, st)

    @block.vector
    def _(dve):
        own = Own(dve, sem("dve_step"))
        for st in stages:
            if st.kind in VECTOR:
                VECTOR[st.kind](dve, own, st)

    @block.tensor
    def _(pe):
        pe.wait_ge(consts, 9)
        for st in stages:
            if st.kind == "lru":
                wait_loaded(pe)
            if st.kind in PE:
                PE[st.kind](pe, st)

    blocks.close()
    cx.close()


def _lay_out(a):
    def slabs(w, cols):
        return [w[:, c:c + SLAB].reshape(-1, P, SLAB).transpose(1, 0, 2).reshape(P, -1) for c in cols]

    def unit(w, c):
        return slabs(w, (c, c + SLAB))

    def unit_tok(w, c):
        return [w[4 * s * P:4 * (s + 1) * P, c:c + BW].reshape(4, P, BW).transpose(1, 0, 2).reshape(P, -1)
                for s in range(2)]

    even = dict(xa=0, ga=512, cp=1024, vb=2048, bp=1536)
    odd = dict(u=0, g=512, q=1024, k=1536, v=2048)
    h0 = 4 * BW
    hyb = dict(aq=0, ak=512, av=1024, az=1536, bq=h0, bk=h0 + 512, bv=h0 + 1024, bo=h0 + 1536, bz=h0 + 2048)
    h1 = 9 * BW + 16
    hyb.update(cq=h1, ck=h1 + 512, cv=h1 + 1024, cz=h1 + 1536)
    gm = h1 + 2048
    w8, wb = [], []
    nres = 0
    for st in plan_stages():
        if st.name == "fox":
            for l in range(LAYERS):
                w8 += slabs(a["w_mod_2"][l], range(0, 3 * D, SLAB))
        elif st.kind in ("units", "tok"):
            put = unit if st.kind == "units" else unit_tok
            for u, ev in enumerate(st.evs):
                if ev == "res":
                    w8 += put((a["mix0_w_out"], a["mix1_w_out"])[nres // 2][0], BW * u)
                    nres += 1
                elif ev == "mres":
                    w8 += put(a["w_out_2"][st.layer], BW * u)
                elif ev in even:
                    w8 += put(a["mix0_w_in"][0], even[ev])
                elif ev in odd:
                    w8 += put(a["mix1_w_in"][0], odd[ev])
                else:
                    w8 += put(a["w_in_2"][st.layer], hyb[ev])
        elif st.kind == "up":
            for i in range(st.step0, st.step0 + st.n):
                w8 += slabs(a["ffn_up"][st.layer], (SLAB * i, F + SLAB * i))
        elif st.kind == "down":
            w = a["ffn_down"][st.layer][SLAB * st.step0:SLAB * st.step0 + P * st.n]
            for slab in slabs(w, range(0, D, SLAB)):
                w8.append(np.pad(slab, ((0, 0), (0, (KT - st.n) * SLAB))))
        elif st.kind == "merge":
            for i in range(4):
                w8 += slabs(a["w_in_2"][st.layer], (gm + D * st.n + SLAB * i,))
                wb += slabs(a["w_br_2"][st.layer, st.n], (SLAB * i,))

    def cols(v):
        return np.asarray(v).reshape(-1, P).T

    def pad8(v):
        o = np.zeros((P, v.shape[1]), np.float32)
        o[:8] = v
        return o

    ffn = []
    for l in range(LAYERS):
        w = np.concatenate([a["ffn_conv_w"][l], a["ffn_conv_b"][l][None]])
        w = w.reshape(4, 2, FI, 2, P)
        ffn.append(w.transpose(4, 2, 1, 3, 0).reshape(P, FI * 16))
    taps = lambda w, b, n: np.concatenate([w, b[None]]).reshape(-1, n, P).transpose(2, 1, 0).reshape(P, -1)
    gb = a["ml_gate_b_2"]
    parts = dict(
        mix0_norm=cols(a["mix0_norm"]), lru_conv=taps(a["lru_conv_w"][0], a["lru_conv_b"][0], 4),
        lru_ba=cols(a["lru_ba"]), lru_bx=cols(a["lru_bx"]), lru_lambda=cols(a["lru_lambda"]),
        sconv=taps(a["sconv_w"][0], a["sconv_b"][0], 4), mix1_norm=cols(a["mix1_norm"]),
        ffn_norm0=cols(a["ffn_norm"][0]), ffn_norm1=cols(a["ffn_norm"][1]), final_norm=cols(a["final_norm"]),
        ffn_conv0=ffn[0], ffn_conv1=ffn[1],
        c=np.stack([cols(a["c_2"]), cols(a["c_ctx_2"])], 2).reshape(P, 16),
        b_mod=np.repeat(cols(a["b_mod_2"]), 2, 1), norm_g=np.repeat(cols(a["norm_g_2"]), 2, 1),
        da_g=cols(a["da_norm_g_2"]),
        ml_conv=np.concatenate([taps(a["ml_conv_w_2"][l], a["ml_conv_b_2"][l], 8) for l in range(LAYERS)], 1),
        ml_g=cols(a["ml_norm_g_2"]), final_g=cols(a["final_g_2"]), fox_bf=pad8(a["fox_bf"].reshape(8, 1)),
        gate_bi=pad8(gb[:, :, 0].reshape(LAYERS, 8).T), gate_bf=pad8(gb[:, :, 1].reshape(LAYERS, 8).T))
    params = np.concatenate([parts[n] for n, _ in PARAMS], 1)
    rows = np.concatenate([a["da_lam_q_2"].reshape(-1), a["da_lam_k_2"].reshape(-1), a["sgu_norm"].reshape(-1)])
    rows = np.broadcast_to(rows, (P, NROW))
    chan = lambda v: v[0].T.reshape(KT, P, -1).transpose(1, 0, 2)
    lru_w = np.stack([a["lru_wa"][0], a["lru_wx"][0]]).reshape(2, 4, 2, 64, 64).transpose(0, 2, 3, 1, 4)
    g0 = 9 * BW
    wg = a["w_in_2"][:, :, g0:g0 + 16].reshape(LAYERS, KT, P, 2, 2, 4).transpose(0, 2, 1, 4, 3, 5)
    wf = a["mix1_w_in"][0][:, 5 * BW:5 * BW + 8].reshape(KT, P, 8).transpose(1, 0, 2)
    rpb = a["na_rpb_2"]
    nb = np.full((LAYERS, 8, 2, 64, 14, 64), -BIG, np.float32)
    for c in range(64):
        lo = min(max(c - 8, 0), 48)
        for par in range(2):
            nb[:, :, par, c, :, lo:lo + 16] = rpb[:, :, 1 - par:15 - par, lo - c + 15:lo - c + 31]
    t = np.arange(T)
    inv = 10000.0 ** (-np.arange(0, 32, 2, dtype=np.float32) / np.float32(32))
    ang = np.concatenate([(t // 64)[:, None].astype(np.float32) * inv.astype(np.float32),
                          (t % 64)[:, None].astype(np.float32) * inv.astype(np.float32)], 1)
    ang = np.tile(np.repeat(ang.T, 2, 0), (2, 1)).astype(np.float32)
    rot = np.zeros((P, P), np.float32)
    for i in range(0, P, 2):
        rot[i + 1, i], rot[i, i + 1] = -1.0, 1.0
    d = dict(x=chan(a["x"]), ctx_in=chan(a["ctx_2"]), w8=np.stack(w8), wb=np.stack(wb),
             wf_in=wf.reshape(P, -1), wg_in=wg.reshape(LAYERS, P, -1), params=params, rows=rows, lru_w=lru_w,
             sgu_w=a["sgu_w"][0].transpose(2, 0, 1), sgu_b=a["sgu_b"][0],
             rope=np.stack([np.cos(ang), np.sin(ang)]), rot=rot, nbias=nb.reshape(LAYERS, 8, P, 14 * 64))
    return {k: np.ascontiguousarray(v, dtype=np.float32) for k, v in d.items()}


def kernel(**inputs):
    import concourse.bacc as bacc
    from concourse.bass_utils import run_bass_kernel_spmd as run

    nc = bacc.Bacc("TRN2", target_bir_lowering=False, num_devices=1)
    laid = _lay_out({k: np.asarray(v) for k, v in inputs.items()})
    arrays, args = {}, {}
    for name, v in laid.items():
        arrays[f"in_{name}"] = v
        args[name] = nc.dram_tensor(f"in_{name}", v.shape, F32, kind="ExternalInput").ap()
    out = nc.dram_tensor("out", (P, KT, T), F32, kind="ExternalOutput").ap()
    build(nc, **args, out=out)
    r = run(nc, [arrays], core_ids=[0])
    got = np.asarray(r.results[0]["out"])
    return np.ascontiguousarray(got.transpose(2, 1, 0).reshape(1, T, D))
```
